# Optimizing a Trainium2 kernel written in Bass

```python
import jax, jax.numpy as jnp
from jax import lax
import numpy as np

D_MODEL = 1024
BATCH = 1
SEQ = 256
DEPTH = 2
DEC_BATCH = 8
DEC_SEQ = 8
PAST_LEN = 1024
PAGE_SIZE = 128

N_A_LAYERS = DEPTH // 2
N_B_LAYERS = DEPTH - N_A_LAYERS
N_DENSE = (DEPTH + 1) // 2
N_MOE = DEPTH // 2
CHUNK = 128
N_GROUPS = 8
D_GATE = 2 * D_MODEL
N_HEADS = 8
Q_RANK = 3 * D_MODEL // 8
KV_RANK = D_MODEL // 4
D_NOPE = 128
D_ROPE = 64
D_V = 128
QBLOCK = 128
ROPE_THETA = 10000.0
D_FF = 2816
N_EXPERTS = 8
TOP_K = 2
EPS = 1e-6
ATTN_SCALE = (D_NOPE + D_ROPE) ** -0.5

kernel_name = 'yoco_chunk_gmlp_mla_moe_step'

def rmsnorm(x, g):
    xf = x.astype(jnp.float32)
    y = xf * lax.rsqrt(jnp.mean(xf * xf, axis=-1, keepdims=True) + EPS)
    return (y * g.astype(jnp.float32)).astype(x.dtype)

def rope(x, pos):
    half = D_ROPE // 2
    inv = ROPE_THETA ** (-jnp.arange(half, dtype=jnp.float32) / half)
    ang = pos.astype(jnp.float32)[:, None] * inv[None, :]
    shape = (ang.shape[0],) + (1,) * (x.ndim - 3) + (half,)
    cos = jnp.cos(ang).reshape(shape)
    sin = jnp.sin(ang).reshape(shape)
    xf = x.astype(jnp.float32)
    x1, x2 = xf[..., :half], xf[..., half:]
    return jnp.concatenate([x1 * cos - x2 * sin, x1 * sin + x2 * cos], axis=-1).astype(x.dtype)

def chunk_gmlp(x, norm_g, w_in, b_in, sgu_g, w_s, b_s, w_out, b_out):
    bsz, s, _ = x.shape
    L = min(s, CHUNK)
    h = rmsnorm(x, norm_g)
    z = jax.nn.gelu(h @ w_in + b_in)
    u, v = z[..., :D_GATE], z[..., D_GATE:]
    v = rmsnorm(v, sgu_g)
    vg = v.reshape(bsz, s // L, L, N_GROUPS, D_GATE // N_GROUPS)
    w = w_s[:, :L, :L] * jnp.tril(jnp.ones((L, L), w_s.dtype))
    mix = jnp.einsum('gij,bnjgc->bnigc', w, vg) + b_s[:, :L].T[None, None, :, :, None]
    out = (u * mix.reshape(bsz, s, D_GATE)) @ w_out + b_out
    return out, v

def dense_swiglu(h, wg, wu, wd):
    return (jax.nn.silu(h @ wg) * (h @ wu)) @ wd

def moe_swiglu(h, w_router, wg, wu, wd):
    shp = h.shape
    t = h.reshape(-1, D_MODEL)
    probs = jax.nn.softmax((t @ w_router).astype(jnp.float32), axis=-1)
    top_p, top_i = lax.top_k(probs, TOP_K)
    top_p = top_p / jnp.sum(top_p, axis=-1, keepdims=True)
    gates = jnp.sum(jax.nn.one_hot(top_i, N_EXPERTS, dtype=jnp.float32) * top_p[..., None], axis=-2)
    gates = gates.astype(h.dtype)

    def expert(acc, xs):
        wg_e, wu_e, wd_e, g_e = xs
        y = (jax.nn.silu(t @ wg_e) * (t @ wu_e)) @ wd_e
        return acc + g_e[:, None] * y, None

    out, _ = lax.scan(expert, jnp.zeros_like(t), (wg, wu, wd, gates.T))
    return out.reshape(shp)

def channel_mixer(x, layer, p):
    h = rmsnorm(x, p['f_norm_g'][layer])
    i = layer // 2
    if layer % 2 == 0:
        return dense_swiglu(h, p['d_w_gate'][i], p['d_w_up'][i], p['d_w_down'][i])
    return moe_swiglu(h, p['m_w_router'][i], p['m_w_gate'][i], p['m_w_up'][i], p['m_w_down'][i])

def shared_key_side(x, pos, kv_norm_g, w_dkv, kv_lat_g, w_kr, kr_g):
    h = rmsnorm(x, kv_norm_g)
    c = rmsnorm(h @ w_dkv, kv_lat_g)
    kr = rope(rmsnorm(h @ w_kr, kr_g), pos)
    return c, kr

def key_rms_scale(c, w_uk):
    k = jnp.einsum('tr,rhd->thd', c, w_uk).astype(jnp.float32)
    return lax.rsqrt(jnp.mean(k * k, axis=-1) + EPS)

def mla_attend_block(q_abs, q_rope, qpos, c, kr, r, kpos):
    s = (jnp.einsum('bqhr,bkr->bhqk', q_abs, c).astype(jnp.float32) * jnp.swapaxes(r, 1, 2)[:, :, None, :]
         + jnp.einsum('bqhd,bkd->bhqk', q_rope, kr).astype(jnp.float32))
    s = jnp.where(kpos[None, :] <= qpos[:, None], s * ATTN_SCALE, -jnp.inf)
    prob = jax.nn.softmax(s, axis=-1).astype(c.dtype)
    return jnp.einsum('bhqk,bkr->bqhr', prob, c)

def mla_attend(q_abs, q_rope, qpos, c, kr, r, kpos):
    bsz, q_len = q_abs.shape[:2]
    L = min(q_len, QBLOCK)
    nb = q_len // L

    def split(a):
        return jnp.swapaxes(a.reshape((bsz, nb, L) + a.shape[2:]), 0, 1)

    o = lax.map(lambda blk: mla_attend_block(blk[0], blk[1], blk[2], c, kr, r, kpos),
                (split(q_abs), split(q_rope), qpos.reshape(nb, L)))
    return jnp.swapaxes(o, 0, 1).reshape(bsz, q_len, N_HEADS, KV_RANK)

def mla_mixer(x, pos, c, kr, r, kpos, norm_g, w_dq, q_lat_g, w_uq, qn_g, qr_g, w_o, kn_g, w_uk, w_uv):
    bsz, s, _ = x.shape
    h = rmsnorm(x, norm_g)
    cq = rmsnorm(h @ w_dq, q_lat_g)
    q = jnp.einsum('bsr,rhd->bshd', cq, w_uq)
    qn = rmsnorm(q[..., :D_NOPE], qn_g)
    qr = rope(rmsnorm(q[..., D_NOPE:], qr_g), pos)
    q_abs = jnp.einsum('bshd,rhd->bshr', qn * kn_g, w_uk)
    o_lat = mla_attend(q_abs, qr, pos, c, kr, r, kpos)
    o = jnp.einsum('bshr,rhd->bshd', o_lat, w_uv)
    return o.reshape(bsz, s, N_HEADS * D_V) @ w_o

def trunk(x, pos, past_c, past_kr, p):
    v_rows = []
    c_new = kr_new = c_all = kr_all = r_all = kpos = None
    for layer in range(DEPTH):
        if layer < N_A_LAYERS:
            a = layer
            out, v = chunk_gmlp(x, p['a_norm_g'][a], p['a_w_in'][a], p['a_b_in'][a], p['a_sgu_g'][a],
                                p['a_w_s'][a], p['a_b_s'][a], p['a_w_out'][a], p['a_b_out'][a])
            x = x + out
            v_rows.append(v)
        else:
            if layer == N_A_LAYERS:
                c_new, kr_new = shared_key_side(x, pos, p['kv_norm_g'], p['w_dkv'], p['kv_lat_g'],
                                                p['w_kr'], p['kr_g'])
                if past_c is None:
                    c_all, kr_all, kpos = c_new, kr_new, pos
                else:
                    c_all = jnp.concatenate([past_c, c_new], axis=1)
                    kr_all = jnp.concatenate([past_kr, kr_new], axis=1)
                    kpos = jnp.arange(c_all.shape[1], dtype=jnp.int32)
                w_uk = p['w_uk']
                r_all = lax.map(lambda cb: key_rms_scale(cb, w_uk), c_all)
            b = layer - N_A_LAYERS
            x = x + mla_mixer(x, pos, c_all, kr_all, r_all, kpos, p['b_norm_g'][b], p['b_w_dq'][b],
                              p['b_q_lat_g'][b], p['b_w_uq'][b], p['b_qn_g'][b], p['b_qr_g'][b],
                              p['b_w_o'][b], p['kn_g'], p['w_uk'], p['w_uv'])
        x = x + channel_mixer(x, layer, p)
    return x, c_new, kr_new, jnp.stack(v_rows)

def setup_inputs(seed: int = 0) -> dict:
    key = jax.random.key(seed)
    ks = jax.random.split(key, 40)
    f32 = jnp.float32

    def nrm(k, shape, scale):
        return scale * jax.random.normal(k, shape, f32)

    def gain(k, shape):
        return 1.0 + 0.05 * jax.random.normal(k, shape, f32)

    n_pages = PAST_LEN // PAGE_SIZE
    n_pool = (5 * DEC_BATCH * n_pages) // 4
    perm = jax.random.permutation(ks[4], n_pool)[: DEC_BATCH * n_pages]
    page_table = perm.reshape(DEC_BATCH, n_pages).astype(jnp.int32)
    na, nb = N_A_LAYERS, N_B_LAYERS
    return {
        'x_prompt': nrm(ks[0], (BATCH, SEQ, D_MODEL), 1.0),
        'x_sample': nrm(ks[1], (DEC_BATCH, DEC_SEQ, D_MODEL), 1.0),
        'cache_latent': nrm(ks[2], (n_pool, PAGE_SIZE, KV_RANK), 1.0),
        'cache_krope': nrm(ks[3], (n_pool, PAGE_SIZE, D_ROPE), 1.0),
        'page_table': page_table,
        'a_norm_g': gain(ks[5], (na, D_MODEL)),
        'a_w_in': nrm(ks[6], (na, D_MODEL, 2 * D_GATE), D_MODEL ** -0.5),
        'a_b_in': nrm(ks[7], (na, 2 * D_GATE), 0.02),
        'a_sgu_g': gain(ks[8], (na, D_GATE)),
        'a_w_s': nrm(ks[9], (na, N_GROUPS, CHUNK, CHUNK), CHUNK ** -0.5),
        'a_b_s': 1.0 + nrm(ks[10], (na, N_GROUPS, CHUNK), 0.02),
        'a_w_out': nrm(ks[11], (na, D_GATE, D_MODEL), D_GATE ** -0.5),
        'a_b_out': nrm(ks[12], (na, D_MODEL), 0.02),
        'kv_norm_g': gain(ks[13], (D_MODEL,)),
        'w_dkv': nrm(ks[14], (D_MODEL, KV_RANK), D_MODEL ** -0.5),
        'kv_lat_g': gain(ks[15], (KV_RANK,)),
        'w_kr': nrm(ks[16], (D_MODEL, D_ROPE), D_MODEL ** -0.5),
        'kr_g': gain(ks[17], (D_ROPE,)),
        'kn_g': gain(ks[18], (D_NOPE,)),
        'w_uk': nrm(ks[19], (KV_RANK, N_HEADS, D_NOPE), KV_RANK ** -0.5),
        'w_uv': nrm(ks[20], (KV_RANK, N_HEADS, D_V), KV_RANK ** -0.5),
        'b_norm_g': gain(ks[21], (nb, D_MODEL)),
        'b_w_dq': nrm(ks[22], (nb, D_MODEL, Q_RANK), D_MODEL ** -0.5),
        'b_q_lat_g': gain(ks[23], (nb, Q_RANK)),
        'b_w_uq': nrm(ks[24], (nb, Q_RANK, N_HEADS, D_NOPE + D_ROPE), Q_RANK ** -0.5),
        'b_qn_g': gain(ks[25], (nb, D_NOPE)),
        'b_qr_g': gain(ks[26], (nb, D_ROPE)),
        'b_w_o': nrm(ks[27], (nb, N_HEADS * D_V, D_MODEL), (N_HEADS * D_V) ** -0.5),
        'f_norm_g': gain(ks[28], (DEPTH, D_MODEL)),
        'd_w_gate': nrm(ks[29], (N_DENSE, D_MODEL, D_FF), D_MODEL ** -0.5),
        'd_w_up': nrm(ks[30], (N_DENSE, D_MODEL, D_FF), D_MODEL ** -0.5),
        'd_w_down': nrm(ks[31], (N_DENSE, D_FF, D_MODEL), D_FF ** -0.5),
        'm_w_router': nrm(ks[32], (N_MOE, D_MODEL, N_EXPERTS), D_MODEL ** -0.5),
        'm_w_gate': nrm(ks[33], (N_MOE, N_EXPERTS, D_MODEL, D_FF), D_MODEL ** -0.5),
        'm_w_up': nrm(ks[34], (N_MOE, N_EXPERTS, D_MODEL, D_FF), D_MODEL ** -0.5),
        'm_w_down': nrm(ks[35], (N_MOE, N_EXPERTS, D_FF, D_MODEL), D_FF ** -0.5),
    }

def reference(x_prompt, x_sample, cache_latent, cache_krope, page_table,
              a_norm_g, a_w_in, a_b_in, a_sgu_g, a_w_s, a_b_s, a_w_out, a_b_out,
              kv_norm_g, w_dkv, kv_lat_g, w_kr, kr_g, kn_g, w_uk, w_uv,
              b_norm_g, b_w_dq, b_q_lat_g, b_w_uq, b_qn_g, b_qr_g, b_w_o,
              f_norm_g, d_w_gate, d_w_up, d_w_down, m_w_router, m_w_gate, m_w_up, m_w_down):
    p = {
        'a_norm_g': a_norm_g, 'a_w_in': a_w_in, 'a_b_in': a_b_in, 'a_sgu_g': a_sgu_g,
        'a_w_s': a_w_s, 'a_b_s': a_b_s, 'a_w_out': a_w_out, 'a_b_out': a_b_out,
        'kv_norm_g': kv_norm_g, 'w_dkv': w_dkv, 'kv_lat_g': kv_lat_g, 'w_kr': w_kr, 'kr_g': kr_g,
        'kn_g': kn_g, 'w_uk': w_uk, 'w_uv': w_uv,
        'b_norm_g': b_norm_g, 'b_w_dq': b_w_dq, 'b_q_lat_g': b_q_lat_g, 'b_w_uq': b_w_uq,
        'b_qn_g': b_qn_g, 'b_qr_g': b_qr_g, 'b_w_o': b_w_o,
        'f_norm_g': f_norm_g, 'd_w_gate': d_w_gate, 'd_w_up': d_w_up, 'd_w_down': d_w_down,
        'm_w_router': m_w_router, 'm_w_gate': m_w_gate, 'm_w_up': m_w_up, 'm_w_down': m_w_down,
    }
    pos_p = jnp.arange(x_prompt.shape[1], dtype=jnp.int32)
    y_p, lat_p, kr_p, _ = trunk(x_prompt, pos_p, None, None, p)
    n_seq, n_pages = page_table.shape
    past_len = n_pages * cache_latent.shape[1]
    past_c = cache_latent[page_table].reshape(n_seq, past_len, KV_RANK)
    past_kr = cache_krope[page_table].reshape(n_seq, past_len, D_ROPE)
    pos_s = past_len + jnp.arange(x_sample.shape[1], dtype=jnp.int32)
    y_s, lat_s, kr_s, v_s = trunk(x_sample, pos_s, past_c, past_kr, p)
    return (y_p, y_s, lat_p, kr_p, lat_s, kr_s, v_s)


_drawn_inputs = setup_inputs


def setup_inputs(seed=0):
    import zlib

    import numpy as np

    out = dict(_drawn_inputs(seed))
    spreads = {}
    factors = {'kn_g': 6.11, 'b_qn_g': 6.305, 'b_qr_g': 6.229}
    for name, (base, spread) in spreads.items():
        noise = np.random.default_rng([zlib.crc32(name.encode()), seed]).standard_normal(out[name].shape)
        drawn = base * np.exp(spread * noise) if base else spread * noise
        out[name] = __import__('jax').numpy.asarray(drawn.astype(out[name].dtype))
    for name, factor in factors.items():
        out[name] = (out[name] * factor).astype(out[name].dtype)
    return out
```

```python
import concourse.bass as bass
from concourse import mybir
from contextlib import ExitStack

P = 128
D_MODEL, SEQ, DEC_BATCH, DEC_SEQ = 1024, 256, 8, 8
PAST_LEN, PAGE = 1024, 128
D_GATE, N_GROUPS, N_HEADS = 2048, 8, 8
Q_RANK, KV_RANK, D_NOPE, D_ROPE = 384, 256, 128, 64
D_FF, N_EXPERTS = 2816, 8
EPS = 1e-6
ATTN_SCALE = (D_NOPE + D_ROPE) ** -0.5
MASKED = -1e30

NT = 3
ROWS = [128, 128, DEC_BATCH * DEC_SEQ]
NTOK = sum(ROWS)
NSMP = ROWS[2]
KC = D_MODEL // P
N_PAGES = PAST_LEN // PAGE
FF_CH = D_FF // P
FF_BL = FF_CH // 2
NKEYS = PAST_LEN + NSMP
CAP = 128
MAX_EXTRA = 4
NITEM = N_EXPERTS + MAX_EXTRA

C_ID, C_TRIU, C_CAUS, C_BLK, C_REP, C_NEWM, C_IOTA = 0, 128, 256, 384, 448, 512, 1024
C_VALID, C_PRI, C_EIDX, C_COS, C_SIN = 1152, 1155, 1163, 1179, 1275
C_END = 1371
G_A, G_BU, G_F0, G_KV, G_B, G_QL, G_QN, G_KN, G_F1 = 0, 8, 24, 32, 40, 48, 51, 52, 53
G_END = 61


def tok(t):
    return slice(t * P, t * P + ROWS[t])


def yoco_step(nc, xp, xs_in, c_lat, c_kr, ptab, consts, cols, b_v, sgu_g, w_in, wsT, b_s, w_out, b_out,
              kv_lat_g, kr_g, qr_g, w_ckr, w_uk, w_ukT, w_uv, w_dq, w_uq, w_o, w_router,
              d_gu, d_down, m_gu, m_down, y_p, y_s, lat_p, kr_p, lat_s, kr_s, v_s):
    f32, i32 = mybir.dt.float32, mybir.dt.int32
    ALU, ACT, AX = mybir.AluOpType, mybir.ActivationFunctionType, mybir.AxisListType.X
    MUL, ADD, SUB = ALU.mult, ALU.add, ALU.subtract
    ctx = ExitStack()
    with ctx:
        def sb(name, shape, dt=f32):
            return ctx.enter_context(nc.sbuf_tensor(name, shape, dt))

        def sem(name):
            return ctx.enter_context(nc.semaphore(name))

        X = sb("X", [P, NT, D_MODEL])
        WSLOT, NW = 4096, 5
        W = sb("W", [P, NW * WSLOT])
        K = sb("K", [P, C_END])
        G = sb("G", [P, G_END])
        brow = sb("brow", [P, KV_RANK + 2 * D_ROPE])
        pages_i = sb("pages_i", [1, DEC_BATCH * N_PAGES], i32)
        st = sb("st", [P, 128])
        rs_m, rs_t = sb("rs_m", [P, 64]), sb("rs_t", [P, 64])
        ARENA = 107 * 256
        arena = sb("arena", [P, ARENA])

        def area(kb, *shape):
            at, n = int(kb * 256), 1
            for s in shape:
                n *= s
            assert at + n <= ARENA
            v = arena[:, at:at + n]
            if len(shape) == 2:
                return v.rearrange("p (a b) -> p a b", a=shape[0])
            if len(shape) == 3:
                return v.rearrange("p (a b c) -> p a b c", a=shape[0], b=shape[1])
            if len(shape) == 4:
                return v.rearrange("p (a b c d) -> p a b c d", a=shape[0], b=shape[1], c=shape[2])
            return v

        ident, triu, causal = K[:, C_ID:C_ID + P], K[:, C_TRIU:C_TRIU + P], K[:, C_CAUS:C_CAUS + P]
        iota = K[:, C_IOTA:C_IOTA + P]
        XS = area(60.5, NT, D_MODEL)
        hT = area(72.5, KC, NTOK)
        hbT = area(82.5, KC, NTOK)
        V = area(0, NT, D_GATE)
        uT = area(24, 16, NTOK)
        bv_bc = area(44, D_GATE)
        sgu_bc = area(52, D_GATE)
        vjunk = area(60.5, D_GATE)
        bs_raw = area(102.5, N_GROUPS, P)
        bs_bc = area(82.5, N_GROUPS, NTOK)
        ws = area(92.5, N_GROUPS, P)
        bout_bc = area(96.5, D_MODEL)
        ws_new = area(100.5, N_GROUPS, DEC_BATCH, DEC_SEQ)
        gtmp = area(102.5, 2, NTOK)
        wrep = area(105, N_GROUPS, DEC_SEQ)
        ffT = area(0, FF_CH, NTOK)
        sg = area(28, 2, NTOK)
        wuk = area(0, 2, N_HEADS * D_NOPE)
        wuv = area(8, 2, N_HEADS * P)
        Cn = area(16, NT, KV_RANK)
        KRn = area(19, NT, D_ROPE)
        cTn = area(20, 2, NTOK)
        krTn = area(22.5, NTOK)
        qrP = area(24, N_HEADS, SEQ)
        qrS = area(32, DEC_BATCH, N_HEADS, DEC_SEQ)
        qnT = area(34, N_HEADS, NTOK)
        wukT = area(44, N_HEADS, KV_RANK)
        cqs = area(52, NT, Q_RANK)
        cqT = area(56.5, 3, NTOK)
        Q = area(60.5, NT, N_HEADS, D_NOPE + D_ROPE)
        QR = area(78.5, NT, N_HEADS, D_ROPE)
        qjunk = area(84.5, N_HEADS, D_NOPE + D_ROPE)
        kjunk = area(102.5, N_HEADS, D_NOPE)
        krtmp = area(92.5, NT, D_ROPE)
        rope1, rope2 = area(94.5, N_HEADS, 32), area(95.5, N_HEADS, 32)
        krope1, krope2 = area(93.5, NT, 32), area(94, NT, 32)
        qaP = area(60.5, 2, N_HEADS, SEQ)
        Rb = area(76.5, N_HEADS, SEQ)
        qaS = area(88.5, DEC_BATCH, 2, N_HEADS * DEC_SEQ)
        OLTp = area(34, 2, N_HEADS, SEQ)
        sP = area(52, 2, SEQ)
        PTp = area(54, 2, 2, P)
        cT = area(34, 2, PAST_LEN)
        krT = area(42.25, PAST_LEN)
        S = area(46.35, NKEYS)
        stmp = area(52, NKEYS)
        Rs = area(56.25, NKEYS)
        RsN = area(23.75, NSMP)
        qab = area(25, 2, N_HEADS * DEC_SEQ)
        qrb = area(26, N_HEADS * DEC_SEQ)
        oT = area(60.5, N_HEADS, NTOK)
        sksb = area(74.5, N_PAGES, N_HEADS * DEC_SEQ)
        rnb = area(58, N_HEADS * DEC_SEQ)
        OLTs = area(70.5, DEC_BATCH, 2, N_HEADS, DEC_SEQ)
        Cpg = [area(92.5, N_PAGES, KV_RANK), area(76.5, N_PAGES, KV_RANK)]
        KRpg = [area(100.5, N_PAGES, D_ROPE), area(102.5, N_PAGES, D_ROPE)]
        PT = area(104.5, 9, N_HEADS * DEC_SEQ)
        sjunk = area(84.5, N_HEADS, D_NOPE)
        Sel = area(24, NT, P)
        SelT = area(26, NTOK)
        xgT = area(28, KC, P)
        gsil = area(32, 2, 256)
        hmul = area(34, 2, 256)
        hmT = area(36, 2, 2, P)
        yg = area(38, D_MODEL)
        gt = area(42, 24, 24)
        item_pos = area(45, NITEM, NT)
        item_gate = area(45.5, NITEM, NT)
        posc = area(46, NT)
        gatec = area(46.1, NT)
        gslot = area(46.2, 1)
        ones = area(50, P)
        wr = area(47, KC, N_EXPERTS)
        xtab = area(48, 8, 48)
        cnt_i = sb("cnt_i", [1, 1 + MAX_EXTRA], i32)

        SS, RSTD, SSV, RSV = 0, 4, 8, 12
        SCK, RCK = 16, 24
        SQL, RQL = 32, 36
        SKN = 40
        SQN, SQR = 64, 88
        PMX, PNM, PSUM_, PRC = 112, 114, 116, 118
        SMX, SNM, SSUM, SRC = 120, 121, 122, 123
        sks = sb("sks", [P, N_PAGES, N_HEADS])

        bank = [ctx.enter_context(nc.psum_tensor(f"bank{i}", [P, 512], f32)) for i in range(8)]

        s_const, s_x, s_rows, s_gm, s_mla, s_wr, s_pt = (sem(n) for n in (
            "const_loaded", "x_loaded", "rows_loaded", "gmlp_rows_loaded", "mla_weights_loaded",
            "router_loaded", "page_table_loaded"))
        w_ready = [sem(f"w_ready{i}") for i in range(NW)]
        w_used = sem("w_used")
        s_out, y_out = sem("keys_written"), sem("y_written")
        rnb_done = sem("new_key_rstd")
        s_zero = sem("zeroed")
        v_out = sem("v_rows_written")
        chain = sem("vector_chain")
        achain = sem("scalar_chain")
        x_ready = [sem(f"x_ready{i}") for i in range(5)]
        nsq = [sem(f"norm_squares{i}") for i in range(4)]
        nxs = [sem(f"norm_scaled{i}") for i in range(4)]
        ntr = [sem(f"norm_transposed{i}") for i in range(4)]
        nht = [sem(f"norm_evacuated{i}") for i in range(4)]
        (v_mm, v_biased, v_gelu, v_sq, v_norm, u_mm, u_done, rep_mm, ws_done, mix_mm, gu_done, gout_mm,
         g_mm, silu_done, up_mm, ff_done, dout_mm) = (sem(n) for n in (
             "v_mm", "v_biased", "v_gelu", "v_squares", "v_normed", "u_mm", "u_gelu", "ws_replicated",
             "ws_ready", "mix_mm", "gated", "gmlp_out_mm", "gate_mm", "silu_done", "up_mm", "ff_done",
             "dense_out_mm"))
        (ckr_mm, ckr_sq, c_new, kr_new, dq_mm, dq_sq, cq_scaled, cq_tr, cqT_done, ck_tr, ckT_done, kn_mm,
         kn_sq, kn_red, q_mm, q_copied, q_sq, q_scaled, qn_tr, qr_tr, qnT_done, qrT_done, qa_mm, qa_act, qa_dve,
         rb_mm, rb_done) = (sem(n) for n in (
             "ckr_mm", "ckr_squares", "c_new", "kr_new", "dq_mm", "dq_squares", "cq_scaled",
             "cq_transposed", "cqT_done", "ck_transposed", "ckT_done", "new_key_mm", "new_key_squares",
             "new_key_reduced", "q_mm", "q_copied", "q_squares", "q_scaled", "qn_transposed", "qr_transposed",
             "qnT_done", "qrT_done", "qabs_mm", "qabs_act", "qabs_dve", "r_spread", "r_copied"))
        (ps_mm, ps_max, ps_exp, ps_prob, pp_tr, pp_done, po_mm, po_done, oTp_mm, oTp_done, oTs_mm, oTs_done,
         wo_mm) = (sem(n) for n in (
             "p_scores_mm", "p_max", "p_exp", "p_prob", "p_prob_tr", "p_probT", "p_out_mm", "p_out",
             "oT_prompt_mm", "oT_prompt", "oT_sample_mm", "oT_sample", "wo_mm"))
        pg_ready = [sem("pages_ready0"), sem("pages_ready1")]
        (q_picked, pg_tr, pg_ev, kk_mm, kk_sq, kk_red, kk_rstd, sa_mm, sb_mm, sb_ev, rr_tr, rr_ev, ss_a, ss_done,
         se_exp, se_prob, st_tr, st_done, so_mm, so_done) = (sem(n) for n in (
             "query_picked", "page_transposed", "page_evacuated", "key_mm", "key_squares", "key_reduced",
             "key_rstd", "score_c_mm", "score_r_mm", "score_r_copied", "r_transposed", "r_evacuated",
             "score_c_read", "scores_max", "s_exp", "s_prob", "s_prob_tr", "s_probT", "s_out_mm", "s_out"))
        (lg_mm, lg_max, lg_exp, mask_done, cum_mm, table_done) = (sem(n) for n in (
            "logits_mm", "logits_max", "logits_exp", "routed", "ranks_mm", "tables_done"))
        gu_ready = [sem(f"expert_gu_ready{i}") for i in range(4)]
        dn_ready = [sem(f"expert_down_ready{i}") for i in range(2)]
        (gu_used, dn_used, e_silu, e_h, e_tr, e_trd, sel_done, ga_mm, ga_done, selT_mm, selT_done, y_mm, y_done,
         sc_mm, sc_done) = (sem(n) for n in (
             "expert_gu_mm", "expert_down_used", "expert_silu", "expert_h", "expert_h_tr", "expert_hT",
             "selection_done", "gather_mm", "gathered", "selT_mm", "selT_done", "expert_y_mm",
             "expert_y_gated", "scatter_mm", "scattered"))

        def rows_of(w, a, b):
            return w[a * P:b * P, :].rearrange("(k p) n -> p k n", p=P)

        items = []
        for n in list(range(4, 8)) + list(range(4)):
            items.append((rows_of(w_in, 0, KC)[:, :, n * 512:(n + 1) * 512], KC, 512))
        IT_OUT = len(items)
        items += [(rows_of(w_out, 4 * n, 4 * n + 4), 4, D_MODEL) for n in range(4)]
        IT_GU = len(items)
        items += [(d_gu[n], KC, 512) for n in range(FF_BL)]
        IT_DN = len(items)
        items += [(rows_of(d_down, 4 * n, min(4 * n + 4, FF_CH)), min(4, FF_CH - 4 * n), D_MODEL) for n in range(6)]
        IT_CK = len(items)
        items.append((rows_of(w_ckr, 0, KC), KC, KV_RANK + D_ROPE))
        IT_DQ = len(items)
        items.append((rows_of(w_dq, 0, KC), KC, Q_RANK))
        IT_UQ = len(items)
        items += [(rows_of(w_uq, 0, 3)[:, :, n * 768:(n + 1) * 768], 3, 768) for n in range(2)]
        IT_WO = len(items)
        items += [(rows_of(w_o, 4 * n, 4 * n + 4), 4, D_MODEL) for n in range(2)]

        def weights(n):
            _, k, c = items[n]
            return W[:, n % NW * WSLOT:n % NW * WSLOT + k * c].rearrange("p (k c) -> p k c", k=k)

        def await_item(eng, n):
            eng.wait_ge(w_ready[n % NW], 16 * (n // NW + 1))

        Wgu = [W[:, i * 4096:(i + 1) * 4096].rearrange("p (k c) -> p k c", k=KC) for i in range(4)]
        Wdn = [W[:, 4 * 4096 + i * 2048:4 * 4096 + (i + 1) * 2048].rearrange("p (k c) -> p k c", k=2) for i in range(2)]
        GU_USES, DN_USES = [3, 3, 3, 2], [6, 5]

        def gu_count(e, j):
            return (e * GU_USES[j % 4] + j // 4 + 1) * 16

        def dn_count(e, j):
            return (e * DN_USES[j % 2] + j // 2 + 1) * 16

        MG = {}

        def group(name, n, empties):
            for i in range(n):
                MG[name, i] = (len(MG), *empties(i))

        group("ckr", 3, lambda i: (c_new, i + 1))
        group("dq", 3, lambda i: (cq_scaled, i + 1))
        group("cqT", 3, lambda i: (cqT_done, i + 1))
        group("ckT", 3, lambda i: (ckT_done, i + 1))
        group("kn", 6, lambda i: (kn_sq, i + 1))
        group("q", 12, lambda i: (q_copied, i + 1))
        group("qT", 12, lambda i: (qnT_done, 2 * (i // 4) + i % 4 + 1) if i % 4 < 2 else (qrT_done, 2 * (i // 4) + i % 4 - 1))
        group("qa", 16, lambda i: (qa_dve, i // 2 + 1) if i % 2 else (qa_act, i // 2 + 1))
        group("rb", 5, lambda i: (rb_done, i + 1))
        MGL = list(MG.values())

        def mla_bank(pe, name, i):
            n = MG[name, i][0]
            if pe is not None and n >= 8:
                pe.wait_ge(MGL[n - 8][1], MGL[n - 8][2])
            return bank[n % 8]

        def over_sequences(eng, body):
            body(0, 0, 0, True)
            with eng.Fori(0, DEC_BATCH // 2 - 1) as i:
                body(2 * i + 1, 1, i, False)
                body(2 * i + 2, 0, i + 1, False)
            body(DEC_BATCH - 1, 1, DEC_BATCH // 2 - 1, False)

        def over_passes(eng, body):
            body(0, False, True)
            with eng.Fori(1, N_EXPERTS - 1) as e:
                body(e, True, True)
            body(N_EXPERTS - 1, True, False)

        def further(eng, body):
            eng.wait_ge(table_done, 1)
            n = eng.value_load(cnt_i[0:1, 0:1], min_val=0, max_val=MAX_EXTRA)
            with eng.If(n > 0):
                with eng.Fori(0, n) as i:
                    body(i)

        def wait_pair(eng, used, e, j):
            if not (isinstance(e, int) and e == 0 and j < 2):
                eng.wait_ge(used, 11 * e + j - (0 if j == 0 else 1))

        mm = nc.tensor.matmul
        block = ctx.enter_context(nc.Block())

        @block.sync
        def _(sp):
            for t in range(NT):
                src = xp[t * P:(t + 1) * P, :] if t < 2 else xs_in
                sp.dma_start(X[0:ROWS[t], t, :], src).then_inc(s_x, 16)
            for n, (src, k, c) in enumerate(items):
                if n >= NW:
                    sp.wait_ge(w_used, n - NW + 1)
                if n == IT_CK:
                    sp.wait_ge(x_ready[2], 3)
                    sp.dma_start(wuk[:, :, :], rows_of(w_uk, 0, 2)).then_inc(s_mla, 16)
                    sp.dma_start(wukT[:, :, :], w_ukT).then_inc(s_mla, 16)
                    sp.dma_start(wuv[:, :, :], rows_of(w_uv, 0, 2)).then_inc(s_mla, 16)
                sp.dma_start(weights(n), src).then_inc(w_ready[n % NW], 16)

            def load_gu(e, j, first=False, expert=None):
                if first and j < 4:
                    need = [n for n in range(len(items)) if n % NW == j]
                    sp.wait_ge(w_used, need[-1] + 1)
                elif j >= 4:
                    sp.wait_ge(gu_used, 11 * e + j - 3)
                else:
                    sp.wait_ge(gu_used, 11 * e - 11 + 8 + (j if j < 3 else -1) + 1)
                x = e if expert is None else expert
                src = m_gu[x, j] if isinstance(x, int) else m_gu[bass.ds(x, 1), j].rearrange("a p n -> (a p) n")
                sp.dma_start(Wgu[j % 4], src.rearrange("p (k c) -> p k c", k=KC)).then_inc(gu_ready[j % 4], 16)

            for j in range(FF_BL):
                load_gu(0, j, True)
            with sp.Fori(1, N_EXPERTS) as e:
                for j in range(FF_BL):
                    load_gu(e, j)


            def sp_further(i):
                e = sp.value_load(cnt_i[0:1, bass.ds(i + 1, 1)], min_val=0, max_val=N_EXPERTS - 1)
                for j in range(FF_BL):
                    load_gu(i + N_EXPERTS, j, expert=e)

            further(sp, sp_further)
            sp.wait_ge(x_ready[4], 1)
            for t in range(NT):
                dst = y_p[t * P:(t + 1) * P, :] if t < 2 else y_s
                sp.dma_start(dst, X[0:ROWS[t], t, :]).then_inc(y_out, 16)
            sp.wait_ge(y_out, 16 * NT)
            sp.wait_ge(s_out, 16 * 4)
            sp.wait_ge(v_out, 16)

        @block.gpsimd
        def _(pool):
            pool.dma_start(pages_i[:, :], ptab).then_inc(s_pt, 16)
            pool.wait_ge(v_norm, 3)
            pool.dma_start(v_s, V[0:NSMP, 2, :]).then_inc(v_out, 16)
            pool.wait_ge(c_new, 3)
            pool.dma_start(lat_p.rearrange("(t p) r -> p t r", p=P), Cn[:, 0:2, :]).then_inc(s_out, 16)
            pool.dma_start(lat_s, Cn[0:NSMP, 2, :]).then_inc(s_out, 16)
            pool.wait_ge(kr_new, 1)
            pool.dma_start(kr_p.rearrange("(t p) r -> p t r", p=P), KRn[:, 0:2, :]).then_inc(s_out, 16)
            pool.dma_start(kr_s, KRn[0:NSMP, 2, :]).then_inc(s_out, 16)
            pool.wait_ge(s_pt, 16)

            def load_pages(b, par):
                for p in range(N_PAGES):
                    page = pool.value_load(pages_i[0:1, bass.ds(b * N_PAGES + p, 1)], min_val=0,
                                           max_val=c_lat.shape[0] - 1)
                    pool.dma_start(Cpg[par][:, p, :], c_lat[bass.ds(page, 1)].rearrange("a p r -> (a p) r"))\
                        .then_inc(pg_ready[par], 16)
                    pool.dma_start(KRpg[par][:, p, :], c_kr[bass.ds(page, 1)].rearrange("a p r -> (a p) r"))\
                        .then_inc(pg_ready[par], 16)

            pool.wait_ge(qnT_done, 6)
            pool.wait_ge(qrT_done, 6)
            load_pages(0, 0)
            pool.wait_ge(po_done, 16)
            load_pages(1, 1)
            with pool.Fori(1, DEC_BATCH // 2) as i:
                for par in range(2):
                    pool.wait_ge(so_mm, 2 * i + par - 1)
                    load_pages(2 * i + par, par)

            def load_dn(e, j, expert=None, first=False):
                if first and j < 2:
                    pool.wait_ge(w_used, len(items))
                elif j >= 2:
                    pool.wait_ge(dn_used, 11 * e + j - 1)
                else:
                    pool.wait_ge(dn_used, 11 * e + (0 if j == 0 else -1))
                x = e if expert is None else expert
                src = m_down[x, j] if isinstance(x, int) else m_down[bass.ds(x, 1), j].rearrange("a p n -> (a p) n")
                pool.dma_start(Wdn[j % 2], src.rearrange("p (k c) -> p k c", k=2)).then_inc(dn_ready[j % 2], 16)

            for j in range(FF_BL):
                load_dn(0, j, first=True)
            with pool.Fori(1, N_EXPERTS) as e:
                for j in range(FF_BL):
                    load_dn(e, j)

            def pool_further(i):
                e = pool.value_load(cnt_i[0:1, bass.ds(i + 1, 1)], min_val=0, max_val=N_EXPERTS - 1)
                for j in range(FF_BL):
                    load_dn(i + N_EXPERTS, j, expert=e)

            further(pool, pool_further)

        @block.scalar
        def _(act):
            A = nc.scalar.activation
            act.dma_start(K[:, :], consts).then_inc(s_const, 16)
            act.dma_start(G[:, :], cols).then_inc(s_const, 16)
            act.dma_start(ws[:, :, :], wsT).then_inc(s_gm, 16)
            act.dma_start(bs_raw, b_s.to_broadcast([P, N_GROUPS * P]).rearrange("p (g i) -> p g i", g=N_GROUPS))\
                .then_inc(s_gm, 16)
            act.dma_start(bv_bc, b_v.to_broadcast([P, D_GATE])).then_inc(s_gm, 16)
            act.dma_start(sgu_bc, sgu_g.to_broadcast([P, D_GATE])).then_inc(s_gm, 16)
            act.dma_start(bout_bc, b_out.to_broadcast([P, D_MODEL])).then_inc(s_gm, 16)
            act.dma_start(brow[:, 0:256], kv_lat_g.to_broadcast([P, KV_RANK])).then_inc(s_rows, 16)
            act.dma_start(brow[:, 256:320], kr_g.to_broadcast([P, D_ROPE])).then_inc(s_rows, 16)
            act.dma_start(brow[:, 320:384], qr_g.to_broadcast([P, D_ROPE])).then_inc(s_rows, 16)

            def norm_squares(s):
                for t in range(NT):
                    if s == 0 and t == 0:
                        act.wait_ge(s_x, 16 * NT)
                    elif s:
                        act.wait_ge(x_ready[s], t + 1)
                    A(XS[0:ROWS[t], t, :], X[0:ROWS[t], t, :], ACT.Square, scale=D_MODEL ** -0.5,
                      accum_out=st[0:ROWS[t], SS + t:SS + t + 1]).then_inc(nsq[s], 1)

            act.wait_ge(s_zero, 1)
            norm_squares(0)
            for o in range(12):
                n, t = o // NT, o % NT
                act.wait_ge(v_biased, o + 1)
                v = V[0:ROWS[t], t, n * 512:(n + 1) * 512]
                A(v, v, ACT.Gelu_apprx_tanh).then_inc(v_gelu, 1)
            for t in range(NT):
                act.wait_ge(v_gelu, 12)
                if t:
                    act.wait_ge(v_sq, t)
                A(vjunk[0:ROWS[t], :], V[0:ROWS[t], t, :], ACT.Square, scale=D_GATE ** -0.5,
                  accum_out=st[0:ROWS[t], SSV + t:SSV + t + 1]).then_inc(v_sq, 1)
            for c in range(16):
                act.wait_ge(u_mm, c + 1)
                A(uT[:, c, :], bank[(12 + c) % 8][:, 0:NTOK], ACT.Gelu_apprx_tanh,
                  bias=G[:, G_BU + c:G_BU + c + 1]).then_inc(u_done, 1)

            norm_squares(1)
            for f in range(FF_CH):
                act.wait_ge(g_mm, f + 1)
                if f >= 2:
                    act.wait_ge(ff_done, f - 1)
                A(sg[:, f % 2, :], bank[2 * (f % 4)][:, 0:NTOK], ACT.Silu).then_inc(silu_done, 1)

            norm_squares(2)
            for t in range(NT):
                R = slice(0, ROWS[t])
                act.wait_ge(ckr_mm, t + 1)
                if t:
                    act.wait_ge(ckr_sq, t)
                b = mla_bank(None, "ckr", t)
                A(kjunk[R, 0:2, :], b[R, 0:256].rearrange("p (a b) -> p a b", a=2), ACT.Square, scale=1 / 16,
                  accum_out=st[R, SCK + 2 * t:SCK + 2 * t + 1])
                A(kjunk[R, 2, 0:64], b[R, 256:320], ACT.Square, scale=1 / 8,
                  accum_out=st[R, SCK + 2 * t + 1:SCK + 2 * t + 2]).then_inc(ckr_sq, 1)
            for t in range(NT):
                R = slice(0, ROWS[t])
                act.wait_ge(dq_mm, t + 1)
                if t:
                    act.wait_ge(dq_sq, t)
                else:
                    act.wait_ge(ckr_sq, 3)
                A(kjunk[R, 0:3, :], mla_bank(None, "dq", t)[R, 0:384].rearrange("p (a b) -> p a b", a=3),
                  ACT.Square, scale=Q_RANK ** -0.5, accum_out=st[R, SQL + t:SQL + t + 1]).then_inc(dq_sq, 1)
            for t in range(NT):
                act.wait_ge(ck_tr, t + 1)
                b, n = mla_bank(None, "ckT", t), ROWS[t]
                A(cTn[:, :, tok(t)], b[:, 0:256].rearrange("p (a b) -> p a b", a=2)[:, :, 0:n], ACT.Copy)
                A(krTn[0:64, tok(t)], b[0:64, 256:256 + n], ACT.Copy).then_inc(ckT_done, 1)
            act.wait_ge(dq_sq, 3)
            for o in range(6):
                t, hf = o // 2, o % 2
                R = slice(0, ROWS[t])
                act.wait_ge(kn_mm, o + 1)
                if hf == 0 and t:
                    act.wait_ge(kn_red, t)
                A(kjunk[R, 4 * hf:4 * hf + 4, :], mla_bank(None, "kn", o)[R, :].rearrange("p (h d) -> p h d", h=4),
                  ACT.Square).then_inc(kn_sq, 1)
            for o in range(12):
                t, n = o // 4, o % 4
                R = slice(0, ROWS[t])
                act.wait_ge(q_mm, o + 1)
                A(Q[R, t, 2 * n:2 * n + 2, :], mla_bank(None, "q", o)[R, 0:384].rearrange("p (h d) -> p h d", h=2),
                  ACT.Copy).then_inc(q_copied, 1)
                if n == 3:
                    act.wait_ge(q_copied, o + 1)
                    if t:
                        act.wait_ge(q_scaled, t)
                    A(qjunk[R, :, :], Q[R, t, :, :], ACT.Square).then_inc(q_sq, 1)
            for t in range(NT):
                for n in range(2):
                    act.wait_ge(qr_tr, 2 * t + n + 1)
                    b = mla_bank(None, "qT", 4 * t + 2 + n)
                    if t < 2:
                        out = qrP[0:64, 4 * n:4 * n + 4, tok(t)]
                        A(out, b[0:64, :].rearrange("p (h q) -> p h q", h=4), ACT.Copy).then_inc(qrT_done, 1)
                    else:
                        for hh in range(4):
                            i = A(qrS[0:64, :, 4 * n + hh, :],
                                  b[0:64, hh * P:hh * P + NSMP].rearrange("p (b q) -> p b q", b=8), ACT.Copy)
                        i.then_inc(qrT_done, 1)
            for h in range(N_HEADS):
                act.wait_ge(qa_mm, 2 * h + 1)
                b = mla_bank(None, "qa", 2 * h)
                A(qaP[:, 0, h, :], b[:, 0:SEQ], ACT.Copy)
                A(qaS[:, :, 0, h * 8:h * 8 + 8], b[:, SEQ:NTOK].rearrange("p (b q) -> p b q", b=8), ACT.Copy)\
                    .then_inc(qa_act, 1)
            for n in range(4):
                act.wait_ge(rb_mm, n + 1)
                A(Rb[:, 2 * n:2 * n + 2, :], mla_bank(None, "rb", n).rearrange("p (h q) -> p h q", h=2), ACT.Copy)\
                    .then_inc(rb_done, 1)
            act.wait_ge(rb_mm, 5)
            A(RsN[0:64, :], mla_bank(None, "rb", 4)[0:64, 0:NSMP], ACT.Copy).then_inc(rb_done, 1)

            for it in range(16 + 2):
                if it < 16:
                    par, nk = it % 2, (it % 2 + 1) * P
                    act.wait_ge(ps_max, it + 1)
                    A(sP[:, par, 0:nk], sP[:, par, 0:nk], ACT.Exp, bias=st[:, PNM + par:PNM + par + 1],
                      scale=ATTN_SCALE, accum_out=st[:, PSUM_ + par:PSUM_ + par + 1]).then_inc(ps_exp, 1)
                if 1 <= it <= 16:
                    n, par, nkt = it - 1, (it - 1) % 2, (it - 1) % 2 + 1
                    act.wait_ge(pp_tr, n + 1)
                    if n >= 2:
                        act.wait_ge(po_mm, n - 1)
                    A(PTp[:, par, 0:nkt, :], bank[2 + par][:, 0:nkt * P].rearrange("p (k q) -> p k q", k=nkt),
                      ACT.Copy).then_inc(pp_done, 1)
                if it >= 2:
                    n = it - 2
                    h, qt = n // 2, n % 2
                    act.wait_ge(po_mm, n + 1)
                    A(OLTp[:, :, h, qt * P:(qt + 1) * P], bank[4 + qt][:, 0:2 * P].rearrange("p (r q) -> p r q", r=2),
                      ACT.Copy).then_inc(po_done, 1)
            for h in range(N_HEADS):
                act.wait_ge(oTp_mm, h + 1)
                A(oT[:, h, 0:SEQ], bank[h % 8][:, 0:SEQ], ACT.Copy).then_inc(oTp_done, 1)

            act.wait_ge(rb_done, 5)
            A(Rs[0:64, PAST_LEN:NKEYS], RsN[0:64, :], ACT.Copy).then_inc(achain, 1)

            def evacuate_page(b, p):
                act.wait_ge(pg_tr, 8 * b + p + 1)
                k = bank[4 + p % 2]
                A(cT[:, :, p * P:(p + 1) * P], k[:, 0:2 * P].rearrange("p (r q) -> p r q", r=2), ACT.Copy)
                A(krT[0:64, p * P:(p + 1) * P], k[0:64, 2 * P:3 * P], ACT.Copy).then_inc(pg_ev, 1)

            def evacuate_probs(b):
                act.wait_ge(st_tr, b + 1)
                A(PT[:, 0:8, :], bank[6].rearrange("p (k q) -> p k q", k=8), ACT.Copy)
                A(PT[0:64, 8, :], bank[7][0:64, 0:64], ACT.Copy).then_inc(st_done, 1)

            def seq_act(b, par, kth, first):
                evacuate_page(b, 0)
                for p in range(N_PAGES):
                    if p < N_PAGES - 1:
                        evacuate_page(b, p + 1)
                    act.wait_ge(kk_mm, 8 * b + p + 1)
                    if not (first and p == 0):
                        act.wait_ge(kk_red, 8 * b + p)
                    for hf in range(2):
                        i = A(sjunk[:, 4 * hf:4 * hf + 4, :],
                              bank[2 * (p % 2) + hf].rearrange("p (h d) -> p h d", h=4), ACT.Square)
                    i.then_inc(kk_sq, 1)
                    if p == 3 and not first:
                        evacuate_probs(b - 1)
                for n in range(3):
                    act.wait_ge(sb_mm, 3 * b + n + 1)
                    src = bank[n][0:64, :] if n < 2 else bank[2][0:64, 64:128]
                    A(S[0:64, n * 512:n * 512 + src.shape[1]], src, ACT.Copy).then_inc(sb_ev, 1)
                for n in range(2):
                    act.wait_ge(rr_tr, 2 * b + n + 1)
                    A(Rs[0:64, n * 512:(n + 1) * 512], bank[4 + n][0:64, :], ACT.Copy).then_inc(rr_ev, 1)
                act.wait_ge(ss_done, b + 1)
                A(S[0:64, :], S[0:64, :], ACT.Exp, bias=st[0:64, SNM:SNM + 1], scale=ATTN_SCALE,
                  accum_out=st[0:64, SSUM:SSUM + 1]).then_inc(se_exp, 1)

            over_sequences(act, seq_act)
            evacuate_probs(DEC_BATCH - 1)
            for h in range(N_HEADS):
                act.wait_ge(oTs_mm, h + 1)
                A(oT[:, h, SEQ:NTOK], bank[h % 4][:, 0:NSMP], ACT.Copy).then_inc(oTs_done, 1)

            act.wait_ge(wo_mm, 1)
            act.dma_start(wr[:, :, :], w_router).then_inc(s_wr, 16)
            norm_squares(3)
            act.wait_ge(lg_max, 1)
            A(gt[:, 1, :], gt[:, 1, :], ACT.Exp).then_inc(lg_exp, 1)

            def evacuate_hT(e, j):
                n = 11 * e + j
                act.wait_ge(e_tr, n + 1)
                wait_pair(act, dn_used, e, j)
                A(hmT[:, j % 2, :, :], bank[4 + j % 2][:, 0:2 * P].rearrange("p (k s) -> p k s", k=2),
                  ACT.Copy).then_inc(e_trd, 1)

            def pass_act(e, prev, nxt):
                for j in range(FF_BL):
                    n = 11 * e + j
                    if j:
                        evacuate_hT(e, j - 1)
                    act.wait_ge(gu_used, n + 1)
                    wait_pair(act, e_h, e, j)
                    A(gsil[:, j % 2, :], bank[2 + j % 2][:, 0:256], ACT.Silu).then_inc(e_silu, 1)
                evacuate_hT(e, FF_BL - 1)
                act.wait_ge(y_mm, e + 1)
                act.wait_ge(selT_done, e + 1)
                if not (isinstance(e, int) and e == 0):
                    act.wait_ge(sc_mm, 6 * e)
                for hf in range(2):
                    A(yg[:, hf * 512:(hf + 1) * 512], bank[hf][:, :], ACT.Copy, scale=gslot[:, 0:1]).then_inc(y_done, 1)

            over_passes(act, pass_act)
            further(act, lambda i: pass_act(i + N_EXPERTS, False, False))

        @block.vector
        def _(dve):
            V_ = nc.vector
            TT, TS, STT, RED, CP = V_.tensor_tensor, V_.tensor_scalar, V_.scalar_tensor_tensor, V_.tensor_reduce, V_.tensor_copy
            count = [0]

            def link(ins):
                count[0] = count[0] + 1
                ins.then_inc(chain, 1)
                dve.wait_ge(chain, count[0])

            def rstd(out, mean, scale=1.0):
                n = out.shape[-1]
                R = slice(0, out.shape[0])
                m, t = rs_m[R, 0:n], rs_t[R, 0:n]
                link(TS(m, mean, scale, EPS, MUL, ADD))
                link(TS(out.bitcast(i32), m.bitcast(i32), -0.5, float(0x5F3759DF), MUL, ADD))
                for _ in range(3):
                    link(TT(t, out, out, MUL))
                    link(STT(t, t, -0.5, m, MUL, MUL))
                    link(STT(out, t, 1.5, out, ADD, MUL))

            def gain(col, n, w):
                return G[:, col:col + n].unsqueeze(2).to_broadcast([P, n, w])

            def norm(s, outs):
                for t in range(NT):
                    R = slice(0, ROWS[t])
                    dve.wait_ge(nsq[s], t + 1)
                    rstd(st[R, RSTD + t:RSTD + t + 1], st[R, SS + t:SS + t + 1])
                    TS(XS[R, t, :], X[R, t, :], st[R, RSTD + t:RSTD + t + 1], None, MUL).then_inc(nxs[s], 1)
                for t in range(NT):
                    for hf in range(2):
                        dve.wait_ge(ntr[s], 2 * t + hf + 1)
                        src = bank[2 * t + hf].rearrange("p (k q) -> p k q", k=4)[:, :, 0:ROWS[t]]
                        for out, col in outs:
                            i = TT(out[:, 4 * hf:4 * hf + 4, tok(t)], src, gain(col + 4 * hf, 4, ROWS[t]), MUL)
                        i.then_inc(nht[s], 1)

            def add_residual(done, ready):
                for t in range(NT):
                    for hf in range(2):
                        x = X[0:ROWS[t], t, hf * 512:(hf + 1) * 512]
                        dve.wait_ge(done, 2 * t + hf + 1)
                        i = TT(x, bank[2 * t + hf][0:ROWS[t], :], x, ADD)
                    i.then_inc(ready, 1)

            V_.memset(st[:, :], 0.0)
            V_.memset(sks[:, :, :], 0.0).then_inc(s_zero, 1)
            dve.wait_ge(s_const, 32)
            dve.wait_ge(s_zero, 1)
            dve.wait_ge(s_x, 48)
            norm(0, [(hT, G_A)])
            dve.wait_ge(s_gm, 16 * 5)
            TT(ws[:, :, :], ws[:, :, :], triu.unsqueeze(1).to_broadcast([P, N_GROUPS, P]), MUL).then_inc(ws_done, 1)
            for t in range(2):
                CP(bs_bc[:, :, tok(t)], bs_raw)
            CP(bs_bc[:, :, tok(2)].rearrange("p g (b i) -> p g b i", b=8),
               bs_raw[:, :, 0:8].unsqueeze(2).to_broadcast([P, N_GROUPS, 8, 8]))
            for t in range(NT):
                R = slice(0, ROWS[t])
                i = TT(X[R, t, :], X[R, t, :], bout_bc[R, :], ADD)
            link(i)
            dve.wait_ge(rep_mm, 1)
            link(CP(wrep[0:64, :, :], bank[7][0:64, 0:64].rearrange("p (g i) -> p g i", g=8)))
            for g in range(N_GROUPS):
                i = TT(ws_new[0:64, g, :, :], wrep[0:64, g, :].unsqueeze(1).to_broadcast([64, 8, 8]),
                       K[0:64, C_BLK:C_BLK + 64].rearrange("p (b i) -> p b i", b=8), MUL)
            i.then_inc(ws_done, 1)
            for o in range(12):
                n, t = o // NT, o % NT
                R, c = slice(0, ROWS[t]), slice(n * 512, (n + 1) * 512)
                dve.wait_ge(v_mm, o + 1)
                TT(V[R, t, c], bank[o % 8][R, :], bv_bc[R, c], ADD).then_inc(v_biased, 1)
            for t in range(NT):
                R = slice(0, ROWS[t])
                dve.wait_ge(v_sq, t + 1)
                rstd(st[R, RSV + t:RSV + t + 1], st[R, SSV + t:SSV + t + 1])
                STT(V[R, t, :], V[R, t, :], st[R, RSV + t:RSV + t + 1], sgu_bc[R, :], MUL, MUL).then_inc(v_norm, 1)
            for c in range(16):
                dve.wait_ge(mix_mm, c + 1)
                dve.wait_ge(u_done, c + 1)
                link(TT(gtmp[:, c % 2, :], bank[(28 + c) % 8][:, 0:NTOK], bs_bc[:, c // 2, :], ADD))
                TT(uT[:, c, :], uT[:, c, :], gtmp[:, c % 2, :], MUL).then_inc(gu_done, 1)
            add_residual(gout_mm, x_ready[1])

            norm(1, [(hT, G_F0)])
            dve.wait_ge(v_out, 16)
            for f in range(FF_CH):
                dve.wait_ge(silu_done, f + 1)
                dve.wait_ge(up_mm, f + 1)
                TT(ffT[:, f, :], sg[:, f % 2, :], bank[2 * (f % 4) + 1][:, 0:NTOK], MUL).then_inc(ff_done, 1)
            add_residual(dout_mm, x_ready[2])

            norm(2, [(hT, G_KV), (hbT, G_B)])
            dve.wait_ge(s_rows, 48)
            link(V_.memset(krtmp[:, :, :], 0.0))
            for t in range(NT):
                R = slice(0, ROWS[t])
                b = mla_bank(None, "ckr", t)
                dve.wait_ge(ckr_sq, t + 1)
                rstd(st[R, RCK + 2 * t:RCK + 2 * t + 2], st[R, SCK + 2 * t:SCK + 2 * t + 2])
                STT(krtmp[R, t, :], b[R, 256:320], st[R, RCK + 2 * t + 1:RCK + 2 * t + 2], brow[R, 256:320], MUL, MUL)
                STT(Cn[R, t, :], b[R, 0:256], st[R, RCK + 2 * t:RCK + 2 * t + 1], brow[R, 0:256], MUL, MUL)\
                    .then_inc(c_new, 1)
            dve.wait_ge(c_new, 3)

            def rotate(out, src, cos, sin, a, b):
                x1, x2 = src[:, :, 0:32], src[:, :, 32:64]
                TT(a, x1, cos, MUL)
                link(TT(b, x2, sin, MUL))
                link(TT(out[:, :, 0:32], a, b, SUB))
                TT(a, x1, sin, MUL)
                link(TT(b, x2, cos, MUL))
                return TT(out[:, :, 32:64], a, b, ADD)

            cos3 = K[:, C_COS:C_COS + 96].rearrange("p (t c) -> p t c", t=3)
            sin3 = K[:, C_SIN:C_SIN + 96].rearrange("p (t c) -> p t c", t=3)
            rotate(KRn, krtmp, cos3, sin3, krope1, krope2).then_inc(kr_new, 1)
            for t in range(NT):
                R = slice(0, ROWS[t])
                dve.wait_ge(dq_sq, t + 1)
                rstd(st[R, RQL + t:RQL + t + 1], st[R, SQL + t:SQL + t + 1])
                TS(cqs[R, t, :], mla_bank(None, "dq", t)[R, 0:384], st[R, RQL + t:RQL + t + 1], None, MUL)\
                    .then_inc(cq_scaled, 1)
            for t in range(NT):
                dve.wait_ge(cq_tr, t + 1)
                TT(cqT[:, :, tok(t)], mla_bank(None, "cqT", t)[:, 0:384].rearrange("p (k q) -> p k q", k=3)[:, :, 0:ROWS[t]],
                   gain(G_QL, 3, ROWS[t]), MUL).then_inc(cqT_done, 1)
            skn = st[:, SKN:SKN + 24].rearrange("p (t h) -> p t h", t=3)
            for t in range(NT):
                R = slice(0, ROWS[t])
                dve.wait_ge(kn_sq, 2 * t + 2)
                RED(skn[R, t, :], kjunk[R, :, :], AX, ADD).then_inc(kn_red, 1)
            dve.wait_ge(kn_red, 3)
            rstd(st[:, SKN:SKN + 24], st[:, SKN:SKN + 24], 1.0 / D_NOPE)
            sqn = st[:, SQN:SQN + 24].rearrange("p (t h) -> p t h", t=3)
            sqr = st[:, SQR:SQR + 24].rearrange("p (t h) -> p t h", t=3)
            for t in range(NT):
                R, n = slice(0, ROWS[t]), ROWS[t]
                dve.wait_ge(q_sq, t + 1)
                RED(sqn[R, t, :], qjunk[R, :, 0:D_NOPE], AX, ADD)
                link(RED(sqr[R, t, :], qjunk[R, :, D_NOPE:192], AX, ADD))
                rstd(sqn[R, t, :], sqn[R, t, :], 1.0 / D_NOPE)
                rstd(sqr[R, t, :], sqr[R, t, :], 1.0 / D_ROPE)
                qn, qr = Q[R, t, :, 0:D_NOPE], Q[R, t, :, D_NOPE:192]
                TT(qn, qn, sqn[R, t, :].unsqueeze(2).to_broadcast([n, 8, D_NOPE]), MUL)
                link(TT(qr, qr, sqr[R, t, :].unsqueeze(2).to_broadcast([n, 8, D_ROPE]), MUL))
                link(TT(qr, qr, brow[R, 320:384].unsqueeze(1).to_broadcast([n, 8, D_ROPE]), MUL))
                rotate(QR[R, t, :, :], qr, cos3[R, t, :].unsqueeze(1).to_broadcast([n, 8, 32]),
                       sin3[R, t, :].unsqueeze(1).to_broadcast([n, 8, 32]), rope1[R, :, :], rope2[R, :, :])\
                    .then_inc(q_scaled, 1)
            for t in range(NT):
                for n in range(2):
                    dve.wait_ge(qn_tr, 2 * t + n + 1)
                    TS(qnT[:, 4 * n:4 * n + 4, tok(t)],
                       mla_bank(None, "qT", 4 * t + n).rearrange("p (h q) -> p h q", h=4)[:, :, 0:ROWS[t]],
                       G[:, G_QN:G_QN + 1], G[:, G_KN:G_KN + 1], MUL, MUL).then_inc(qnT_done, 1)
            for h in range(N_HEADS):
                dve.wait_ge(qa_mm, 2 * h + 2)
                b = mla_bank(None, "qa", 2 * h + 1)
                CP(qaP[:, 1, h, :], b[:, 0:SEQ])
                CP(qaS[:, :, 1, h * 8:h * 8 + 8], b[:, SEQ:NTOK].rearrange("p (b q) -> p b q", b=8)).then_inc(qa_dve, 1)

            CP(rnb[0:64, :].rearrange("p (h q) -> p h q", h=8), st[0:64, SKN + 16:SKN + 24].unsqueeze(2).to_broadcast([64, 8, 8]))\
                .then_inc(rnb_done, 1)

            dve.wait_ge(rb_done, 4)
            for it in range(16 + 1):
                if it < 16:
                    h, qt, par = it // 2, it % 2, it % 2
                    nk = (qt + 1) * P
                    s, b = sP[:, par, 0:nk], bank[par]
                    dve.wait_ge(ps_mm, it + 1)
                    if it >= 2:
                        dve.wait_ge(pp_tr, it - 1)
                    link(TT(s, b[:, 0:nk], Rb[:, h, 0:nk], MUL))
                    link(TT(s, b[:, 256:256 + nk], s, ADD))
                    link(TT(sP[:, par, nk - P:nk], sP[:, par, nk - P:nk], causal, ADD))
                    link(RED(st[:, PMX + par:PMX + par + 1], s, AX, ALU.max))
                    TS(st[:, PNM + par:PNM + par + 1], st[:, PMX + par:PMX + par + 1], -ATTN_SCALE, None, MUL)\
                        .then_inc(ps_max, 1)
                if it >= 1:
                    n = it - 1
                    par, nk = n % 2, (n % 2 + 1) * P
                    dve.wait_ge(ps_exp, n + 1)
                    link(V_.reciprocal(st[:, PRC + par:PRC + par + 1], st[:, PSUM_ + par:PSUM_ + par + 1]))
                    TS(sP[:, par, 0:nk], sP[:, par, 0:nk], st[:, PRC + par:PRC + par + 1], None, MUL).then_inc(ps_prob, 1)

            def pick_query(b):
                CP(qab, qaS[:, bass.ds(b, 1), :, :].rearrange("p a r q -> p (a r) q"))
                CP(qrb[0:64], qrS[0:64, bass.ds(b, 1), :, :].rearrange("p a h q -> p (a h q)")).then_inc(q_picked, 1)

            def take_out(b):
                dve.wait_ge(so_mm, b + 1)
                CP(OLTs[:, bass.ds(b, 1), :, :, :].rearrange("p a r h q -> p (a r h q)"), bank[7][:, 128:256])\
                    .then_inc(so_done, 1)

            SEQ_LINKS = 15
            seq_base = count[0]

            def seq_dve(b, par, kth, first):
                count[0] = seq_base + SEQ_LINKS * b
                if first:
                    dve.wait_ge(ps_mm, 16)
                else:
                    dve.wait_ge(sb_mm, 3 * b)
                pick_query(b)
                for p in range(N_PAGES):
                    dve.wait_ge(kk_sq, 8 * b + p + 1)
                    if p == 0 and not first:
                        dve.wait_ge(rr_tr, 2 * b)
                    RED(sks[:, p, :], sjunk, AX, ADD).then_inc(kk_red, 1)
                    if p == 3 and not first:
                        take_out(b - 1)
                dve.wait_ge(kk_red, 8 * b + 8)
                k = sks[:, :, :].rearrange("p a h -> p (a h)")
                rstd(k, k, 1.0 / D_NOPE)
                CP(sksb[:, :, :].rearrange("p a (h q) -> p (a h) q", h=8), k.unsqueeze(2).to_broadcast([P, 64, 8]))\
                    .then_inc(kk_rstd, 1)
                for n in range(2):
                    dve.wait_ge(sa_mm, 2 * b + n + 1)
                    dve.wait_ge(rr_ev, 2 * b + n + 1)
                    c = slice(n * 512, (n + 1) * 512)
                    TT(stmp[0:64, c], bank[6 + n][0:64, :], Rs[0:64, c], MUL).then_inc(ss_a, 1)
                new = slice(PAST_LEN, NKEYS)
                dve.wait_ge(sb_mm, 3 * b + 3)
                TT(stmp[0:64, new], bank[2][0:64, 0:64], Rs[0:64, new], MUL).then_inc(ss_a, 1)
                dve.wait_ge(ss_a, 3 * b + 3)
                link(TT(stmp[0:64, new], stmp[0:64, new],
                        K[0:64, C_NEWM:C_NEWM + 512].rearrange("p (b k) -> p b k", b=8)[:, bass.ds(b, 1), :]
                        .rearrange("p a k -> p (a k)"), ADD))
                dve.wait_ge(sb_ev, 3 * b + 3)
                link(TT(S[0:64, :], stmp[0:64, :], S[0:64, :], ADD))
                link(RED(st[0:64, SMX:SMX + 1], S[0:64, :], AX, ALU.max))
                TS(st[0:64, SNM:SNM + 1], st[0:64, SMX:SMX + 1], -ATTN_SCALE, None, MUL).then_inc(ss_done, 1)
                dve.wait_ge(se_exp, b + 1)
                link(V_.reciprocal(st[0:64, SRC:SRC + 1], st[0:64, SSUM:SSUM + 1]))
                TS(S[0:64, :], S[0:64, :], st[0:64, SRC:SRC + 1], None, MUL).then_inc(se_prob, 1)
                assert not first or count[0] == seq_base + SEQ_LINKS

            over_sequences(dve, seq_dve)
            count[0] = seq_base + SEQ_LINKS * DEC_BATCH
            take_out(DEC_BATCH - 1)
            add_residual(wo_mm, x_ready[3])

            norm(3, [(hT, G_F1)])
            LG, EX, PR, EQ, O1, P2, O2, GA, MK, PO, T0, T1, CUM = 0, 1, 2, 3, 4, 5, 6, 7, 8, 9, 10, 11, 12
            NE, F, FA, FB = 14, 15, 16, 17

            def g(i, w=24):
                return gt[:, i, 0:w]

            def g3(i):
                return gt[:, i, :].rearrange("p (t e) -> p t e", t=3)

            def c3(i):
                return gt[:, 13, 3 * i:3 * i + 3]

            def b3(i):
                return c3(i).unsqueeze(2).to_broadcast([P, 3, 8])

            pri3 = K[:, C_PRI:C_PRI + 8].unsqueeze(1).to_broadcast([P, 3, 8])
            V_.memset(ones, 1.0)
            link(V_.memset(gt[:, :, :], 0.0))
            dve.wait_ge(lg_mm, 1)
            for t in range(NT):
                i = CP(gt[0:ROWS[t], LG, 8 * t:8 * t + 8], bank[0][0:ROWS[t], 8 * t:8 * t + 8])
            link(i)
            link(RED(c3(0), g3(LG), AX, ALU.max))
            TT(g3(EX), g3(LG), b3(0), SUB).then_inc(lg_max, 1)
            dve.wait_ge(lg_exp, 1)
            link(RED(c3(1), g3(EX), AX, ADD))
            link(V_.reciprocal(c3(1), c3(1)))
            link(TT(g3(PR), g3(EX), b3(1), MUL))

            def top(src, c, onehot):
                link(RED(c3(c), g3(src), AX, ALU.max))
                link(TT(g3(EQ), g3(src), b3(c), ALU.is_equal))
                link(TT(g3(EQ), g3(EQ), pri3, MUL))
                link(RED(c3(c + 1), g3(EQ), AX, ALU.max))
                link(TT(g3(onehot), g3(EQ), b3(c + 1), ALU.is_equal))

            top(PR, 2, O1)
            link(STT(g(P2), g(O1), -2.0, g(PR), MUL, ADD))
            top(P2, 4, O2)
            link(TT(c3(6), c3(2), c3(4), ADD))
            link(V_.reciprocal(c3(6), c3(6)))
            link(TT(g3(T0), g3(O1), b3(2), MUL))
            link(TT(g3(T1), g3(O2), b3(4), MUL))
            link(TT(g(T0), g(T0), g(T1), ADD))
            link(TT(g3(GA), g3(T0), b3(6), MUL))
            link(TT(g(MK), g(O1), g(O2), ADD))
            TT(g3(MK), g3(MK), K[:, C_VALID:C_VALID + 3].unsqueeze(2).to_broadcast([P, 3, 8]), MUL).then_inc(mask_done, 1)
            dve.wait_ge(cum_mm, 1)
            CP(g(NE, 8), bank[1][:, 24:32])
            link(TT(g(T0), bank[1][:, 0:24], g(MK), MUL))
            link(TS(g(PO), g(T0), -1.0, None, ADD))
            CP(item_pos[:, 0:8, :], g3(PO).rearrange("p t e -> p e t"))
            CP(item_gate[:, 0:8, :], g3(GA).rearrange("p t e -> p e t"))
            for k in range(2):
                i = TS(gt[:, F, 8 * k:8 * k + 8], g(NE, 8), float(CAP * (k + 1)), None, ALU.is_gt)
            link(i)
            link(CP(g(FA, 16), g(F, 16)))
            a, b = FA, FB
            for sh in (1, 2, 4, 8):
                CP(gt[:, b, 0:sh], gt[:, a, 0:sh])
                link(TT(gt[:, b, sh:16], gt[:, a, sh:16], gt[:, a, 0:16 - sh], ADD))
                a, b = b, a
            link(CP(gt[:, 18, 0:1], gt[:, a, 15:16]))
            link(TT(g(T1, 16), g(a, 16), g(F, 16), SUB))
            for k in range(2):
                xp3 = xtab[:, 0, :].rearrange("p (t k e) -> p t k e", t=3, k=2)
                xg3 = xtab[:, 1, :].rearrange("p (t k e) -> p t k e", t=3, k=2)
                TS(xp3[:, :, k, :], g3(PO), -float(CAP * (k + 1)), None, ADD)
                i = CP(xg3[:, :, k, :], g3(GA))
            link(i)
            for o in range(MAX_EXTRA):
                link(TS(g(T0, 16), g(T1, 16), float(o), None, ALU.is_equal))
                link(TT(g(T0, 16), g(T0, 16), g(F, 16), MUL))
                pick = gt[:, T0, 0:16].unsqueeze(1).to_broadcast([P, 3, 16])
                for x, dst in ((0, item_pos), (1, item_gate)):
                    y = xtab[:, 2 + x, :].rearrange("p (t k) -> p t k", t=3)
                    link(TT(y, xtab[:, x, :].rearrange("p (t k) -> p t k", t=3), pick, MUL))
                    link(RED(dst[:, 8 + o, :], y, AX, ADD))
                link(TT(xtab[:, 4, 0:16], gt[:, T0, 0:16], K[:, C_EIDX:C_EIDX + 16], MUL))
                link(RED(gt[:, 18, o + 1:o + 2], xtab[:, 4, 0:16], AX, ADD))
            CP(cnt_i[0:1, :], gt[0:1, 18, 0:1 + MAX_EXTRA]).then_inc(table_done, 1)

            def select(e, first=False):
                if not first:
                    dve.wait_ge(selT_mm, e)
                CP(gatec, item_gate[:, bass.ds(e, 1), :].rearrange("p a t -> p (a t)"))
                link(CP(posc, item_pos[:, bass.ds(e, 1), :].rearrange("p a t -> p (a t)")))
                for t in range(NT):
                    R = slice(0, ROWS[t])
                    i = TS(Sel[R, t, :], iota[R, :], posc[R, t:t + 1], None, ALU.is_equal)
                i.then_inc(sel_done, 1)

            def gather_out(e):
                for hf in range(2):
                    dve.wait_ge(ga_mm, 2 * e + hf + 1)
                    if hf == 0 and not (isinstance(e, int) and e == 0):
                        dve.wait_ge(gu_used, 11 * e)
                    TT(xgT[:, 4 * hf:4 * hf + 4, :], bank[6 + hf].rearrange("p (k q) -> p k q", k=4),
                       gain(G_F1 + 4 * hf, 4, P), MUL).then_inc(ga_done, 1)

            def scatter_out(e):
                for n in range(6):
                    t, hf = n // 2, n % 2
                    x = X[0:ROWS[t], t, hf * 512:(hf + 1) * 512]
                    dve.wait_ge(sc_mm, 6 * e + n + 1)
                    TT(x, bank[6 + hf][0:ROWS[t], :], x, ADD).then_inc(sc_done, 1)

            def pass_dve(e, prev, nxt):
                for j in range(FF_BL):
                    n = 11 * e + j
                    dve.wait_ge(e_silu, n + 1)
                    wait_pair(dve, e_tr, e, j)
                    TT(hmul[:, j % 2, :], gsil[:, j % 2, :], bank[2 + j % 2][:, 256:512], MUL).then_inc(e_h, 1)
                    if j == 1:
                        if prev:
                            scatter_out(e - 1)
                        dve.wait_ge(selT_mm, e + 1)
                        if not (isinstance(e, int) and e == 0):
                            dve.wait_ge(y_done, 2 * e)
                        CP(SelT, bank[6][:, 0:NTOK])
                        CP(gslot, bank[7][:, 0:1]).then_inc(selT_done, 1)
                        if nxt:
                            count[0] = pass_base + e
                            select(e + 1)
                if nxt:
                    gather_out(e + 1)

            dve.wait_ge(table_done, 1)
            select(0, True)
            gather_out(0)
            pass_base = count[0]
            over_passes(dve, pass_dve)
            count[0] = pass_base + N_EXPERTS - 1
            scatter_out(N_EXPERTS - 1)
            far_base = count[0]

            def dve_further(i):
                count[0] = far_base + i
                select(i + N_EXPERTS)
                gather_out(i + N_EXPERTS)
                pass_dve(i + N_EXPERTS, False, False)
                scatter_out(i + N_EXPERTS)

            further(dve, dve_further)
            dve.drain().then_inc(x_ready[4], 1)

        @block.tensor
        def _(pe):
            T = nc.tensor.transpose

            def norm(s):
                for t in range(NT):
                    pe.wait_ge(nxs[s], t + 1)
                    n = ROWS[t]
                    for hf in range(2):
                        for k in range(4):
                            i = T(bank[2 * t + hf][:, k * P:k * P + n],
                                  XS[0:n, t, (4 * hf + k) * P:(4 * hf + k + 1) * P], ident[0:n, 0:n])
                        i.then_inc(ntr[s], 1)
                pe.wait_ge(nht[s], 6)

            def residual_mm(n0, chunks, lhs, ready, done):
                for c in range(chunks):
                    if c % 4 == 0:
                        await_item(pe, n0 + c // 4)
                    for t in range(NT):
                        for hf in range(2):
                            i = mm(bank[2 * t + hf][0:ROWS[t], :], lhs(c, t),
                                   weights(n0 + c // 4)[:, c % 4, hf * 512:(hf + 1) * 512],
                                   start=(c == 0), stop=(c == chunks - 1))
                            if c == chunks - 1:
                                i.then_inc(done, 1)
                    if c % 4 == 3 or c == chunks - 1:
                        if c == chunks - 1:
                            pe.wait_ge(done, 6)
                            pe.sem_inc(w_used, 1)
                        else:
                            i.then_inc(w_used, 1)

            pe.wait_ge(s_const, 32)
            norm(0)
            pe.wait_ge(ws_done, 1)
            mm(bank[7][0:64, 0:64], K[0:8, C_REP:C_REP + 64], ws[0:8, :, 0:8], start=True, stop=True).then_inc(rep_mm, 1)
            for o in range(12):
                n, t = o // NT, o % NT
                if t == 0:
                    await_item(pe, n)
                if o == 7:
                    pe.wait_ge(ws_done, 2)
                if o >= 8:
                    pe.wait_ge(v_biased, o - 7)
                for k in range(KC):
                    i = mm(bank[o % 8][0:ROWS[t], :], hT[:, k, tok(t)], weights(n)[:, k, :], start=(k == 0), stop=(k == KC - 1))
                i.then_inc(v_mm, 1)
                if t == 2:
                    pe.wait_ge(v_mm, o + 1)
                    pe.sem_inc(w_used, 1)
            for c in range(16):
                n, o = 4 + c // 4, 12 + c
                if c % 4 == 0:
                    await_item(pe, n)
                if o < 20:
                    pe.wait_ge(v_biased, o - 7)
                else:
                    pe.wait_ge(u_done, o - 19)
                for k in range(KC):
                    i = mm(bank[o % 8][:, 0:NTOK], weights(n)[:, k, c % 4 * P:(c % 4 + 1) * P], hT[:, k, :],
                           start=(k == 0), stop=(k == KC - 1))
                i.then_inc(u_mm, 1)
                if c % 4 == 3:
                    pe.wait_ge(u_mm, c + 1)
                    pe.sem_inc(w_used, 1)
            pe.wait_ge(v_norm, 3)
            pe.wait_ge(ws_done, 2)
            for c in range(16):
                o = 28 + c
                if o < 36:
                    pe.wait_ge(u_done, o - 19)
                else:
                    pe.wait_ge(gu_done, o - 35)
                for t in range(2):
                    mm(bank[o % 8][:, tok(t)], V[:, t, c * P:(c + 1) * P], ws[:, c // 2, :], start=True, stop=True)
                mm(bank[o % 8][:, tok(2)], V[0:NSMP, 2, c * P:(c + 1) * P],
                   ws_new[0:NSMP, c // 2, :, :].rearrange("p b i -> p (b i)"), start=True, stop=True).then_inc(mix_mm, 1)
            pe.wait_ge(gu_done, 16)
            residual_mm(IT_OUT, 16, lambda c, t: uT[:, c, tok(t)], None, gout_mm)

            norm(1)
            for f in range(FF_CH):
                n, q = IT_GU + f // 2, f % 2
                if q == 0:
                    await_item(pe, n)
                if f >= 4:
                    pe.wait_ge(ff_done, f - 3)
                for h, done in ((0, g_mm), (1, up_mm)):
                    for k in range(KC):
                        i = mm(bank[2 * (f % 4) + h][:, 0:NTOK], weights(n)[:, k, h * 256 + q * P:h * 256 + (q + 1) * P],
                               hT[:, k, :], start=(k == 0), stop=(k == KC - 1))
                    i.then_inc(done, 1)
                if q == 1:
                    pe.wait_ge(up_mm, f + 1)
                    pe.sem_inc(w_used, 1)
            pe.wait_ge(ff_done, FF_CH)
            residual_mm(IT_DN, FF_CH, lambda c, t: ffT[:, c, tok(t)], None, dout_mm)

            norm(2)
            for name, it, w, src, done in (("ckr", IT_CK, 320, hT, ckr_mm), ("dq", IT_DQ, Q_RANK, hbT, dq_mm)):
                await_item(pe, it)
                for t in range(NT):
                    b = mla_bank(pe, name, t)
                    for k in range(KC):
                        i = mm(b[0:ROWS[t], 0:w], src[:, k, tok(t)], weights(it)[:, k, :], start=(k == 0), stop=(k == KC - 1))
                    i.then_inc(done, 1)
                pe.wait_ge(done, 3)
                pe.sem_inc(w_used, 1)
            for t in range(NT):
                b, n = mla_bank(pe, "cqT", t), ROWS[t]
                pe.wait_ge(cq_scaled, t + 1)
                for k in range(3):
                    i = T(b[:, k * P:k * P + n], cqs[0:n, t, k * P:(k + 1) * P], ident[0:n, 0:n])
                i.then_inc(cq_tr, 1)
            pe.wait_ge(c_new, 3)
            pe.wait_ge(kr_new, 1)
            for t in range(NT):
                b, n = mla_bank(pe, "ckT", t), ROWS[t]
                for r in range(2):
                    T(b[:, r * P:r * P + n], Cn[0:n, t, r * P:(r + 1) * P], ident[0:n, 0:n])
                T(b[0:64, 256:256 + n], KRn[0:n, t, :], ident[0:n, 0:n]).then_inc(ck_tr, 1)
            pe.wait_ge(s_mla, 48)
            for o in range(6):
                t, hf = o // 2, o % 2
                b = mla_bank(pe, "kn", o)
                pe.wait_ge(ckT_done, t + 1)
                for r in range(2):
                    i = mm(b[0:ROWS[t], :], cTn[:, r, tok(t)], wuk[:, r, hf * 512:(hf + 1) * 512], start=(r == 0), stop=(r == 1))
                i.then_inc(kn_mm, 1)
            pe.wait_ge(cqT_done, 3)
            await_item(pe, IT_UQ)
            await_item(pe, IT_UQ + 1)
            for o in range(12):
                t, n = o // 4, o % 4
                b = mla_bank(pe, "q", o)
                for k in range(3):
                    i = mm(b[0:ROWS[t], 0:384], cqT[:, k, tok(t)], weights(IT_UQ + n // 2)[:, k, n % 2 * 384:(n % 2 + 1) * 384],
                           start=(k == 0), stop=(k == 2))
                i.then_inc(q_mm, 1)
            pe.wait_ge(q_mm, 12)
            pe.sem_inc(w_used, 2)
            for t in range(NT):
                n = ROWS[t]
                pe.wait_ge(q_scaled, t + 1)
                for i4 in range(4):
                    b = mla_bank(pe, "qT", 4 * t + i4)
                    for hh in range(4):
                        if i4 < 2:
                            i = T(b[:, hh * P:hh * P + n], Q[0:n, t, 4 * i4 + hh, 0:D_NOPE], ident[0:n, 0:n])
                        else:
                            i = T(b[0:64, hh * P:hh * P + n], QR[0:n, t, 4 * (i4 - 2) + hh, :], ident[0:n, 0:n])
                    i.then_inc(qn_tr if i4 < 2 else qr_tr, 1)
            pe.wait_ge(qnT_done, 6)
            for o in range(16):
                h, r = o // 2, o % 2
                mm(mla_bank(pe, "qa", o)[:, 0:NTOK], wukT[:, h, r * P:(r + 1) * P], qnT[:, h, :], start=True, stop=True)\
                    .then_inc(qa_mm, 1)
            pe.wait_ge(rnb_done, 1)
            skn = st[:, SKN:SKN + 24].rearrange("p (t h) -> p t h", t=3)
            for n in range(4):
                b = mla_bank(pe, "rb", n)
                for h in range(2):
                    for t in range(2):
                        i = mm(b[:, (2 * h + t) * P:(2 * h + t + 1) * P],
                               skn[:, t, 2 * n + h:2 * n + h + 1].to_broadcast([P, P]), ident, start=True, stop=True)
                i.then_inc(rb_mm, 1)
            mm(mla_bank(pe, "rb", 4)[0:64, 0:64], rnb[0:64, :],
               ident[0:64, 0:64], start=True, stop=True).then_inc(rb_mm, 1)

            pe.wait_ge(rb_done, 5)
            pe.wait_ge(qa_dve, 8)
            pe.wait_ge(qrT_done, 6)
            for it in range(16 + 2):
                if it < 16:
                    h, qt = it // 2, it % 2
                    nk, b = (qt + 1) * P, bank[it % 2]
                    if it >= 2:
                        pe.wait_ge(ps_max, it - 1)
                    for r in range(2):
                        mm(b[:, 0:nk], qaP[:, r, h, tok(qt)], cTn[:, r, 0:nk], start=(r == 0), stop=(r == 1))
                    mm(b[:, 256:256 + nk], qrP[0:64, h, tok(qt)], krTn[0:64, 0:nk], start=True, stop=True).then_inc(ps_mm, 1)
                if 1 <= it <= 16:
                    n, nkt = it - 1, (it - 1) % 2 + 1
                    pe.wait_ge(ps_prob, n + 1)
                    if n >= 2:
                        pe.wait_ge(pp_done, n - 1)
                    for k in range(nkt):
                        i = T(bank[2 + n % 2][:, k * P:(k + 1) * P], sP[:, n % 2, k * P:(k + 1) * P], ident)
                    i.then_inc(pp_tr, 1)
                if it >= 2:
                    n, nkt = it - 2, it % 2 + 1
                    pe.wait_ge(pp_done, n + 1)
                    if n >= 2:
                        pe.wait_ge(po_done, n - 1)
                    for r in range(2):
                        for k in range(nkt):
                            i = mm(bank[4 + n % 2][:, r * P:(r + 1) * P], Cn[:, k, r * P:(r + 1) * P], PTp[:, n % 2, k, :],
                                   start=(k == 0), stop=(k == nkt - 1))
                    i.then_inc(po_mm, 1)
            pe.wait_ge(po_done, 16)
            for h in range(N_HEADS):
                for r in range(2):
                    i = mm(bank[h][:, 0:SEQ], wuv[:, r, h * P:(h + 1) * P], OLTp[:, r, h, :], start=(r == 0), stop=(r == 1))
                i.then_inc(oTp_mm, 1)

            pe.wait_ge(oTp_done, 8)

            def page_tr(b, par, p):
                if p < 2:
                    pe.wait_ge(rr_ev, 2 * b) if not isinstance(b, int) or b else None
                if not (isinstance(b, int) and b == 0 and p < 2):
                    pe.wait_ge(pg_ev, 8 * b + p - 1)
                k = bank[4 + p % 2]
                for r in range(2):
                    T(k[:, r * P:(r + 1) * P], Cpg[par][:, p, r * P:(r + 1) * P], ident)
                T(k[0:64, 2 * P:3 * P], KRpg[par][:, p, :], ident).then_inc(pg_tr, 1)

            def outputs_mm(b, par):
                pe.wait_ge(s_const, 32)
                pe.wait_ge(se_prob, b + 1)
                for p in range(N_PAGES):
                    T(bank[6][:, p * 64:(p + 1) * 64], S[0:64, p * P:(p + 1) * P], ident[0:64, 0:64])
                T(bank[7][0:64, 0:64], S[0:64, PAST_LEN:NKEYS], ident[0:64, 0:64]).then_inc(st_tr, 1)
                pe.wait_ge(st_done, b + 1)
                for r in range(2):
                    o = bank[7][:, 128 + r * 64:192 + r * 64]
                    for p in range(N_PAGES):
                        mm(o, Cpg[par][:, p, r * P:(r + 1) * P], PT[:, p, :], start=(p == 0), stop=False)
                    i = mm(o, Cn[0:64, 2, r * P:(r + 1) * P], PT[0:64, 8, :], start=False, stop=True)
                i.then_inc(so_mm, 1)

            def seq_pe(b, par, kth, first):
                pe.wait_ge(pg_ready[par], 256 * kth + 256)
                page_tr(b, par, 0)
                for p in range(N_PAGES):
                    if p < N_PAGES - 1:
                        page_tr(b, par, p + 1)
                    pe.wait_ge(pg_ev, 8 * b + p + 1)
                    if not (first and p < 2):
                        pe.wait_ge(kk_sq, 8 * b + p - 1)
                    if not first and p < 2:
                        pe.wait_ge(sb_ev, 3 * b)
                        pe.wait_ge(ss_a, 3 * b)
                    for hf in range(2):
                        for r in range(2):
                            i = mm(bank[2 * (p % 2) + hf][:, :], cT[:, r, p * P:(p + 1) * P], wuk[:, r, hf * 512:(hf + 1) * 512],
                                   start=(r == 0), stop=(r == 1))
                    i.then_inc(kk_mm, 1)
                    if p == 3 and not first:
                        outputs_mm(b - 1, 1 - par)
                pe.wait_ge(q_picked, b + 1)
                if not first:
                    pe.wait_ge(so_done, b)
                for n in range(2):
                    for r in range(2):
                        i = mm(bank[6 + n][0:64, :], qab[:, r, :], cT[:, r, n * 512:(n + 1) * 512], start=(r == 0), stop=(r == 1))
                    i.then_inc(sa_mm, 1)
                pe.wait_ge(kk_sq, 8 * b + 8)
                for r in range(2):
                    mm(bank[2][0:64, 0:64], qab[:, r, :], cTn[:, r, SEQ:NTOK], start=(r == 0), stop=(r == 1))
                for n in range(2):
                    mm(bank[n][0:64, :], qrb[0:64, :], krT[0:64, n * 512:(n + 1) * 512], start=True, stop=True).then_inc(sb_mm, 1)
                mm(bank[2][0:64, 64:128], qrb[0:64, :], krTn[0:64, SEQ:NTOK], start=True, stop=True).then_inc(sb_mm, 1)
                pe.wait_ge(s_const, 32)
                pe.wait_ge(kk_rstd, b + 1)
                for n in range(2):
                    for p in range(4):
                        i = T(bank[4 + n][0:64, p * P:(p + 1) * P],
                              sksb[:, 4 * n + p, :], ident)
                    i.then_inc(rr_tr, 1)

            over_sequences(pe, seq_pe)
            outputs_mm(DEC_BATCH - 1, 1)
            pe.wait_ge(so_done, 8)
            for h in range(N_HEADS):
                if h >= 4:
                    pe.wait_ge(oTs_done, h - 3)
                for r in range(2):
                    i = mm(bank[h % 4][:, 0:NSMP], wuv[:, r, h * P:(h + 1) * P], OLTs[:, :, r, h, :], start=(r == 0), stop=(r == 1))
                i.then_inc(oTs_mm, 1)
            pe.wait_ge(oTs_done, 8)
            residual_mm(IT_WO, N_HEADS, lambda c, t: oT[:, c, tok(t)], None, wo_mm)

            norm(3)
            pe.wait_ge(s_wr, 16)
            for t in range(NT):
                for k in range(KC):
                    i = mm(bank[0][0:ROWS[t], 8 * t:8 * t + 8], hT[:, k, tok(t)], wr[:, k, :], start=(k == 0), stop=(k == KC - 1))
            i.then_inc(lg_mm, 1)
            pe.wait_ge(mask_done, 1)
            for t in range(NT):
                for u in range(t + 1):
                    mm(bank[1][:, 8 * t:8 * t + 8], triu if u == t else ones, gt[:, 8, 8 * u:8 * u + 8],
                       start=(u == 0), stop=(u == t))
            for u in range(NT):
                i = mm(bank[1][:, 24:32], ones, gt[:, 8, 8 * u:8 * u + 8], start=(u == 0), stop=(u == 2))
            i.then_inc(cum_mm, 1)

            def gather_mm(e, halves=(0, 1)):
                if 0 in halves:
                    pe.wait_ge(sel_done, e + 1)
                for hf in halves:
                    for k in range(4):
                        for t in range(NT):
                            R = slice(0, ROWS[t])
                            i = mm(bank[6 + hf][:, k * P:(k + 1) * P], XS[R, t, (4 * hf + k) * P:(4 * hf + k + 1) * P],
                                   Sel[R, t, :], start=(t == 0), stop=(t == 2))
                    i.then_inc(ga_mm, 1)

            def scatter_mm(e):
                pe.wait_ge(y_done, 2 * e + 2)
                for n in range(6):
                    t, hf = n // 2, n % 2
                    if n >= 2:
                        pe.wait_ge(sc_done, 6 * e + n - 1)
                    mm(bank[6 + hf][0:ROWS[t], :], SelT[:, tok(t)], yg[:, hf * 512:(hf + 1) * 512], start=True, stop=True)\
                        .then_inc(sc_mm, 1)

            def h_tr(e, j):
                pe.wait_ge(e_h, 11 * e + j + 1)
                wait_pair(pe, e_trd, e, j)
                for q in range(2):
                    i = T(bank[4 + j % 2][:, q * P:(q + 1) * P], hmul[:, j % 2, q * P:(q + 1) * P], ident)
                i.then_inc(e_tr, 1)

            def down_mm(e, j):
                pe.wait_ge(e_trd, 11 * e + j + 1)
                pe.wait_ge(dn_ready[j % 2], dn_count(e, j))
                if j == 0 and not (isinstance(e, int) and e == 0):
                    pe.wait_ge(y_done, 2 * e)
                for q in range(2):
                    for hf in range(2):
                        i = mm(bank[hf][:, :], hmT[:, j % 2, q, :], Wdn[j % 2][:, q, hf * 512:(hf + 1) * 512],
                               start=(j == 0 and q == 0), stop=(j == FF_BL - 1 and q == 1))
                i.then_inc(dn_used, 1)

            def pass_pe(e, prev, nxt):
                for j in range(FF_BL):
                    if j == 0:
                        pe.wait_ge(ga_done, 2 * e + 2)
                    pe.wait_ge(gu_ready[j % 4], gu_count(e, j))
                    wait_pair(pe, e_h, e, j)
                    for k in range(KC):
                        if k == 4 and j:
                            h_tr(e, j - 1)
                        i = mm(bank[2 + j % 2][:, :], xgT[:, k, :], Wgu[j % 4][:, k, :], start=(k == 0), stop=(k == KC - 1))
                    i.then_inc(gu_used, 1)
                    if j:
                        down_mm(e, j - 1)
                    if j == 1:
                        if prev:
                            scatter_mm(e - 1)
                            pe.wait_ge(sc_done, 6 * e)
                        for t in range(NT):
                            R = slice(0, ROWS[t])
                            T(bank[6][:, tok(t)], Sel[R, t, :], ident[R, R])
                        for t in range(NT):
                            R = slice(0, ROWS[t])
                            i = mm(bank[7][:, 0:1], Sel[R, t, :], gatec[R, t:t + 1], start=(t == 0), stop=(t == 2))
                        i.then_inc(selT_mm, 1)
                if nxt:
                    pe.wait_ge(selT_done, e + 1)
                    gather_mm(e + 1, (0,))
                h_tr(e, FF_BL - 1)
                if nxt:
                    gather_mm(e + 1, (1,))
                down_mm(e, FF_BL - 1)
                pe.wait_ge(dn_used, 11 * e + 11)
                pe.sem_inc(y_mm, 1)

            gather_mm(0)
            over_passes(pe, pass_pe)
            scatter_mm(N_EXPERTS - 1)

            def pe_further(i):
                e = i + N_EXPERTS
                pe.wait_ge(sc_done, 6 * e)
                gather_mm(e)
                pass_pe(e, False, False)
                scatter_mm(e)

            further(pe, pe_further)


_OUTS = [("y_p", (SEQ, D_MODEL)), ("y_s", (64, D_MODEL)), ("lat_p", (SEQ, KV_RANK)), ("kr_p", (SEQ, D_ROPE)),
         ("lat_s", (64, KV_RANK)), ("kr_s", (64, D_ROPE)), ("v_s", (64, D_GATE))]


def _constants():
    import numpy as np
    K = np.zeros((P, C_END), np.float32)
    r = np.arange(P)
    K[:, C_ID:C_ID + P] = np.eye(P)
    K[:, C_TRIU:C_TRIU + P] = r[:, None] <= r[None, :]
    K[:, C_CAUS:C_CAUS + P] = np.where(r[None, :] <= r[:, None], 0, MASKED)
    K[0:64, C_BLK:C_BLK + 64] = np.kron(np.eye(8), np.ones((8, 8)))
    K[0:8, C_REP:C_REP + 64] = np.tile(np.eye(8), (1, 8))
    h, q, b, b2, s = np.ix_(*[np.arange(8)] * 5)
    new = np.where((b == b2) & (s <= q) & (h >= 0), 0, MASKED)
    K[0:64, C_NEWM:C_NEWM + 512] = new.reshape(64, 512)
    K[:, C_IOTA:C_IOTA + P] = r[None, :]
    K[:, C_VALID:C_VALID + 3] = r[:, None] < np.array(ROWS)[None, :]
    K[:, C_PRI:C_PRI + 8] = np.arange(8, 0, -1)[None, :]
    K[:, C_EIDX:C_EIDX + 16] = np.tile(np.arange(8), 2)[None, :]
    pos = np.stack([r, r + P, PAST_LEN + r % DEC_SEQ], 1).astype(np.float32)
    half = D_ROPE // 2
    inv = np.float32(10000.0) ** (-np.arange(half, dtype=np.float32) / np.float32(half))
    ang = pos[:, :, None] * inv[None, None, :]
    K[:, C_COS:C_COS + 96] = np.cos(ang).reshape(P, 96)
    K[:, C_SIN:C_SIN + 96] = np.sin(ang).reshape(P, 96)
    return K


def kernel(**x):
    import numpy as np
    import concourse.bacc as bacc
    from concourse.bass_utils import run_bass_kernel_spmd

    x = {k: np.asarray(v) for k, v in x.items()}

    def columns(v):
        return v.reshape(-1, P).T

    def gate_up(g, u):
        n = g.shape[0]
        w = np.stack([a.reshape(n, KC, P, FF_BL, 256) for a in (g, u)], 4)
        return np.ascontiguousarray(w.transpose(0, 3, 2, 1, 4, 5)).reshape(n, FF_BL, P, KC * 512)

    G = np.concatenate([columns(x[k].reshape(-1)) if isinstance(k, str) else columns(k) for k in (
        "a_norm_g", x["a_b_in"][0, :D_GATE], x["f_norm_g"][0], "kv_norm_g", "b_norm_g", "b_q_lat_g", "b_qn_g",
        "kn_g", x["f_norm_g"][1])], 1)
    md = x["m_w_down"][0].reshape(N_EXPERTS, FF_BL, 2, P, D_MODEL).transpose(0, 1, 3, 2, 4)
    data = {
        "xp": x["x_prompt"][0], "xs_in": x["x_sample"].reshape(64, D_MODEL), "c_lat": x["cache_latent"],
        "c_kr": x["cache_krope"], "ptab": x["page_table"].reshape(1, -1), "consts": _constants(), "cols": G,
        "b_v": x["a_b_in"][:, D_GATE:], "sgu_g": x["a_sgu_g"], "w_in": x["a_w_in"][0],
        "wsT": x["a_w_s"][0].transpose(2, 0, 1), "b_s": x["a_b_s"].reshape(1, -1), "w_out": x["a_w_out"][0],
        "b_out": x["a_b_out"], "kv_lat_g": x["kv_lat_g"][None], "kr_g": x["kr_g"][None], "qr_g": x["b_qr_g"],
        "w_ckr": np.concatenate([x["w_dkv"], x["w_kr"]], 1), "w_uk": x["w_uk"].reshape(KV_RANK, -1),
        "w_ukT": x["w_uk"].transpose(2, 1, 0), "w_uv": x["w_uv"].reshape(KV_RANK, -1), "w_dq": x["b_w_dq"][0],
        "w_uq": x["b_w_uq"][0].reshape(Q_RANK, -1), "w_o": x["b_w_o"][0],
        "w_router": x["m_w_router"][0].reshape(KC, P, N_EXPERTS).transpose(1, 0, 2),
        "d_gu": gate_up(x["d_w_gate"], x["d_w_up"])[0].reshape(FF_BL, P, KC, 512), "d_down": x["d_w_down"][0],
        "m_gu": gate_up(x["m_w_gate"][0], x["m_w_up"][0]), "m_down": np.ascontiguousarray(md).reshape(N_EXPERTS, FF_BL, P, 2048),
    }
    nc = bacc.Bacc("TRN2", target_bir_lowering=False, num_devices=1)
    arrays, args = {}, {}
    for name, a in data.items():
        a = np.ascontiguousarray(a)
        arrays["in_" + name] = a
        args[name] = nc.dram_tensor("in_" + name, a.shape, mybir.dt.from_np(a.dtype), kind="ExternalInput").ap()
    for name, shape in _OUTS:
        args[name] = nc.dram_tensor("out_" + name, shape, mybir.dt.float32, kind="ExternalOutput").ap()
    yoco_step(nc, **args)
    r = run_bass_kernel_spmd(nc, [arrays], core_ids=[0]).results[0]
    y_p, y_s, lat_p, kr_p, lat_s, kr_s, v_s = (r["out_" + n] for n, _ in _OUTS)
    return (y_p[None], y_s.reshape(8, 8, -1), lat_p[None], kr_p[None], lat_s.reshape(8, 8, -1),
            kr_s.reshape(8, 8, -1), v_s.reshape(1, 8, 8, -1))
```

```python
import concourse.bass as bass
from concourse import mybir
from contextlib import ExitStack

P = 128
D_MODEL, SEQ, DEC_BATCH, DEC_SEQ = 1024, 256, 8, 8
PAST_LEN, PAGE = 1024, 128
D_GATE, N_GROUPS, N_HEADS = 2048, 8, 8
Q_RANK, KV_RANK, D_NOPE, D_ROPE = 384, 256, 128, 64
D_FF, N_EXPERTS = 2816, 8
EPS = 1e-6
ATTN_SCALE = (D_NOPE + D_ROPE) ** -0.5
MASKED = -1e30

NT = 3
ROWS = [128, 128, DEC_BATCH * DEC_SEQ]
NTOK = sum(ROWS)
NSMP = ROWS[2]
KC = D_MODEL // P
N_PAGES = PAST_LEN // PAGE
UNIT = 2048
FF_CH = D_FF // P
FF_BL = FF_CH // 2
NKEYS = PAST_LEN + NSMP
CAP = 128
MAX_EXTRA = 4
NITEM = N_EXPERTS + MAX_EXTRA

C_ID, C_TRIU, C_CAUS, C_BLK, C_REP, C_NEWM, C_IOTA = 0, 128, 256, 384, 448, 512, 1024
C_VALID, C_PRI, C_EIDX, C_COS, C_SIN = 1152, 1155, 1163, 1179, 1275
C_END = 1371
G_A, G_BU, G_F0, G_KV, G_B, G_QL, G_QN, G_KN, G_F1 = 0, 8, 24, 32, 40, 48, 51, 52, 53
G_END = 61


def tok(t):
    return slice(t * P, t * P + ROWS[t])


def yoco_step(nc, xp, xs_in, c_lat, c_kr, ptab, consts, cols, b_v, sgu_g, w_in, wsT, b_s, w_out, b_out,
              kv_lat_g, kr_g, qr_g, w_ckr, w_uk, w_ukT, w_uv, w_dq, w_uq, w_o, w_router,
              d_gu, d_down, m_un, y_p, y_s, lat_p, kr_p, lat_s, kr_s, v_s):
    f32, f32r, i32 = mybir.dt.float32, mybir.dt.float32r, mybir.dt.int32
    ALU, ACT, AX = mybir.AluOpType, mybir.ActivationFunctionType, mybir.AxisListType.X
    MUL, ADD, SUB = ALU.mult, ALU.add, ALU.subtract
    ctx = ExitStack()
    with ctx:
        def sb(name, shape, dt=f32):
            return ctx.enter_context(nc.sbuf_tensor(name, shape, dt))

        def sem(name):
            return ctx.enter_context(nc.semaphore(name))

        WSLOT, NW = 4096, 5
        W_KB = 107
        ARENA = W_KB * 256 + NW * WSLOT
        slab_at = -(-nc.sbuf_base // 32) * 32
        ctx.enter_context(nc.sbuf_tensor("slab", [P, ARENA], f32))
        placed = {}
        X = sb("X", [P, NT, D_MODEL])
        K = sb("K", [P, C_END])
        G = sb("G", [P, G_END])
        brow = sb("brow", [P, KV_RANK + 2 * D_ROPE])
        pages_i = sb("pages_i", [1, DEC_BATCH * N_PAGES], i32)
        st = sb("st", [P, 128])
        rs_m, rs_t = sb("rs_m", [P, 64]), sb("rs_t", [P, 64])

        def area(kb, *shape, r=False):
            n = 1
            for s in shape:
                n *= s
            assert int(kb * 256) + n <= ARENA and kb * 32 == int(kb * 32)
            name = f"at{kb}_{n}" + ("_r" if r else "")
            if name not in placed:
                placed[name] = nc.alloc_sbuf_tensor_at(name.replace(".", "_"), [P, n], f32r if r else f32,
                                                       offset=slab_at + int(kb * 1024))
            v = placed[name][:, :]
            if len(shape) == 2:
                return v.rearrange("p (a b) -> p a b", a=shape[0])
            if len(shape) == 3:
                return v.rearrange("p (a b c) -> p a b c", a=shape[0], b=shape[1])
            if len(shape) == 4:
                return v.rearrange("p (a b c d) -> p a b c d", a=shape[0], b=shape[1], c=shape[2])
            return v

        ident, triu, causal = K[:, C_ID:C_ID + P], K[:, C_TRIU:C_TRIU + P], K[:, C_CAUS:C_CAUS + P]
        iota = K[:, C_IOTA:C_IOTA + P]
        XS = area(60.5, NT, D_MODEL)
        hT = area(72.5, KC, NTOK)
        hbT = area(82.5, KC, NTOK)
        V = area(0, NT, D_GATE)
        uT = area(24, 16, NTOK)
        bv_bc = area(44, D_GATE)
        sgu_bc = area(52, D_GATE)
        vjunk = area(60.5, D_GATE)
        bs_raw = area(102.5, N_GROUPS, P)
        bs_bc = area(82.5, N_GROUPS, NTOK)
        ws = area(92.5, N_GROUPS, P)
        bout_bc = area(96.5, D_MODEL)
        ws_new = area(100.5, N_GROUPS, DEC_BATCH, DEC_SEQ)
        gtmp = area(102.5, 2, NTOK)
        wrep = area(105, N_GROUPS, DEC_SEQ)
        ffT = area(0, FF_CH, NTOK)
        sg = area(28, 2, NTOK)
        wuk = area(0, 2, N_HEADS * D_NOPE)
        wuv = area(8, 2, N_HEADS * P)
        Cn = area(16, NT, KV_RANK)
        KRn = area(19, NT, D_ROPE)
        cTn = area(20, 2, NTOK)
        krTn = area(22.5, NTOK)
        qrP = area(24, N_HEADS, SEQ)
        qrS = area(32, DEC_BATCH, N_HEADS, DEC_SEQ)
        qnT = area(34, N_HEADS, NTOK)
        wukT = area(44, N_HEADS, KV_RANK)
        cqs = area(52, NT, Q_RANK)
        cqT = area(56.5, 3, NTOK)
        Q = area(60.5, NT, N_HEADS, D_NOPE + D_ROPE)
        QR = area(78.5, NT, N_HEADS, D_ROPE)
        qjunk = area(84.5, N_HEADS, D_NOPE + D_ROPE)
        kjunk = area(102.5, N_HEADS, D_NOPE)
        krtmp = area(92.5, NT, D_ROPE)
        rope1, rope2 = area(94.5, N_HEADS, 32), area(95.5, N_HEADS, 32)
        krope1, krope2 = area(93.5, NT, 32), area(94, NT, 32)
        qaP = area(60.5, 2, N_HEADS, SEQ)
        Rb = area(76.5, N_HEADS, SEQ)
        qaS = area(88.5, DEC_BATCH, 2, N_HEADS * DEC_SEQ)
        OLTp = area(34, 2, N_HEADS, SEQ)
        sP = area(52, 2, SEQ)
        PTp = area(54, 2, 2, P)
        cT = area(34, 2, PAST_LEN)
        krT = area(42.25, PAST_LEN)
        S = area(46.34375, NKEYS)
        stmp = area(52, NKEYS)
        Rs = area(56.25, NKEYS)
        RsN = area(23.75, NSMP)
        qab = area(25, 2, N_HEADS * DEC_SEQ)
        qrb = area(26, N_HEADS * DEC_SEQ)
        oT = area(60.5, N_HEADS, NTOK)
        sksb = area(74.5, N_PAGES, N_HEADS * DEC_SEQ)
        rnb = area(58, N_HEADS * DEC_SEQ)
        OLTs = area(70.5, DEC_BATCH, 2, N_HEADS, DEC_SEQ)
        Cpg = [area(92.5, N_PAGES, KV_RANK), area(76.5, N_PAGES, KV_RANK)]
        KRpg = [area(100.5, N_PAGES, D_ROPE), area(102.5, N_PAGES, D_ROPE)]
        PT = area(104.5, 9, N_HEADS * DEC_SEQ)
        sjunk = area(84.5, N_HEADS, D_NOPE)
        at_raw = [W_KB + 8 * i for i in range(9)]
        raw = [area(k, UNIT) for k in at_raw]
        low_part = [area(k, UNIT, r=True) for k in at_raw]
        high_part = [area(k, UNIT, r=True) for k in (W_KB + 72, 0, 8, 16, 24, 72.5)]
        Sel = area(32, NT, P, r=True)
        SelT = area(34, NTOK, r=True)
        xg = area(36, KC, P)
        xgT = (area(40, KC, P, r=True), area(44, KC, P, r=True))
        gsil = area(48, 2, 256)
        hmul = area(50, 2, 256)
        hmT = (area(52, 2, 2, P, r=True), area(54, 2, 2, P, r=True))
        yg = area(56, D_MODEL)
        ygp = (area(94.5, D_MODEL, r=True), area(98.5, D_MODEL, r=True))
        XSp = (area(82.5, NT, D_MODEL, r=True), area(60.5, NT, D_MODEL, r=True))
        gt = area(102.5, 24, 24)
        item_pos = area(105, NITEM, NT)
        item_gate = area(105.25, NITEM, NT)
        posc = area(105.5, NT)
        gatec = area(105.59375, NT)
        gslot = area(105.6875, 1)
        wr = area(106.5, KC, N_EXPERTS)
        xtab = area(80.5, 8, 48)
        ones = area(82, P)
        cnt_i = sb("cnt_i", [1, 1 + MAX_EXTRA], i32)

        SS, RSTD, SSV, RSV = 0, 4, 8, 12
        SCK, RCK = 16, 24
        SQL, RQL = 32, 36
        SKN = 40
        SQN, SQR = 64, 88
        PMX, PNM, PSUM_, PRC = 112, 114, 116, 118
        SMX, SNM, SSUM, SRC = 120, 121, 122, 123
        sks = sb("sks", [P, N_PAGES, N_HEADS])

        bank = [ctx.enter_context(nc.psum_tensor(f"bank{i}", [P, 512], f32)) for i in range(8)]

        s_const, s_x, s_rows, s_gm, s_mla, s_wr, s_pt = (sem(n) for n in (
            "const_loaded", "x_loaded", "rows_loaded", "gmlp_rows_loaded", "mla_weights_loaded",
            "router_loaded", "page_table_loaded"))
        w_ready = [sem(f"w_ready{i}") for i in range(NW)]
        w_used = sem("w_used")
        s_out, y_out = sem("keys_written"), sem("y_written")
        rnb_done = sem("new_key_rstd")
        s_zero = sem("zeroed")
        v_out = sem("v_rows_written")
        chain = sem("vector_chain")
        achain = sem("scalar_chain")
        x_ready = [sem(f"x_ready{i}") for i in range(5)]
        nsq = [sem(f"norm_squares{i}") for i in range(4)]
        nxs = [sem(f"norm_scaled{i}") for i in range(4)]
        ntr = [sem(f"norm_transposed{i}") for i in range(4)]
        nht = [sem(f"norm_evacuated{i}") for i in range(4)]
        (v_mm, v_biased, v_gelu, v_sq, v_norm, u_mm, u_done, rep_mm, ws_done, mix_mm, gu_done, gout_mm,
         g_mm, silu_done, up_mm, ff_done, dout_mm) = (sem(n) for n in (
             "v_mm", "v_biased", "v_gelu", "v_squares", "v_normed", "u_mm", "u_gelu", "ws_replicated",
             "ws_ready", "mix_mm", "gated", "gmlp_out_mm", "gate_mm", "silu_done", "up_mm", "ff_done",
             "dense_out_mm"))
        (ckr_mm, ckr_sq, c_new, kr_new, dq_mm, dq_sq, cq_scaled, cq_tr, cqT_done, ck_tr, ckT_done, kn_mm,
         kn_sq, kn_red, q_mm, q_copied, q_sq, q_scaled, qn_tr, qr_tr, qnT_done, qrT_done, qa_mm, qa_act, qa_dve,
         rb_mm, rb_done) = (sem(n) for n in (
             "ckr_mm", "ckr_squares", "c_new", "kr_new", "dq_mm", "dq_squares", "cq_scaled",
             "cq_transposed", "cqT_done", "ck_transposed", "ckT_done", "new_key_mm", "new_key_squares",
             "new_key_reduced", "q_mm", "q_copied", "q_squares", "q_scaled", "qn_transposed", "qr_transposed",
             "qnT_done", "qrT_done", "qabs_mm", "qabs_act", "qabs_dve", "r_spread", "r_copied"))
        (ps_mm, ps_max, ps_exp, ps_prob, pp_tr, pp_done, po_mm, po_done, oTp_mm, oTp_done, oTs_mm, oTs_done,
         wo_mm) = (sem(n) for n in (
             "p_scores_mm", "p_max", "p_exp", "p_prob", "p_prob_tr", "p_probT", "p_out_mm", "p_out",
             "oT_prompt_mm", "oT_prompt", "oT_sample_mm", "oT_sample", "wo_mm"))
        pg_ready = [sem("pages_ready0"), sem("pages_ready1")]
        (q_picked, pg_tr, pg_ev, kk_mm, kk_sq, kk_red, kk_rstd, sa_mm, sb_mm, sb_ev, rr_tr, rr_ev, ss_a, ss_done,
         se_exp, se_prob, st_tr, st_done, so_mm, so_done) = (sem(n) for n in (
             "query_picked", "page_transposed", "page_evacuated", "key_mm", "key_squares", "key_reduced",
             "key_rstd", "score_c_mm", "score_r_mm", "score_r_copied", "r_transposed", "r_evacuated",
             "score_c_read", "scores_max", "s_exp", "s_prob", "s_prob_tr", "s_probT", "s_out_mm", "s_out"))
        (lg_mm, lg_max, lg_exp, mask_done, cum_mm, table_done) = (sem(n) for n in (
            "logits_mm", "logits_max", "logits_exp", "routed", "ranks_mm", "tables_done"))
        raw_ready = [sem(f"unit_loaded{i}") for i in range(9)]
        (u_hi, u_lo, unit_used, xs_hi, xs_lo, e_low, xg_hi, xg_lo, y_hi, y_lo, e_silu, e_h, e_tr, e_trd, sel_done, ga_mm, ga_done, selT_mm, selT_done, y_done,
         sc_mm, sc_done) = (sem(n) for n in (
             "unit_high", "unit_split", "unit_used", "rows_high", "rows_split", "expert_hT_split", "gathered_high",
             "gathered_split", "y_high", "y_split", "expert_silu", "expert_h", "expert_h_tr", "expert_hT",
             "selection_done", "gather_mm", "gathered", "selT_mm", "selT_done",
             "expert_y_gated", "scatter_mm", "scattered"))

        def rows_of(w, a, b):
            return w[a * P:b * P, :].rearrange("(k p) n -> p k n", p=P)

        items = []
        for n in list(range(4, 8)) + list(range(4)):
            items.append((rows_of(w_in, 0, KC)[:, :, n * 512:(n + 1) * 512], KC, 512))
        IT_OUT = len(items)
        items += [(rows_of(w_out, 4 * n, 4 * n + 4), 4, D_MODEL) for n in range(4)]
        IT_GU = len(items)
        items += [(d_gu[n], KC, 512) for n in range(FF_BL)]
        IT_DN = len(items)
        items += [(rows_of(d_down, 4 * n, min(4 * n + 4, FF_CH)), min(4, FF_CH - 4 * n), D_MODEL) for n in range(6)]
        IT_CK = len(items)
        items.append((rows_of(w_ckr, 0, KC), KC, KV_RANK + D_ROPE))
        IT_DQ = len(items)
        items.append((rows_of(w_dq, 0, KC), KC, Q_RANK))
        IT_UQ = len(items)
        items += [(rows_of(w_uq, 0, 3)[:, :, n * 768:(n + 1) * 768], 3, 768) for n in range(2)]
        IT_WO = len(items)
        items += [(rows_of(w_o, 4 * n, 4 * n + 4), 4, D_MODEL) for n in range(2)]

        def weights(n):
            _, k, c = items[n]
            return area(W_KB + n % NW * 16, k, c)

        def await_item(eng, n):
            eng.wait_ge(w_ready[n % NW], 16 * (n // NW + 1))

        NU = 3 * FF_BL

        def pos_gu(j, half):
            return 2 * j + half + max(0, j - 2)

        def pos_dn(j):
            return min(3 * j + 6, NU - FF_BL + j)

        def cycle(groups):
            slots = [i for n in groups for i in range(n)]
            assert len(slots) == NU
            last = [max(k for k in range(-NU, q) if slots[k % NU] == slots[q]) for q in range(NU)]
            return slots, last, [slots[:q].count(slots[q]) for q in range(NU)]

        raw_slot, raw_last, raw_nth = cycle([9] + [8] * 3)
        hi_slot, hi_last, _ = cycle([6] * 3 + [5] * 3)

        SCATTER_AT = {3: (0, 1), 4: (2, 3), 5: (4, 5)}
        SELECT_AT = 6
        GATHER_AT = {7: 0, 8: 1}

        def split_in(j, nxt):
            a = pos_gu(j, 0) + 4
            early, late = ([], [5]) if j == 0 else ([a], [a + 1] if j in (1, FF_BL - 1) else [a + 1, a + 2])
            return [[q for q in x if q < NU or nxt] for x in (early, late)]

        LAST_SPLIT = range(NU + 1, NU + 5)

        def unit_parts(q):
            return high_part[hi_slot[q]], low_part[raw_slot[q]]

        def raw_count(e, q):
            return (e * raw_slot.count(raw_slot[q]) + raw_nth[q] + 1) * 16

        def wait_last(eng, done, e, last):
            if not (isinstance(e, int) and NU * e + last < 0):
                eng.wait_ge(done, NU * e + last + 1)

        MG = {}

        def group(name, n, empties):
            for i in range(n):
                MG[name, i] = (len(MG), *empties(i))

        group("ckr", 3, lambda i: (c_new, i + 1))
        group("dq", 3, lambda i: (cq_scaled, i + 1))
        group("cqT", 3, lambda i: (cqT_done, i + 1))
        group("ckT", 3, lambda i: (ckT_done, i + 1))
        group("kn", 6, lambda i: (kn_sq, i + 1))
        group("q", 12, lambda i: (q_copied, i + 1))
        group("qT", 12, lambda i: (qnT_done, 2 * (i // 4) + i % 4 + 1) if i % 4 < 2 else (qrT_done, 2 * (i // 4) + i % 4 - 1))
        group("qa", 16, lambda i: (qa_dve, i // 2 + 1) if i % 2 else (qa_act, i // 2 + 1))
        group("rb", 5, lambda i: (rb_done, i + 1))
        MGL = list(MG.values())

        def mla_bank(pe, name, i):
            n = MG[name, i][0]
            if pe is not None and n >= 8:
                pe.wait_ge(MGL[n - 8][1], MGL[n - 8][2])
            return bank[n % 8]

        def over_sequences(eng, body):
            body(0, 0, 0, True)
            with eng.Fori(0, DEC_BATCH // 2 - 1) as i:
                body(2 * i + 1, 1, i, False)
                body(2 * i + 2, 0, i + 1, False)
            body(DEC_BATCH - 1, 1, DEC_BATCH // 2 - 1, False)

        def over_passes(eng, body):
            body(0, False, True)
            with eng.Fori(1, N_EXPERTS - 1) as e:
                body(e, True, True)
            body(N_EXPERTS - 1, True, False)

        def further(eng, body):
            eng.wait_ge(table_done, 1)
            n = eng.value_load(cnt_i[0:1, 0:1], min_val=0, max_val=MAX_EXTRA)
            with eng.If(n > 0):
                with eng.Fori(0, n) as i:
                    body(i)

        def wait_pair(eng, used, e, j):
            if not (isinstance(e, int) and e == 0 and j < 2):
                eng.wait_ge(used, 11 * e + j - (0 if j == 0 else 1))

        mm = nc.tensor.matmul
        block = ctx.enter_context(nc.Block())

        @block.sync
        def _(sp):
            for t in range(NT):
                src = xp[t * P:(t + 1) * P, :] if t < 2 else xs_in
                sp.dma_start(X[0:ROWS[t], t, :], src).then_inc(s_x, 16)
            for n, (src, k, c) in enumerate(items):
                if n >= NW:
                    sp.wait_ge(w_used, n - NW + 1)
                if n == IT_CK:
                    sp.wait_ge(x_ready[2], 3)
                    sp.dma_start(wuk[:, :, :], rows_of(w_uk, 0, 2)).then_inc(s_mla, 16)
                    sp.dma_start(wukT[:, :, :], w_ukT).then_inc(s_mla, 16)
                    sp.dma_start(wuv[:, :, :], rows_of(w_uv, 0, 2)).then_inc(s_mla, 16)
                sp.dma_start(weights(n), src).then_inc(w_ready[n % NW], 16)

            def load_unit(e, q, expert=None):
                wait_last(sp, unit_used, e, raw_last[q])
                x = e if expert is None else expert
                src = m_un[x, q] if isinstance(x, int) else m_un[bass.ds(x, 1), q].rearrange("a p n -> (a p) n")
                sp.dma_start(raw[raw_slot[q]], src).then_inc(raw_ready[raw_slot[q]], 16)

            for q in range(NU):
                if q < 9:
                    sp.wait_ge(w_used, len(items) - NW + q // 2 + 1)
                load_unit(0, q)
            with sp.Fori(1, N_EXPERTS) as e:
                for q in range(NU):
                    load_unit(e, q)

            def sp_further(i):
                e = sp.value_load(cnt_i[0:1, bass.ds(i + 1, 1)], min_val=0, max_val=N_EXPERTS - 1)
                for q in range(NU):
                    load_unit(i + N_EXPERTS, q, expert=e)

            further(sp, sp_further)
            sp.wait_ge(x_ready[4], 1)
            for t in range(NT):
                dst = y_p[t * P:(t + 1) * P, :] if t < 2 else y_s
                sp.dma_start(dst, X[0:ROWS[t], t, :]).then_inc(y_out, 16)
            sp.wait_ge(y_out, 16 * NT)
            sp.wait_ge(s_out, 16 * 4)
            sp.wait_ge(v_out, 16)

        @block.gpsimd
        def _(pool):
            pool.dma_start(pages_i[:, :], ptab).then_inc(s_pt, 16)
            pool.wait_ge(v_norm, 3)
            pool.dma_start(v_s, V[0:NSMP, 2, :]).then_inc(v_out, 16)
            pool.wait_ge(c_new, 3)
            pool.dma_start(lat_p.rearrange("(t p) r -> p t r", p=P), Cn[:, 0:2, :]).then_inc(s_out, 16)
            pool.dma_start(lat_s, Cn[0:NSMP, 2, :]).then_inc(s_out, 16)
            pool.wait_ge(kr_new, 1)
            pool.dma_start(kr_p.rearrange("(t p) r -> p t r", p=P), KRn[:, 0:2, :]).then_inc(s_out, 16)
            pool.dma_start(kr_s, KRn[0:NSMP, 2, :]).then_inc(s_out, 16)
            pool.wait_ge(s_pt, 16)

            def load_pages(b, par):
                for p in range(N_PAGES):
                    page = pool.value_load(pages_i[0:1, bass.ds(b * N_PAGES + p, 1)], min_val=0,
                                           max_val=c_lat.shape[0] - 1)
                    pool.dma_start(Cpg[par][:, p, :], c_lat[bass.ds(page, 1)].rearrange("a p r -> (a p) r"))\
                        .then_inc(pg_ready[par], 16)
                    pool.dma_start(KRpg[par][:, p, :], c_kr[bass.ds(page, 1)].rearrange("a p r -> (a p) r"))\
                        .then_inc(pg_ready[par], 16)

            pool.wait_ge(qnT_done, 6)
            pool.wait_ge(qrT_done, 6)
            load_pages(0, 0)
            pool.wait_ge(po_done, 16)
            load_pages(1, 1)
            with pool.Fori(1, DEC_BATCH // 2) as i:
                for par in range(2):
                    pool.wait_ge(so_mm, 2 * i + par - 1)
                    load_pages(2 * i + par, par)

        @block.scalar
        def _(act):
            A = nc.scalar.activation
            act.dma_start(K[:, :], consts).then_inc(s_const, 16)
            act.dma_start(G[:, :], cols).then_inc(s_const, 16)
            act.dma_start(ws[:, :, :], wsT).then_inc(s_gm, 16)
            act.dma_start(bs_raw, b_s.to_broadcast([P, N_GROUPS * P]).rearrange("p (g i) -> p g i", g=N_GROUPS))\
                .then_inc(s_gm, 16)
            act.dma_start(bv_bc, b_v.to_broadcast([P, D_GATE])).then_inc(s_gm, 16)
            act.dma_start(sgu_bc, sgu_g.to_broadcast([P, D_GATE])).then_inc(s_gm, 16)
            act.dma_start(bout_bc, b_out.to_broadcast([P, D_MODEL])).then_inc(s_gm, 16)
            act.dma_start(brow[:, 0:256], kv_lat_g.to_broadcast([P, KV_RANK])).then_inc(s_rows, 16)
            act.dma_start(brow[:, 256:320], kr_g.to_broadcast([P, D_ROPE])).then_inc(s_rows, 16)
            act.dma_start(brow[:, 320:384], qr_g.to_broadcast([P, D_ROPE])).then_inc(s_rows, 16)

            def norm_squares(s):
                for t in range(NT):
                    if s == 0 and t == 0:
                        act.wait_ge(s_x, 16 * NT)
                    elif s:
                        act.wait_ge(x_ready[s], t + 1)
                    A(XS[0:ROWS[t], t, :], X[0:ROWS[t], t, :], ACT.Square, scale=D_MODEL ** -0.5,
                      accum_out=st[0:ROWS[t], SS + t:SS + t + 1]).then_inc(nsq[s], 1)

            act.wait_ge(s_zero, 1)
            norm_squares(0)
            for o in range(12):
                n, t = o // NT, o % NT
                act.wait_ge(v_biased, o + 1)
                v = V[0:ROWS[t], t, n * 512:(n + 1) * 512]
                A(v, v, ACT.Gelu_apprx_tanh).then_inc(v_gelu, 1)
            for t in range(NT):
                act.wait_ge(v_gelu, 12)
                if t:
                    act.wait_ge(v_sq, t)
                A(vjunk[0:ROWS[t], :], V[0:ROWS[t], t, :], ACT.Square, scale=D_GATE ** -0.5,
                  accum_out=st[0:ROWS[t], SSV + t:SSV + t + 1]).then_inc(v_sq, 1)
            for c in range(16):
                act.wait_ge(u_mm, c + 1)
                A(uT[:, c, :], bank[(12 + c) % 8][:, 0:NTOK], ACT.Gelu_apprx_tanh,
                  bias=G[:, G_BU + c:G_BU + c + 1]).then_inc(u_done, 1)

            norm_squares(1)
            for f in range(FF_CH):
                act.wait_ge(g_mm, f + 1)
                if f >= 2:
                    act.wait_ge(ff_done, f - 1)
                A(sg[:, f % 2, :], bank[2 * (f % 4)][:, 0:NTOK], ACT.Silu).then_inc(silu_done, 1)

            norm_squares(2)
            for t in range(NT):
                R = slice(0, ROWS[t])
                act.wait_ge(ckr_mm, t + 1)
                if t:
                    act.wait_ge(ckr_sq, t)
                b = mla_bank(None, "ckr", t)
                A(kjunk[R, 0:2, :], b[R, 0:256].rearrange("p (a b) -> p a b", a=2), ACT.Square, scale=1 / 16,
                  accum_out=st[R, SCK + 2 * t:SCK + 2 * t + 1])
                A(kjunk[R, 2, 0:64], b[R, 256:320], ACT.Square, scale=1 / 8,
                  accum_out=st[R, SCK + 2 * t + 1:SCK + 2 * t + 2]).then_inc(ckr_sq, 1)
            for t in range(NT):
                R = slice(0, ROWS[t])
                act.wait_ge(dq_mm, t + 1)
                if t:
                    act.wait_ge(dq_sq, t)
                else:
                    act.wait_ge(ckr_sq, 3)
                A(kjunk[R, 0:3, :], mla_bank(None, "dq", t)[R, 0:384].rearrange("p (a b) -> p a b", a=3),
                  ACT.Square, scale=Q_RANK ** -0.5, accum_out=st[R, SQL + t:SQL + t + 1]).then_inc(dq_sq, 1)
            for t in range(NT):
                act.wait_ge(ck_tr, t + 1)
                b, n = mla_bank(None, "ckT", t), ROWS[t]
                A(cTn[:, :, tok(t)], b[:, 0:256].rearrange("p (a b) -> p a b", a=2)[:, :, 0:n], ACT.Copy)
                A(krTn[0:64, tok(t)], b[0:64, 256:256 + n], ACT.Copy).then_inc(ckT_done, 1)
            act.wait_ge(dq_sq, 3)
            for o in range(6):
                t, hf = o // 2, o % 2
                R = slice(0, ROWS[t])
                act.wait_ge(kn_mm, o + 1)
                if hf == 0 and t:
                    act.wait_ge(kn_red, t)
                A(kjunk[R, 4 * hf:4 * hf + 4, :], mla_bank(None, "kn", o)[R, :].rearrange("p (h d) -> p h d", h=4),
                  ACT.Square).then_inc(kn_sq, 1)
            for o in range(12):
                t, n = o // 4, o % 4
                R = slice(0, ROWS[t])
                act.wait_ge(q_mm, o + 1)
                A(Q[R, t, 2 * n:2 * n + 2, :], mla_bank(None, "q", o)[R, 0:384].rearrange("p (h d) -> p h d", h=2),
                  ACT.Copy).then_inc(q_copied, 1)
                if n == 3:
                    act.wait_ge(q_copied, o + 1)
                    if t:
                        act.wait_ge(q_scaled, t)
                    A(qjunk[R, :, :], Q[R, t, :, :], ACT.Square).then_inc(q_sq, 1)
            for t in range(NT):
                for n in range(2):
                    act.wait_ge(qr_tr, 2 * t + n + 1)
                    b = mla_bank(None, "qT", 4 * t + 2 + n)
                    if t < 2:
                        out = qrP[0:64, 4 * n:4 * n + 4, tok(t)]
                        A(out, b[0:64, :].rearrange("p (h q) -> p h q", h=4), ACT.Copy).then_inc(qrT_done, 1)
                    else:
                        for hh in range(4):
                            i = A(qrS[0:64, :, 4 * n + hh, :],
                                  b[0:64, hh * P:hh * P + NSMP].rearrange("p (b q) -> p b q", b=8), ACT.Copy)
                        i.then_inc(qrT_done, 1)
            for h in range(N_HEADS):
                act.wait_ge(qa_mm, 2 * h + 1)
                b = mla_bank(None, "qa", 2 * h)
                A(qaP[:, 0, h, :], b[:, 0:SEQ], ACT.Copy)
                A(qaS[:, :, 0, h * 8:h * 8 + 8], b[:, SEQ:NTOK].rearrange("p (b q) -> p b q", b=8), ACT.Copy)\
                    .then_inc(qa_act, 1)
            for n in range(4):
                act.wait_ge(rb_mm, n + 1)
                A(Rb[:, 2 * n:2 * n + 2, :], mla_bank(None, "rb", n).rearrange("p (h q) -> p h q", h=2), ACT.Copy)\
                    .then_inc(rb_done, 1)
            act.wait_ge(rb_mm, 5)
            A(RsN[0:64, :], mla_bank(None, "rb", 4)[0:64, 0:NSMP], ACT.Copy).then_inc(rb_done, 1)

            for it in range(16 + 2):
                if it < 16:
                    par, nk = it % 2, (it % 2 + 1) * P
                    act.wait_ge(ps_max, it + 1)
                    A(sP[:, par, 0:nk], sP[:, par, 0:nk], ACT.Exp, bias=st[:, PNM + par:PNM + par + 1],
                      scale=ATTN_SCALE, accum_out=st[:, PSUM_ + par:PSUM_ + par + 1]).then_inc(ps_exp, 1)
                if 1 <= it <= 16:
                    n, par, nkt = it - 1, (it - 1) % 2, (it - 1) % 2 + 1
                    act.wait_ge(pp_tr, n + 1)
                    if n >= 2:
                        act.wait_ge(po_mm, n - 1)
                    A(PTp[:, par, 0:nkt, :], bank[2 + par][:, 0:nkt * P].rearrange("p (k q) -> p k q", k=nkt),
                      ACT.Copy).then_inc(pp_done, 1)
                if it >= 2:
                    n = it - 2
                    h, qt = n // 2, n % 2
                    act.wait_ge(po_mm, n + 1)
                    A(OLTp[:, :, h, qt * P:(qt + 1) * P], bank[4 + qt][:, 0:2 * P].rearrange("p (r q) -> p r q", r=2),
                      ACT.Copy).then_inc(po_done, 1)
            for h in range(N_HEADS):
                act.wait_ge(oTp_mm, h + 1)
                A(oT[:, h, 0:SEQ], bank[h % 8][:, 0:SEQ], ACT.Copy).then_inc(oTp_done, 1)

            act.wait_ge(rb_done, 5)
            A(Rs[0:64, PAST_LEN:NKEYS], RsN[0:64, :], ACT.Copy).then_inc(achain, 1)

            def evacuate_page(b, p):
                act.wait_ge(pg_tr, 8 * b + p + 1)
                k = bank[4 + p % 2]
                A(cT[:, :, p * P:(p + 1) * P], k[:, 0:2 * P].rearrange("p (r q) -> p r q", r=2), ACT.Copy)
                A(krT[0:64, p * P:(p + 1) * P], k[0:64, 2 * P:3 * P], ACT.Copy).then_inc(pg_ev, 1)

            def evacuate_probs(b):
                act.wait_ge(st_tr, b + 1)
                A(PT[:, 0:8, :], bank[6].rearrange("p (k q) -> p k q", k=8), ACT.Copy)
                A(PT[0:64, 8, :], bank[7][0:64, 0:64], ACT.Copy).then_inc(st_done, 1)

            def seq_act(b, par, kth, first):
                evacuate_page(b, 0)
                for p in range(N_PAGES):
                    if p < N_PAGES - 1:
                        evacuate_page(b, p + 1)
                    act.wait_ge(kk_mm, 8 * b + p + 1)
                    if not (first and p == 0):
                        act.wait_ge(kk_red, 8 * b + p)
                    for hf in range(2):
                        i = A(sjunk[:, 4 * hf:4 * hf + 4, :],
                              bank[2 * (p % 2) + hf].rearrange("p (h d) -> p h d", h=4), ACT.Square)
                    i.then_inc(kk_sq, 1)
                    if p == 3 and not first:
                        evacuate_probs(b - 1)
                for n in range(3):
                    act.wait_ge(sb_mm, 3 * b + n + 1)
                    src = bank[n][0:64, :] if n < 2 else bank[2][0:64, 64:128]
                    A(S[0:64, n * 512:n * 512 + src.shape[1]], src, ACT.Copy).then_inc(sb_ev, 1)
                for n in range(2):
                    act.wait_ge(rr_tr, 2 * b + n + 1)
                    A(Rs[0:64, n * 512:(n + 1) * 512], bank[4 + n][0:64, :], ACT.Copy).then_inc(rr_ev, 1)
                act.wait_ge(ss_done, b + 1)
                A(S[0:64, :], S[0:64, :], ACT.Exp, bias=st[0:64, SNM:SNM + 1], scale=ATTN_SCALE,
                  accum_out=st[0:64, SSUM:SSUM + 1]).then_inc(se_exp, 1)

            over_sequences(act, seq_act)
            evacuate_probs(DEC_BATCH - 1)
            for h in range(N_HEADS):
                act.wait_ge(oTs_mm, h + 1)
                A(oT[:, h, SEQ:NTOK], bank[h % 4][:, 0:NSMP], ACT.Copy).then_inc(oTs_done, 1)

            act.wait_ge(wo_mm, 1)
            act.dma_start(wr[:, :, :], w_router).then_inc(s_wr, 16)
            norm_squares(3)
            for t in range(NT):
                R = slice(0, ROWS[t])
                act.wait_ge(nxs[3], t + 1)
                A(XSp[0][R, t, :], XS[R, t, :], ACT.Copy).then_inc(xs_hi, 1)
            act.wait_ge(w_used, len(items))
            act.wait_ge(s_out, 64)

            def high(e, q):
                if q >= NU:
                    e, q = e + 1, q - NU
                act.wait_ge(raw_ready[raw_slot[q]], raw_count(e, q))
                wait_last(act, unit_used, e, hi_last[q])
                A(high_part[hi_slot[q]], raw[raw_slot[q]], ACT.Copy).then_inc(u_hi, 1)

            def prologue(e):
                for q in range(5):
                    high(e, q)

            def gathered(e, hf):
                act.wait_ge(ga_done, 2 * e + hf + 1)
                if hf == 0 and not (isinstance(e, int) and e == 0):
                    wait_last(act, unit_used, e, pos_gu(FF_BL - 1, 1) - NU)
                A(xgT[0][:, 4 * hf:4 * hf + 4, :], xg[:, 4 * hf:4 * hf + 4, :], ACT.Copy).then_inc(xg_hi, 1)

            def evacuate_hT(e, j):
                n = 11 * e + j
                act.wait_ge(e_tr, n + 1)
                wait_last(act, unit_used, e, pos_dn(j - 2) if j >= 2 else j - 1 - 1)
                A(hmT[0][:, j % 2, :, :], bank[4 + j % 2][:, 0:2 * P].rearrange("p (k s) -> p k s", k=2),
                  ACT.Copy).then_inc(e_trd, 1)

            def pass_act(e, prev, nxt):
                for j in range(FF_BL):
                    early, late = split_in(j, nxt)
                    if j:
                        evacuate_hT(e, j - 1)
                    for q in early:
                        high(e, q)
                    wait_last(act, unit_used, e, pos_gu(j, 1))
                    wait_pair(act, e_h, e, j)
                    A(gsil[:, j % 2, :], bank[2 + j % 2][:, 0:256], ACT.Silu).then_inc(e_silu, 1)
                    if j == FF_BL - 1 and nxt:
                        gathered(e + 1, 0)
                        gathered(e + 1, 1)
                    for q in late:
                        high(e, q)
                evacuate_hT(e, FF_BL - 1)
                if nxt:
                    for q in LAST_SPLIT:
                        high(e, q)
                wait_last(act, unit_used, e, NU - 1)
                act.wait_ge(selT_done, e + 1)
                if not (isinstance(e, int) and e == 0):
                    act.wait_ge(sc_mm, 6 * e)
                for hf in range(2):
                    A(yg[:, hf * 512:(hf + 1) * 512], bank[hf][:, :], ACT.Copy, scale=gslot[:, 0:1]).then_inc(y_done, 1)
                for hf in range(2):
                    act.wait_ge(y_done, 2 * e + hf + 1)
                    A(ygp[0][:, hf * 512:(hf + 1) * 512], yg[:, hf * 512:(hf + 1) * 512], ACT.Copy).then_inc(y_hi, 1)

            prologue(0)
            act.wait_ge(lg_max, 1)
            A(gt[:, 1, :], gt[:, 1, :], ACT.Exp).then_inc(lg_exp, 1)
            gathered(0, 0)
            gathered(0, 1)
            over_passes(act, pass_act)

            def act_further(i):
                e = i + N_EXPERTS
                prologue(e)
                gathered(e, 0)
                gathered(e, 1)
                pass_act(e, False, False)

            further(act, act_further)

        @block.vector
        def _(dve):
            V_ = nc.vector
            TT, TS, STT, RED, CP = V_.tensor_tensor, V_.tensor_scalar, V_.scalar_tensor_tensor, V_.tensor_reduce, V_.tensor_copy
            count = [0]

            def link(ins):
                count[0] = count[0] + 1
                ins.then_inc(chain, 1)
                dve.wait_ge(chain, count[0])

            def rstd(out, mean, scale=1.0):
                n = out.shape[-1]
                R = slice(0, out.shape[0])
                m, t = rs_m[R, 0:n], rs_t[R, 0:n]
                link(TS(m, mean, scale, EPS, MUL, ADD))
                link(TS(out.bitcast(i32), m.bitcast(i32), -0.5, float(0x5F3759DF), MUL, ADD))
                for _ in range(3):
                    link(TT(t, out, out, MUL))
                    link(STT(t, t, -0.5, m, MUL, MUL))
                    link(STT(out, t, 1.5, out, ADD, MUL))

            def gain(col, n, w):
                return G[:, col:col + n].unsqueeze(2).to_broadcast([P, n, w])

            def norm(s, outs):
                for t in range(NT):
                    R = slice(0, ROWS[t])
                    dve.wait_ge(nsq[s], t + 1)
                    rstd(st[R, RSTD + t:RSTD + t + 1], st[R, SS + t:SS + t + 1])
                    TS(XS[R, t, :], X[R, t, :], st[R, RSTD + t:RSTD + t + 1], None, MUL).then_inc(nxs[s], 1)
                for t in range(NT):
                    for hf in range(2):
                        dve.wait_ge(ntr[s], 2 * t + hf + 1)
                        src = bank[2 * t + hf].rearrange("p (k q) -> p k q", k=4)[:, :, 0:ROWS[t]]
                        for out, col in outs:
                            i = TT(out[:, 4 * hf:4 * hf + 4, tok(t)], src, gain(col + 4 * hf, 4, ROWS[t]), MUL)
                        i.then_inc(nht[s], 1)

            def add_residual(done, ready):
                for t in range(NT):
                    for hf in range(2):
                        x = X[0:ROWS[t], t, hf * 512:(hf + 1) * 512]
                        dve.wait_ge(done, 2 * t + hf + 1)
                        i = TT(x, bank[2 * t + hf][0:ROWS[t], :], x, ADD)
                    i.then_inc(ready, 1)

            V_.memset(st[:, :], 0.0)
            V_.memset(sks[:, :, :], 0.0).then_inc(s_zero, 1)
            dve.wait_ge(s_const, 32)
            dve.wait_ge(s_zero, 1)
            dve.wait_ge(s_x, 48)
            norm(0, [(hT, G_A)])
            dve.wait_ge(s_gm, 16 * 5)
            TT(ws[:, :, :], ws[:, :, :], triu.unsqueeze(1).to_broadcast([P, N_GROUPS, P]), MUL).then_inc(ws_done, 1)
            for t in range(2):
                CP(bs_bc[:, :, tok(t)], bs_raw)
            CP(bs_bc[:, :, tok(2)].rearrange("p g (b i) -> p g b i", b=8),
               bs_raw[:, :, 0:8].unsqueeze(2).to_broadcast([P, N_GROUPS, 8, 8]))
            for t in range(NT):
                R = slice(0, ROWS[t])
                i = TT(X[R, t, :], X[R, t, :], bout_bc[R, :], ADD)
            link(i)
            dve.wait_ge(rep_mm, 1)
            link(CP(wrep[0:64, :, :], bank[7][0:64, 0:64].rearrange("p (g i) -> p g i", g=8)))
            for g in range(N_GROUPS):
                i = TT(ws_new[0:64, g, :, :], wrep[0:64, g, :].unsqueeze(1).to_broadcast([64, 8, 8]),
                       K[0:64, C_BLK:C_BLK + 64].rearrange("p (b i) -> p b i", b=8), MUL)
            i.then_inc(ws_done, 1)
            for o in range(12):
                n, t = o // NT, o % NT
                R, c = slice(0, ROWS[t]), slice(n * 512, (n + 1) * 512)
                dve.wait_ge(v_mm, o + 1)
                TT(V[R, t, c], bank[o % 8][R, :], bv_bc[R, c], ADD).then_inc(v_biased, 1)
            for t in range(NT):
                R = slice(0, ROWS[t])
                dve.wait_ge(v_sq, t + 1)
                rstd(st[R, RSV + t:RSV + t + 1], st[R, SSV + t:SSV + t + 1])
                STT(V[R, t, :], V[R, t, :], st[R, RSV + t:RSV + t + 1], sgu_bc[R, :], MUL, MUL).then_inc(v_norm, 1)
            for c in range(16):
                dve.wait_ge(mix_mm, c + 1)
                dve.wait_ge(u_done, c + 1)
                link(TT(gtmp[:, c % 2, :], bank[(28 + c) % 8][:, 0:NTOK], bs_bc[:, c // 2, :], ADD))
                TT(uT[:, c, :], uT[:, c, :], gtmp[:, c % 2, :], MUL).then_inc(gu_done, 1)
            add_residual(gout_mm, x_ready[1])

            norm(1, [(hT, G_F0)])
            dve.wait_ge(v_out, 16)
            for f in range(FF_CH):
                dve.wait_ge(silu_done, f + 1)
                dve.wait_ge(up_mm, f + 1)
                TT(ffT[:, f, :], sg[:, f % 2, :], bank[2 * (f % 4) + 1][:, 0:NTOK], MUL).then_inc(ff_done, 1)
            add_residual(dout_mm, x_ready[2])

            norm(2, [(hT, G_KV), (hbT, G_B)])
            dve.wait_ge(s_rows, 48)
            link(V_.memset(krtmp[:, :, :], 0.0))
            for t in range(NT):
                R = slice(0, ROWS[t])
                b = mla_bank(None, "ckr", t)
                dve.wait_ge(ckr_sq, t + 1)
                rstd(st[R, RCK + 2 * t:RCK + 2 * t + 2], st[R, SCK + 2 * t:SCK + 2 * t + 2])
                STT(krtmp[R, t, :], b[R, 256:320], st[R, RCK + 2 * t + 1:RCK + 2 * t + 2], brow[R, 256:320], MUL, MUL)
                STT(Cn[R, t, :], b[R, 0:256], st[R, RCK + 2 * t:RCK + 2 * t + 1], brow[R, 0:256], MUL, MUL)\
                    .then_inc(c_new, 1)
            dve.wait_ge(c_new, 3)

            def rotate(out, src, cos, sin, a, b):
                x1, x2 = src[:, :, 0:32], src[:, :, 32:64]
                TT(a, x1, cos, MUL)
                link(TT(b, x2, sin, MUL))
                link(TT(out[:, :, 0:32], a, b, SUB))
                TT(a, x1, sin, MUL)
                link(TT(b, x2, cos, MUL))
                return TT(out[:, :, 32:64], a, b, ADD)

            cos3 = K[:, C_COS:C_COS + 96].rearrange("p (t c) -> p t c", t=3)
            sin3 = K[:, C_SIN:C_SIN + 96].rearrange("p (t c) -> p t c", t=3)
            rotate(KRn, krtmp, cos3, sin3, krope1, krope2).then_inc(kr_new, 1)
            for t in range(NT):
                R = slice(0, ROWS[t])
                dve.wait_ge(dq_sq, t + 1)
                rstd(st[R, RQL + t:RQL + t + 1], st[R, SQL + t:SQL + t + 1])
                TS(cqs[R, t, :], mla_bank(None, "dq", t)[R, 0:384], st[R, RQL + t:RQL + t + 1], None, MUL)\
                    .then_inc(cq_scaled, 1)
            for t in range(NT):
                dve.wait_ge(cq_tr, t + 1)
                TT(cqT[:, :, tok(t)], mla_bank(None, "cqT", t)[:, 0:384].rearrange("p (k q) -> p k q", k=3)[:, :, 0:ROWS[t]],
                   gain(G_QL, 3, ROWS[t]), MUL).then_inc(cqT_done, 1)
            skn = st[:, SKN:SKN + 24].rearrange("p (t h) -> p t h", t=3)
            for t in range(NT):
                R = slice(0, ROWS[t])
                dve.wait_ge(kn_sq, 2 * t + 2)
                RED(skn[R, t, :], kjunk[R, :, :], AX, ADD).then_inc(kn_red, 1)
            dve.wait_ge(kn_red, 3)
            rstd(st[:, SKN:SKN + 24], st[:, SKN:SKN + 24], 1.0 / D_NOPE)
            sqn = st[:, SQN:SQN + 24].rearrange("p (t h) -> p t h", t=3)
            sqr = st[:, SQR:SQR + 24].rearrange("p (t h) -> p t h", t=3)
            for t in range(NT):
                R, n = slice(0, ROWS[t]), ROWS[t]
                dve.wait_ge(q_sq, t + 1)
                RED(sqn[R, t, :], qjunk[R, :, 0:D_NOPE], AX, ADD)
                link(RED(sqr[R, t, :], qjunk[R, :, D_NOPE:192], AX, ADD))
                rstd(sqn[R, t, :], sqn[R, t, :], 1.0 / D_NOPE)
                rstd(sqr[R, t, :], sqr[R, t, :], 1.0 / D_ROPE)
                qn, qr = Q[R, t, :, 0:D_NOPE], Q[R, t, :, D_NOPE:192]
                TT(qn, qn, sqn[R, t, :].unsqueeze(2).to_broadcast([n, 8, D_NOPE]), MUL)
                link(TT(qr, qr, sqr[R, t, :].unsqueeze(2).to_broadcast([n, 8, D_ROPE]), MUL))
                link(TT(qr, qr, brow[R, 320:384].unsqueeze(1).to_broadcast([n, 8, D_ROPE]), MUL))
                rotate(QR[R, t, :, :], qr, cos3[R, t, :].unsqueeze(1).to_broadcast([n, 8, 32]),
                       sin3[R, t, :].unsqueeze(1).to_broadcast([n, 8, 32]), rope1[R, :, :], rope2[R, :, :])\
                    .then_inc(q_scaled, 1)
            for t in range(NT):
                for n in range(2):
                    dve.wait_ge(qn_tr, 2 * t + n + 1)
                    TS(qnT[:, 4 * n:4 * n + 4, tok(t)],
                       mla_bank(None, "qT", 4 * t + n).rearrange("p (h q) -> p h q", h=4)[:, :, 0:ROWS[t]],
                       G[:, G_QN:G_QN + 1], G[:, G_KN:G_KN + 1], MUL, MUL).then_inc(qnT_done, 1)
            for h in range(N_HEADS):
                dve.wait_ge(qa_mm, 2 * h + 2)
                b = mla_bank(None, "qa", 2 * h + 1)
                CP(qaP[:, 1, h, :], b[:, 0:SEQ])
                CP(qaS[:, :, 1, h * 8:h * 8 + 8], b[:, SEQ:NTOK].rearrange("p (b q) -> p b q", b=8)).then_inc(qa_dve, 1)

            CP(rnb[0:64, :].rearrange("p (h q) -> p h q", h=8), st[0:64, SKN + 16:SKN + 24].unsqueeze(2).to_broadcast([64, 8, 8]))\
                .then_inc(rnb_done, 1)

            dve.wait_ge(rb_done, 4)
            for it in range(16 + 1):
                if it < 16:
                    h, qt, par = it // 2, it % 2, it % 2
                    nk = (qt + 1) * P
                    s, b = sP[:, par, 0:nk], bank[par]
                    dve.wait_ge(ps_mm, it + 1)
                    if it >= 2:
                        dve.wait_ge(pp_tr, it - 1)
                    link(TT(s, b[:, 0:nk], Rb[:, h, 0:nk], MUL))
                    link(TT(s, b[:, 256:256 + nk], s, ADD))
                    link(TT(sP[:, par, nk - P:nk], sP[:, par, nk - P:nk], causal, ADD))
                    link(RED(st[:, PMX + par:PMX + par + 1], s, AX, ALU.max))
                    TS(st[:, PNM + par:PNM + par + 1], st[:, PMX + par:PMX + par + 1], -ATTN_SCALE, None, MUL)\
                        .then_inc(ps_max, 1)
                if it >= 1:
                    n = it - 1
                    par, nk = n % 2, (n % 2 + 1) * P
                    dve.wait_ge(ps_exp, n + 1)
                    link(V_.reciprocal(st[:, PRC + par:PRC + par + 1], st[:, PSUM_ + par:PSUM_ + par + 1]))
                    TS(sP[:, par, 0:nk], sP[:, par, 0:nk], st[:, PRC + par:PRC + par + 1], None, MUL).then_inc(ps_prob, 1)

            def pick_query(b):
                CP(qab, qaS[:, bass.ds(b, 1), :, :].rearrange("p a r q -> p (a r) q"))
                CP(qrb[0:64], qrS[0:64, bass.ds(b, 1), :, :].rearrange("p a h q -> p (a h q)")).then_inc(q_picked, 1)

            def take_out(b):
                dve.wait_ge(so_mm, b + 1)
                CP(OLTs[:, bass.ds(b, 1), :, :, :].rearrange("p a r h q -> p (a r h q)"), bank[7][:, 128:256])\
                    .then_inc(so_done, 1)

            SEQ_LINKS = 15
            seq_base = count[0]

            def seq_dve(b, par, kth, first):
                count[0] = seq_base + SEQ_LINKS * b
                if first:
                    dve.wait_ge(ps_mm, 16)
                else:
                    dve.wait_ge(sb_mm, 3 * b)
                pick_query(b)
                for p in range(N_PAGES):
                    dve.wait_ge(kk_sq, 8 * b + p + 1)
                    if p == 0 and not first:
                        dve.wait_ge(rr_tr, 2 * b)
                    RED(sks[:, p, :], sjunk, AX, ADD).then_inc(kk_red, 1)
                    if p == 3 and not first:
                        take_out(b - 1)
                dve.wait_ge(kk_red, 8 * b + 8)
                k = sks[:, :, :].rearrange("p a h -> p (a h)")
                rstd(k, k, 1.0 / D_NOPE)
                CP(sksb[:, :, :].rearrange("p a (h q) -> p (a h) q", h=8), k.unsqueeze(2).to_broadcast([P, 64, 8]))\
                    .then_inc(kk_rstd, 1)
                for n in range(2):
                    dve.wait_ge(sa_mm, 2 * b + n + 1)
                    dve.wait_ge(rr_ev, 2 * b + n + 1)
                    c = slice(n * 512, (n + 1) * 512)
                    TT(stmp[0:64, c], bank[6 + n][0:64, :], Rs[0:64, c], MUL).then_inc(ss_a, 1)
                new = slice(PAST_LEN, NKEYS)
                dve.wait_ge(sb_mm, 3 * b + 3)
                TT(stmp[0:64, new], bank[2][0:64, 0:64], Rs[0:64, new], MUL).then_inc(ss_a, 1)
                dve.wait_ge(ss_a, 3 * b + 3)
                link(TT(stmp[0:64, new], stmp[0:64, new],
                        K[0:64, C_NEWM:C_NEWM + 512].rearrange("p (b k) -> p b k", b=8)[:, bass.ds(b, 1), :]
                        .rearrange("p a k -> p (a k)"), ADD))
                dve.wait_ge(sb_ev, 3 * b + 3)
                link(TT(S[0:64, :], stmp[0:64, :], S[0:64, :], ADD))
                link(RED(st[0:64, SMX:SMX + 1], S[0:64, :], AX, ALU.max))
                TS(st[0:64, SNM:SNM + 1], st[0:64, SMX:SMX + 1], -ATTN_SCALE, None, MUL).then_inc(ss_done, 1)
                dve.wait_ge(se_exp, b + 1)
                link(V_.reciprocal(st[0:64, SRC:SRC + 1], st[0:64, SSUM:SSUM + 1]))
                TS(S[0:64, :], S[0:64, :], st[0:64, SRC:SRC + 1], None, MUL).then_inc(se_prob, 1)
                assert not first or count[0] == seq_base + SEQ_LINKS

            over_sequences(dve, seq_dve)
            count[0] = seq_base + SEQ_LINKS * DEC_BATCH
            take_out(DEC_BATCH - 1)
            add_residual(wo_mm, x_ready[3])

            norm(3, [(hT, G_F1)])
            LG, EX, PR, EQ, O1, P2, O2, GA, MK, PO, T0, T1, CUM = 0, 1, 2, 3, 4, 5, 6, 7, 8, 9, 10, 11, 12
            NE, F, FA, FB = 14, 15, 16, 17

            def g(i, w=24):
                return gt[:, i, 0:w]

            def g3(i):
                return gt[:, i, :].rearrange("p (t e) -> p t e", t=3)

            def c3(i):
                return gt[:, 13, 3 * i:3 * i + 3]

            def b3(i):
                return c3(i).unsqueeze(2).to_broadcast([P, 3, 8])

            pri3 = K[:, C_PRI:C_PRI + 8].unsqueeze(1).to_broadcast([P, 3, 8])
            link(V_.memset(gt[:, :, :], 0.0))
            dve.wait_ge(lg_mm, 1)
            V_.memset(ones, 1.0)
            for t in range(NT):
                i = CP(gt[0:ROWS[t], LG, 8 * t:8 * t + 8], bank[0][0:ROWS[t], 8 * t:8 * t + 8])
            link(i)
            link(RED(c3(0), g3(LG), AX, ALU.max))
            TT(g3(EX), g3(LG), b3(0), SUB).then_inc(lg_max, 1)
            dve.wait_ge(lg_exp, 1)
            link(RED(c3(1), g3(EX), AX, ADD))
            link(V_.reciprocal(c3(1), c3(1)))
            link(TT(g3(PR), g3(EX), b3(1), MUL))

            def top(src, c, onehot):
                link(RED(c3(c), g3(src), AX, ALU.max))
                link(TT(g3(EQ), g3(src), b3(c), ALU.is_equal))
                link(TT(g3(EQ), g3(EQ), pri3, MUL))
                link(RED(c3(c + 1), g3(EQ), AX, ALU.max))
                link(TT(g3(onehot), g3(EQ), b3(c + 1), ALU.is_equal))

            top(PR, 2, O1)
            link(STT(g(P2), g(O1), -2.0, g(PR), MUL, ADD))
            top(P2, 4, O2)
            link(TT(c3(6), c3(2), c3(4), ADD))
            link(V_.reciprocal(c3(6), c3(6)))
            link(TT(g3(T0), g3(O1), b3(2), MUL))
            link(TT(g3(T1), g3(O2), b3(4), MUL))
            link(TT(g(T0), g(T0), g(T1), ADD))
            link(TT(g3(GA), g3(T0), b3(6), MUL))
            link(TT(g(MK), g(O1), g(O2), ADD))
            TT(g3(MK), g3(MK), K[:, C_VALID:C_VALID + 3].unsqueeze(2).to_broadcast([P, 3, 8]), MUL).then_inc(mask_done, 1)
            dve.wait_ge(cum_mm, 1)
            CP(g(NE, 8), bank[1][:, 24:32])
            link(TT(g(T0), bank[1][:, 0:24], g(MK), MUL))
            link(TS(g(PO), g(T0), -1.0, None, ADD))
            CP(item_pos[:, 0:8, :], g3(PO).rearrange("p t e -> p e t"))
            CP(item_gate[:, 0:8, :], g3(GA).rearrange("p t e -> p e t"))
            for k in range(2):
                i = TS(gt[:, F, 8 * k:8 * k + 8], g(NE, 8), float(CAP * (k + 1)), None, ALU.is_gt)
            link(i)
            link(CP(g(FA, 16), g(F, 16)))
            a, b = FA, FB
            for sh in (1, 2, 4, 8):
                CP(gt[:, b, 0:sh], gt[:, a, 0:sh])
                link(TT(gt[:, b, sh:16], gt[:, a, sh:16], gt[:, a, 0:16 - sh], ADD))
                a, b = b, a
            link(CP(gt[:, 18, 0:1], gt[:, a, 15:16]))
            link(TT(g(T1, 16), g(a, 16), g(F, 16), SUB))
            for k in range(2):
                xp3 = xtab[:, 0, :].rearrange("p (t k e) -> p t k e", t=3, k=2)
                xg3 = xtab[:, 1, :].rearrange("p (t k e) -> p t k e", t=3, k=2)
                TS(xp3[:, :, k, :], g3(PO), -float(CAP * (k + 1)), None, ADD)
                i = CP(xg3[:, :, k, :], g3(GA))
            link(i)
            for o in range(MAX_EXTRA):
                link(TS(g(T0, 16), g(T1, 16), float(o), None, ALU.is_equal))
                link(TT(g(T0, 16), g(T0, 16), g(F, 16), MUL))
                pick = gt[:, T0, 0:16].unsqueeze(1).to_broadcast([P, 3, 16])
                for x, dst in ((0, item_pos), (1, item_gate)):
                    y = xtab[:, 2 + x, :].rearrange("p (t k) -> p t k", t=3)
                    link(TT(y, xtab[:, x, :].rearrange("p (t k) -> p t k", t=3), pick, MUL))
                    link(RED(dst[:, 8 + o, :], y, AX, ADD))
                link(TT(xtab[:, 4, 0:16], gt[:, T0, 0:16], K[:, C_EIDX:C_EIDX + 16], MUL))
                link(RED(gt[:, 18, o + 1:o + 2], xtab[:, 4, 0:16], AX, ADD))
            CP(cnt_i[0:1, :], gt[0:1, 18, 0:1 + MAX_EXTRA]).then_inc(table_done, 1)

            def select(e, first=False):
                if not first:
                    dve.wait_ge(selT_mm, e)
                CP(gatec, item_gate[:, bass.ds(e, 1), :].rearrange("p a t -> p (a t)"))
                link(CP(posc, item_pos[:, bass.ds(e, 1), :].rearrange("p a t -> p (a t)")))
                for t in range(NT):
                    R = slice(0, ROWS[t])
                    i = TS(Sel[R, t, :], iota[R, :], posc[R, t:t + 1], None, ALU.is_equal)
                i.then_inc(sel_done, 1)

            def low(e, q):
                if q >= NU:
                    e, q = e + 1, q - NU
                dve.wait_ge(u_hi, NU * e + q + 1)
                TT(low_part[raw_slot[q]], raw[raw_slot[q]], high_part[hi_slot[q]].bitcast(f32), SUB).then_inc(u_lo, 1)

            def gather_out(e, hf):
                dve.wait_ge(ga_mm, 2 * e + hf + 1)
                if not (isinstance(e, int) and e == 0):
                    dve.wait_ge(xg_lo, 2 * e)
                TT(xg[:, 4 * hf:4 * hf + 4, :], bank[6 + hf].rearrange("p (k q) -> p k q", k=4),
                   gain(G_F1 + 4 * hf, 4, P), MUL).then_inc(ga_done, 1)

            def gather_low(e, hf):
                h = slice(4 * hf, 4 * hf + 4)
                dve.wait_ge(xg_hi, 2 * e + hf + 1)
                TT(xgT[1][:, h, :], xg[:, h, :], xgT[0][:, h, :].bitcast(f32), SUB).then_inc(xg_lo, 1)

            def h_low(e, j):
                dve.wait_ge(e_trd, 11 * e + j + 1)
                TT(hmT[1][:, j % 2, :, :], bank[4 + j % 2][:, 0:2 * P].rearrange("p (k s) -> p k s", k=2),
                   hmT[0][:, j % 2, :, :].bitcast(f32), SUB).then_inc(e_low, 1)

            def y_low(e):
                for hf in range(2):
                    c = slice(hf * 512, (hf + 1) * 512)
                    dve.wait_ge(y_hi, 2 * e + hf + 1)
                    TT(ygp[1][:, c], yg[:, c], ygp[0][:, c].bitcast(f32), SUB).then_inc(y_lo, 1)

            def scatter_out(e, steps=range(6)):
                for n in steps:
                    t, hf = n // 2, n % 2
                    x = X[0:ROWS[t], t, hf * 512:(hf + 1) * 512]
                    dve.wait_ge(sc_mm, 6 * e + n + 1)
                    TT(x, bank[6 + hf][0:ROWS[t], :], x, ADD).then_inc(sc_done, 1)

            def pass_dve(e, prev, nxt):
                for j in range(FF_BL):
                    early, late = split_in(j, nxt)
                    if j:
                        h_low(e, j - 1)
                    for q in early:
                        low(e, q)
                    dve.wait_ge(e_silu, 11 * e + j + 1)
                    wait_pair(dve, e_tr, e, j)
                    TT(hmul[:, j % 2, :], gsil[:, j % 2, :], bank[2 + j % 2][:, 256:512], MUL).then_inc(e_h, 1)
                    if j == FF_BL - 1 and nxt:
                        gather_low(e + 1, 0)
                        gather_low(e + 1, 1)
                    for q in late:
                        low(e, q)
                    if j == 2 and prev:
                        y_low(e - 1)
                    if j in SCATTER_AT and prev:
                        scatter_out(e - 1, SCATTER_AT[j])
                    if j == SELECT_AT:
                        dve.wait_ge(selT_mm, e + 1)
                        if not (isinstance(e, int) and e == 0):
                            dve.wait_ge(y_done, 2 * e)
                        CP(SelT, bank[6][:, 0:NTOK])
                        CP(gslot, bank[7][:, 0:1]).then_inc(selT_done, 1)
                        if nxt:
                            count[0] = pass_base + e
                            select(e + 1)
                    if j in GATHER_AT and nxt:
                        gather_out(e + 1, GATHER_AT[j])
                h_low(e, FF_BL - 1)
                if nxt:
                    for q in LAST_SPLIT:
                        low(e, q)

            for t in range(NT):
                R = slice(0, ROWS[t])
                dve.wait_ge(xs_hi, t + 1)
                dve.wait_ge(ntr[3], 6)
                TT(XSp[1][R, t, :], XS[R, t, :], XSp[0][R, t, :].bitcast(f32), SUB).then_inc(xs_lo, 1)
            dve.wait_ge(table_done, 1)
            select(0, True)
            for q in range(5):
                low(0, q)
            for step in (gather_out, gather_low):
                for hf in range(2):
                    step(0, hf)
            pass_base = count[0]
            over_passes(dve, pass_dve)
            count[0] = pass_base + N_EXPERTS - 1
            y_low(N_EXPERTS - 1)
            scatter_out(N_EXPERTS - 1)
            far_base = count[0]

            def dve_further(i):
                count[0] = far_base + i
                for q in range(5):
                    low(i + N_EXPERTS, q)
                select(i + N_EXPERTS)
                for step in (gather_out, gather_low):
                    for hf in range(2):
                        step(i + N_EXPERTS, hf)
                pass_dve(i + N_EXPERTS, False, False)
                y_low(i + N_EXPERTS)
                scatter_out(i + N_EXPERTS)

            further(dve, dve_further)
            dve.drain().then_inc(x_ready[4], 1)

        @block.tensor
        def _(pe):
            T = nc.tensor.transpose

            def norm(s):
                for t in range(NT):
                    pe.wait_ge(nxs[s], t + 1)
                    n = ROWS[t]
                    for hf in range(2):
                        for k in range(4):
                            i = T(bank[2 * t + hf][:, k * P:k * P + n],
                                  XS[0:n, t, (4 * hf + k) * P:(4 * hf + k + 1) * P], ident[0:n, 0:n])
                        i.then_inc(ntr[s], 1)
                pe.wait_ge(nht[s], 6)

            def residual_mm(n0, chunks, lhs, ready, done):
                for c in range(chunks):
                    if c % 4 == 0:
                        await_item(pe, n0 + c // 4)
                    for t in range(NT):
                        for hf in range(2):
                            i = mm(bank[2 * t + hf][0:ROWS[t], :], lhs(c, t),
                                   weights(n0 + c // 4)[:, c % 4, hf * 512:(hf + 1) * 512],
                                   start=(c == 0), stop=(c == chunks - 1))
                            if c == chunks - 1:
                                i.then_inc(done, 1)
                    if c % 4 == 3 or c == chunks - 1:
                        if c == chunks - 1:
                            pe.wait_ge(done, 6)
                            pe.sem_inc(w_used, 1)
                        else:
                            i.then_inc(w_used, 1)

            pe.wait_ge(s_const, 32)
            norm(0)
            pe.wait_ge(ws_done, 1)
            mm(bank[7][0:64, 0:64], K[0:8, C_REP:C_REP + 64], ws[0:8, :, 0:8], start=True, stop=True).then_inc(rep_mm, 1)
            for o in range(12):
                n, t = o // NT, o % NT
                if t == 0:
                    await_item(pe, n)
                if o == 7:
                    pe.wait_ge(ws_done, 2)
                if o >= 8:
                    pe.wait_ge(v_biased, o - 7)
                for k in range(KC):
                    i = mm(bank[o % 8][0:ROWS[t], :], hT[:, k, tok(t)], weights(n)[:, k, :], start=(k == 0), stop=(k == KC - 1))
                i.then_inc(v_mm, 1)
                if t == 2:
                    pe.wait_ge(v_mm, o + 1)
                    pe.sem_inc(w_used, 1)
            for c in range(16):
                n, o = 4 + c // 4, 12 + c
                if c % 4 == 0:
                    await_item(pe, n)
                if o < 20:
                    pe.wait_ge(v_biased, o - 7)
                else:
                    pe.wait_ge(u_done, o - 19)
                for k in range(KC):
                    i = mm(bank[o % 8][:, 0:NTOK], weights(n)[:, k, c % 4 * P:(c % 4 + 1) * P], hT[:, k, :],
                           start=(k == 0), stop=(k == KC - 1))
                i.then_inc(u_mm, 1)
                if c % 4 == 3:
                    pe.wait_ge(u_mm, c + 1)
                    pe.sem_inc(w_used, 1)
            pe.wait_ge(v_norm, 3)
            pe.wait_ge(ws_done, 2)
            for c in range(16):
                o = 28 + c
                if o < 36:
                    pe.wait_ge(u_done, o - 19)
                else:
                    pe.wait_ge(gu_done, o - 35)
                for t in range(2):
                    mm(bank[o % 8][:, tok(t)], V[:, t, c * P:(c + 1) * P], ws[:, c // 2, :], start=True, stop=True)
                mm(bank[o % 8][:, tok(2)], V[0:NSMP, 2, c * P:(c + 1) * P],
                   ws_new[0:NSMP, c // 2, :, :].rearrange("p b i -> p (b i)"), start=True, stop=True).then_inc(mix_mm, 1)
            pe.wait_ge(gu_done, 16)
            residual_mm(IT_OUT, 16, lambda c, t: uT[:, c, tok(t)], None, gout_mm)

            norm(1)
            for f in range(FF_CH):
                n, q = IT_GU + f // 2, f % 2
                if q == 0:
                    await_item(pe, n)
                if f >= 4:
                    pe.wait_ge(ff_done, f - 3)
                for h, done in ((0, g_mm), (1, up_mm)):
                    for k in range(KC):
                        i = mm(bank[2 * (f % 4) + h][:, 0:NTOK], weights(n)[:, k, h * 256 + q * P:h * 256 + (q + 1) * P],
                               hT[:, k, :], start=(k == 0), stop=(k == KC - 1))
                    i.then_inc(done, 1)
                if q == 1:
                    pe.wait_ge(up_mm, f + 1)
                    pe.sem_inc(w_used, 1)
            pe.wait_ge(ff_done, FF_CH)
            residual_mm(IT_DN, FF_CH, lambda c, t: ffT[:, c, tok(t)], None, dout_mm)

            norm(2)
            for name, it, w, src, done in (("ckr", IT_CK, 320, hT, ckr_mm), ("dq", IT_DQ, Q_RANK, hbT, dq_mm)):
                await_item(pe, it)
                for t in range(NT):
                    b = mla_bank(pe, name, t)
                    for k in range(KC):
                        i = mm(b[0:ROWS[t], 0:w], src[:, k, tok(t)], weights(it)[:, k, :], start=(k == 0), stop=(k == KC - 1))
                    i.then_inc(done, 1)
                pe.wait_ge(done, 3)
                pe.sem_inc(w_used, 1)
            for t in range(NT):
                b, n = mla_bank(pe, "cqT", t), ROWS[t]
                pe.wait_ge(cq_scaled, t + 1)
                for k in range(3):
                    i = T(b[:, k * P:k * P + n], cqs[0:n, t, k * P:(k + 1) * P], ident[0:n, 0:n])
                i.then_inc(cq_tr, 1)
            pe.wait_ge(c_new, 3)
            pe.wait_ge(kr_new, 1)
            for t in range(NT):
                b, n = mla_bank(pe, "ckT", t), ROWS[t]
                for r in range(2):
                    T(b[:, r * P:r * P + n], Cn[0:n, t, r * P:(r + 1) * P], ident[0:n, 0:n])
                T(b[0:64, 256:256 + n], KRn[0:n, t, :], ident[0:n, 0:n]).then_inc(ck_tr, 1)
            pe.wait_ge(s_mla, 48)
            for o in range(6):
                t, hf = o // 2, o % 2
                b = mla_bank(pe, "kn", o)
                pe.wait_ge(ckT_done, t + 1)
                for r in range(2):
                    i = mm(b[0:ROWS[t], :], cTn[:, r, tok(t)], wuk[:, r, hf * 512:(hf + 1) * 512], start=(r == 0), stop=(r == 1))
                i.then_inc(kn_mm, 1)
            pe.wait_ge(cqT_done, 3)
            await_item(pe, IT_UQ)
            await_item(pe, IT_UQ + 1)
            for o in range(12):
                t, n = o // 4, o % 4
                b = mla_bank(pe, "q", o)
                for k in range(3):
                    i = mm(b[0:ROWS[t], 0:384], cqT[:, k, tok(t)], weights(IT_UQ + n // 2)[:, k, n % 2 * 384:(n % 2 + 1) * 384],
                           start=(k == 0), stop=(k == 2))
                i.then_inc(q_mm, 1)
            pe.wait_ge(q_mm, 12)
            pe.sem_inc(w_used, 2)
            for t in range(NT):
                n = ROWS[t]
                pe.wait_ge(q_scaled, t + 1)
                for i4 in range(4):
                    b = mla_bank(pe, "qT", 4 * t + i4)
                    for hh in range(4):
                        if i4 < 2:
                            i = T(b[:, hh * P:hh * P + n], Q[0:n, t, 4 * i4 + hh, 0:D_NOPE], ident[0:n, 0:n])
                        else:
                            i = T(b[0:64, hh * P:hh * P + n], QR[0:n, t, 4 * (i4 - 2) + hh, :], ident[0:n, 0:n])
                    i.then_inc(qn_tr if i4 < 2 else qr_tr, 1)
            pe.wait_ge(qnT_done, 6)
            for o in range(16):
                h, r = o // 2, o % 2
                mm(mla_bank(pe, "qa", o)[:, 0:NTOK], wukT[:, h, r * P:(r + 1) * P], qnT[:, h, :], start=True, stop=True)\
                    .then_inc(qa_mm, 1)
            pe.wait_ge(rnb_done, 1)
            skn = st[:, SKN:SKN + 24].rearrange("p (t h) -> p t h", t=3)
            for n in range(4):
                b = mla_bank(pe, "rb", n)
                for h in range(2):
                    for t in range(2):
                        i = mm(b[:, (2 * h + t) * P:(2 * h + t + 1) * P],
                               skn[:, t, 2 * n + h:2 * n + h + 1].to_broadcast([P, P]), ident, start=True, stop=True)
                i.then_inc(rb_mm, 1)
            mm(mla_bank(pe, "rb", 4)[0:64, 0:64], rnb[0:64, :],
               ident[0:64, 0:64], start=True, stop=True).then_inc(rb_mm, 1)

            pe.wait_ge(rb_done, 5)
            pe.wait_ge(qa_dve, 8)
            pe.wait_ge(qrT_done, 6)
            for it in range(16 + 2):
                if it < 16:
                    h, qt = it // 2, it % 2
                    nk, b = (qt + 1) * P, bank[it % 2]
                    if it >= 2:
                        pe.wait_ge(ps_max, it - 1)
                    for r in range(2):
                        mm(b[:, 0:nk], qaP[:, r, h, tok(qt)], cTn[:, r, 0:nk], start=(r == 0), stop=(r == 1))
                    mm(b[:, 256:256 + nk], qrP[0:64, h, tok(qt)], krTn[0:64, 0:nk], start=True, stop=True).then_inc(ps_mm, 1)
                if 1 <= it <= 16:
                    n, nkt = it - 1, (it - 1) % 2 + 1
                    pe.wait_ge(ps_prob, n + 1)
                    if n >= 2:
                        pe.wait_ge(pp_done, n - 1)
                    for k in range(nkt):
                        i = T(bank[2 + n % 2][:, k * P:(k + 1) * P], sP[:, n % 2, k * P:(k + 1) * P], ident)
                    i.then_inc(pp_tr, 1)
                if it >= 2:
                    n, nkt = it - 2, it % 2 + 1
                    pe.wait_ge(pp_done, n + 1)
                    if n >= 2:
                        pe.wait_ge(po_done, n - 1)
                    for r in range(2):
                        for k in range(nkt):
                            i = mm(bank[4 + n % 2][:, r * P:(r + 1) * P], Cn[:, k, r * P:(r + 1) * P], PTp[:, n % 2, k, :],
                                   start=(k == 0), stop=(k == nkt - 1))
                    i.then_inc(po_mm, 1)
            pe.wait_ge(po_done, 16)
            for h in range(N_HEADS):
                for r in range(2):
                    i = mm(bank[h][:, 0:SEQ], wuv[:, r, h * P:(h + 1) * P], OLTp[:, r, h, :], start=(r == 0), stop=(r == 1))
                i.then_inc(oTp_mm, 1)

            pe.wait_ge(oTp_done, 8)

            def page_tr(b, par, p):
                if p < 2:
                    pe.wait_ge(rr_ev, 2 * b) if not isinstance(b, int) or b else None
                if not (isinstance(b, int) and b == 0 and p < 2):
                    pe.wait_ge(pg_ev, 8 * b + p - 1)
                k = bank[4 + p % 2]
                for r in range(2):
                    T(k[:, r * P:(r + 1) * P], Cpg[par][:, p, r * P:(r + 1) * P], ident)
                T(k[0:64, 2 * P:3 * P], KRpg[par][:, p, :], ident).then_inc(pg_tr, 1)

            def outputs_mm(b, par):
                pe.wait_ge(s_const, 32)
                pe.wait_ge(se_prob, b + 1)
                for p in range(N_PAGES):
                    T(bank[6][:, p * 64:(p + 1) * 64], S[0:64, p * P:(p + 1) * P], ident[0:64, 0:64])
                T(bank[7][0:64, 0:64], S[0:64, PAST_LEN:NKEYS], ident[0:64, 0:64]).then_inc(st_tr, 1)
                pe.wait_ge(st_done, b + 1)
                for r in range(2):
                    o = bank[7][:, 128 + r * 64:192 + r * 64]
                    for p in range(N_PAGES):
                        mm(o, Cpg[par][:, p, r * P:(r + 1) * P], PT[:, p, :], start=(p == 0), stop=False)
                    i = mm(o, Cn[0:64, 2, r * P:(r + 1) * P], PT[0:64, 8, :], start=False, stop=True)
                i.then_inc(so_mm, 1)

            def seq_pe(b, par, kth, first):
                pe.wait_ge(pg_ready[par], 256 * kth + 256)
                page_tr(b, par, 0)
                for p in range(N_PAGES):
                    if p < N_PAGES - 1:
                        page_tr(b, par, p + 1)
                    pe.wait_ge(pg_ev, 8 * b + p + 1)
                    if not (first and p < 2):
                        pe.wait_ge(kk_sq, 8 * b + p - 1)
                    if not first and p < 2:
                        pe.wait_ge(sb_ev, 3 * b)
                        pe.wait_ge(ss_a, 3 * b)
                    for hf in range(2):
                        for r in range(2):
                            i = mm(bank[2 * (p % 2) + hf][:, :], cT[:, r, p * P:(p + 1) * P], wuk[:, r, hf * 512:(hf + 1) * 512],
                                   start=(r == 0), stop=(r == 1))
                    i.then_inc(kk_mm, 1)
                    if p == 3 and not first:
                        outputs_mm(b - 1, 1 - par)
                pe.wait_ge(q_picked, b + 1)
                if not first:
                    pe.wait_ge(so_done, b)
                for n in range(2):
                    for r in range(2):
                        i = mm(bank[6 + n][0:64, :], qab[:, r, :], cT[:, r, n * 512:(n + 1) * 512], start=(r == 0), stop=(r == 1))
                    i.then_inc(sa_mm, 1)
                pe.wait_ge(kk_sq, 8 * b + 8)
                for r in range(2):
                    mm(bank[2][0:64, 0:64], qab[:, r, :], cTn[:, r, SEQ:NTOK], start=(r == 0), stop=(r == 1))
                for n in range(2):
                    mm(bank[n][0:64, :], qrb[0:64, :], krT[0:64, n * 512:(n + 1) * 512], start=True, stop=True).then_inc(sb_mm, 1)
                mm(bank[2][0:64, 64:128], qrb[0:64, :], krTn[0:64, SEQ:NTOK], start=True, stop=True).then_inc(sb_mm, 1)
                pe.wait_ge(s_const, 32)
                pe.wait_ge(kk_rstd, b + 1)
                for n in range(2):
                    for p in range(4):
                        i = T(bank[4 + n][0:64, p * P:(p + 1) * P],
                              sksb[:, 4 * n + p, :], ident)
                    i.then_inc(rr_tr, 1)

            over_sequences(pe, seq_pe)
            outputs_mm(DEC_BATCH - 1, 1)
            pe.wait_ge(so_done, 8)
            for h in range(N_HEADS):
                if h >= 4:
                    pe.wait_ge(oTs_done, h - 3)
                for r in range(2):
                    i = mm(bank[h % 4][:, 0:NSMP], wuv[:, r, h * P:(h + 1) * P], OLTs[:, :, r, h, :], start=(r == 0), stop=(r == 1))
                i.then_inc(oTs_mm, 1)
            pe.wait_ge(oTs_done, 8)
            residual_mm(IT_WO, N_HEADS, lambda c, t: oT[:, c, tok(t)], None, wo_mm)

            norm(3)
            pe.wait_ge(s_wr, 16)
            for t in range(NT):
                for k in range(KC):
                    i = mm(bank[0][0:ROWS[t], 8 * t:8 * t + 8], hT[:, k, tok(t)], wr[:, k, :], start=(k == 0), stop=(k == KC - 1))
            i.then_inc(lg_mm, 1)
            pe.wait_ge(mask_done, 1)
            for t in range(NT):
                for u in range(t + 1):
                    mm(bank[1][:, 8 * t:8 * t + 8], triu if u == t else ones, gt[:, 8, 8 * u:8 * u + 8],
                       start=(u == 0), stop=(u == t))
            for u in range(NT):
                i = mm(bank[1][:, 24:32], ones, gt[:, 8, 8 * u:8 * u + 8], start=(u == 0), stop=(u == 2))
            i.then_inc(cum_mm, 1)

            def products(out, x, w, first, last):
                (xh, xl), (wh, wl) = x, w
                mm(out, xh, wh, start=first, stop=False)
                mm(out, xh, wl, start=False, stop=False)
                return mm(out, xl, wh, start=False, stop=last)

            def gather_mm(e, halves=(0, 1)):
                pe.wait_ge(sel_done, e + 1)
                for hf in halves:
                    for k in range(4):
                        c = slice((4 * hf + k) * P, (4 * hf + k + 1) * P)
                        for part in range(2):
                            for t in range(NT):
                                R = slice(0, ROWS[t])
                                i = mm(bank[6 + hf][:, k * P:(k + 1) * P], XSp[part][R, t, c], Sel[R, t, :],
                                       start=(part == 0 and t == 0), stop=(part == 1 and t == 2))
                    i.then_inc(ga_mm, 1)

            def scatter_mm(e, steps=range(6)):
                pe.wait_ge(y_lo, 2 * e + 2)
                for n in steps:
                    t, hf = n // 2, n % 2
                    if n >= 2:
                        pe.wait_ge(sc_done, 6 * e + n - 1)
                    for part in range(2):
                        i = mm(bank[6 + hf][0:ROWS[t], :], SelT[:, tok(t)], ygp[part][:, hf * 512:(hf + 1) * 512],
                               start=(part == 0), stop=(part == 1))
                    i.then_inc(sc_mm, 1)

            def h_tr(e, j):
                pe.wait_ge(e_h, 11 * e + j + 1)
                wait_pair(pe, e_low, e, j)
                for q in range(2):
                    i = T(bank[4 + j % 2][:, q * P:(q + 1) * P], hmul[:, j % 2, q * P:(q + 1) * P], ident)
                i.then_inc(e_tr, 1)

            def down_mm(e, j):
                pe.wait_ge(e_low, 11 * e + j + 1)
                pe.wait_ge(u_lo, NU * e + pos_dn(j) + 1)
                if j == 0 and not (isinstance(e, int) and e == 0):
                    pe.wait_ge(y_done, 2 * e)
                w = [x.rearrange("p (k c) -> p k c", k=2) for x in unit_parts(pos_dn(j))]
                for q in range(2):
                    for hf in range(2):
                        i = products(bank[hf][:, :], [x[:, j % 2, q, :] for x in hmT],
                                     [x[:, q, hf * 512:(hf + 1) * 512] for x in w],
                                     j == 0 and q == 0, j == FF_BL - 1 and q == 1)
                i.then_inc(unit_used, 1)

            def pass_pe(e, prev, nxt):
                for j in range(FF_BL):
                    if j == 0:
                        pe.wait_ge(xg_lo, 2 * e + 2)
                    wait_pair(pe, e_h, e, j)
                    for half in range(2):
                        if half and j:
                            h_tr(e, j - 1)
                        pe.wait_ge(u_lo, NU * e + pos_gu(j, half) + 1)
                        w = [x.rearrange("p (k c) -> p k c", k=4) for x in unit_parts(pos_gu(j, half))]
                        for k in range(4):
                            i = products(bank[2 + j % 2][:, :], [x[:, 4 * half + k, :] for x in xgT],
                                         [x[:, k, :] for x in w], half == 0 and k == 0, half == 1 and k == 3)
                        i.then_inc(unit_used, 1)
                    if j >= 2:
                        down_mm(e, j - 2)
                    if j in SCATTER_AT and prev:
                        scatter_mm(e - 1, SCATTER_AT[j])
                    if j == SELECT_AT:
                        if prev:
                            pe.wait_ge(sc_done, 6 * e)
                        for t in range(NT):
                            R = slice(0, ROWS[t])
                            T(bank[6][:, tok(t)], Sel[R, t, :].bitcast(f32), ident[R, R])
                        for t in range(NT):
                            R = slice(0, ROWS[t])
                            i = mm(bank[7][:, 0:1], Sel[R, t, :].bitcast(f32), gatec[R, t:t + 1], start=(t == 0), stop=(t == 2))
                        i.then_inc(selT_mm, 1)
                    if j in GATHER_AT and nxt:
                        pe.wait_ge(selT_done, e + 1)
                        gather_mm(e + 1, (GATHER_AT[j],))
                h_tr(e, FF_BL - 1)
                down_mm(e, FF_BL - 2)
                down_mm(e, FF_BL - 1)

            pe.wait_ge(xs_lo, 3)
            gather_mm(0)
            over_passes(pe, pass_pe)
            scatter_mm(N_EXPERTS - 1)

            def pe_further(i):
                e = i + N_EXPERTS
                pe.wait_ge(sc_done, 6 * e)
                gather_mm(e)
                pass_pe(e, False, False)
                scatter_mm(e)

            further(pe, pe_further)


_OUTS = [("y_p", (SEQ, D_MODEL)), ("y_s", (64, D_MODEL)), ("lat_p", (SEQ, KV_RANK)), ("kr_p", (SEQ, D_ROPE)),
         ("lat_s", (64, KV_RANK)), ("kr_s", (64, D_ROPE)), ("v_s", (64, D_GATE))]


def _constants():
    import numpy as np
    K = np.zeros((P, C_END), np.float32)
    r = np.arange(P)
    K[:, C_ID:C_ID + P] = np.eye(P)
    K[:, C_TRIU:C_TRIU + P] = r[:, None] <= r[None, :]
    K[:, C_CAUS:C_CAUS + P] = np.where(r[None, :] <= r[:, None], 0, MASKED)
    K[0:64, C_BLK:C_BLK + 64] = np.kron(np.eye(8), np.ones((8, 8)))
    K[0:8, C_REP:C_REP + 64] = np.tile(np.eye(8), (1, 8))
    h, q, b, b2, s = np.ix_(*[np.arange(8)] * 5)
    new = np.where((b == b2) & (s <= q) & (h >= 0), 0, MASKED)
    K[0:64, C_NEWM:C_NEWM + 512] = new.reshape(64, 512)
    K[:, C_IOTA:C_IOTA + P] = r[None, :]
    K[:, C_VALID:C_VALID + 3] = r[:, None] < np.array(ROWS)[None, :]
    K[:, C_PRI:C_PRI + 8] = np.arange(8, 0, -1)[None, :]
    K[:, C_EIDX:C_EIDX + 16] = np.tile(np.arange(8), 2)[None, :]
    pos = np.stack([r, r + P, PAST_LEN + r % DEC_SEQ], 1).astype(np.float32)
    half = D_ROPE // 2
    inv = np.float32(10000.0) ** (-np.arange(half, dtype=np.float32) / np.float32(half))
    ang = pos[:, :, None] * inv[None, None, :]
    K[:, C_COS:C_COS + 96] = np.cos(ang).reshape(P, 96)
    K[:, C_SIN:C_SIN + 96] = np.sin(ang).reshape(P, 96)
    return K


def kernel(**x):
    import numpy as np
    import concourse.bacc as bacc
    from concourse.bass_utils import run_bass_kernel_spmd

    x = {k: np.asarray(v) for k, v in x.items()}

    def columns(v):
        return v.reshape(-1, P).T

    def gate_up(g, u):
        n = g.shape[0]
        w = np.stack([a.reshape(n, KC, P, FF_BL, 256) for a in (g, u)], 4)
        return np.ascontiguousarray(w.transpose(0, 3, 2, 1, 4, 5)).reshape(n, FF_BL, P, KC * 512)

    G = np.concatenate([columns(x[k].reshape(-1)) if isinstance(k, str) else columns(k) for k in (
        "a_norm_g", x["a_b_in"][0, :D_GATE], x["f_norm_g"][0], "kv_norm_g", "b_norm_g", "b_q_lat_g", "b_qn_g",
        "kn_g", x["f_norm_g"][1])], 1)
    md = x["m_w_down"][0].reshape(N_EXPERTS, FF_BL, 2, P, D_MODEL).transpose(0, 1, 3, 2, 4)
    gu = gate_up(x["m_w_gate"][0], x["m_w_up"][0]).reshape(N_EXPERTS, FF_BL, P, 2, UNIT)
    units = np.empty((N_EXPERTS, 3 * FF_BL, P, UNIT), np.float32)
    for j in range(FF_BL):
        for half in range(2):
            units[:, 2 * j + half + max(0, j - 2)] = gu[:, j, :, half]
        units[:, min(3 * j + 6, 2 * FF_BL + j)] = md[:, j].reshape(N_EXPERTS, P, UNIT)
    data = {
        "xp": x["x_prompt"][0], "xs_in": x["x_sample"].reshape(64, D_MODEL), "c_lat": x["cache_latent"],
        "c_kr": x["cache_krope"], "ptab": x["page_table"].reshape(1, -1), "consts": _constants(), "cols": G,
        "b_v": x["a_b_in"][:, D_GATE:], "sgu_g": x["a_sgu_g"], "w_in": x["a_w_in"][0],
        "wsT": x["a_w_s"][0].transpose(2, 0, 1), "b_s": x["a_b_s"].reshape(1, -1), "w_out": x["a_w_out"][0],
        "b_out": x["a_b_out"], "kv_lat_g": x["kv_lat_g"][None], "kr_g": x["kr_g"][None], "qr_g": x["b_qr_g"],
        "w_ckr": np.concatenate([x["w_dkv"], x["w_kr"]], 1), "w_uk": x["w_uk"].reshape(KV_RANK, -1),
        "w_ukT": x["w_uk"].transpose(2, 1, 0), "w_uv": x["w_uv"].reshape(KV_RANK, -1), "w_dq": x["b_w_dq"][0],
        "w_uq": x["b_w_uq"][0].reshape(Q_RANK, -1), "w_o": x["b_w_o"][0],
        "w_router": x["m_w_router"][0].reshape(KC, P, N_EXPERTS).transpose(1, 0, 2),
        "d_gu": gate_up(x["d_w_gate"], x["d_w_up"])[0].reshape(FF_BL, P, KC, 512), "d_down": x["d_w_down"][0],
        "m_un": units,
    }
    nc = bacc.Bacc("TRN2", target_bir_lowering=False, num_devices=1)
    arrays, args = {}, {}
    for name, a in data.items():
        a = np.ascontiguousarray(a)
        arrays["in_" + name] = a
        args[name] = nc.dram_tensor("in_" + name, a.shape, mybir.dt.from_np(a.dtype), kind="ExternalInput").ap()
    for name, shape in _OUTS:
        args[name] = nc.dram_tensor("out_" + name, shape, mybir.dt.float32, kind="ExternalOutput").ap()
    yoco_step(nc, **args)
    r = run_bass_kernel_spmd(nc, [arrays], core_ids=[0]).results[0]
    y_p, y_s, lat_p, kr_p, lat_s, kr_s, v_s = (r["out_" + n] for n, _ in _OUTS)
    return (y_p[None], y_s.reshape(8, 8, -1), lat_p[None], kr_p[None], lat_s.reshape(8, 8, -1),
            kr_s.reshape(8, 8, -1), v_s.reshape(1, 8, 8, -1))
```

```python
import concourse.bass as bass
from concourse import mybir
from contextlib import ExitStack

P = 128
D_MODEL, SEQ, DEC_BATCH, DEC_SEQ = 1024, 256, 8, 8
PAST_LEN, PAGE = 1024, 128
D_GATE, N_GROUPS, N_HEADS = 2048, 8, 8
Q_RANK, KV_RANK, D_NOPE, D_ROPE = 384, 256, 128, 64
D_FF, N_EXPERTS = 2816, 8
EPS = 1e-6
ATTN_SCALE = (D_NOPE + D_ROPE) ** -0.5
MASKED = -1e30

NT = 3
ROWS = [128, 128, DEC_BATCH * DEC_SEQ]
NTOK = sum(ROWS)
NSMP = ROWS[2]
KC = D_MODEL // P
N_PAGES = PAST_LEN // PAGE
UNIT = 2048
FF_CH = D_FF // P
FF_BL = FF_CH // 2
NKEYS = PAST_LEN + NSMP
CAP = 128
MAX_EXTRA = 4
NITEM = N_EXPERTS + MAX_EXTRA

C_ID, C_TRIU, C_CAUS, C_BLK, C_REP, C_NEWM, C_IOTA = 0, 128, 256, 384, 448, 512, 1024
C_VALID, C_PRI, C_EIDX, C_COS, C_SIN = 1152, 1155, 1163, 1179, 1275
C_END = 1371
G_A, G_BU, G_F0, G_KV, G_B, G_QL, G_QN, G_KN, G_F1 = 0, 8, 24, 32, 40, 48, 51, 52, 53
G_END = 61


def tok(t):
    return slice(t * P, t * P + ROWS[t])


def yoco_step(nc, xp, xs_in, c_lat, c_kr, ptab, consts, cols, b_v, sgu_g, w_in, wsT, b_s, w_out, b_out,
              kv_lat_g, kr_g, qr_g, w_ckr, w_uk, w_ukT, w_uv, w_dq, w_uq, w_o, w_router,
              d_gu, d_down, m_un, y_p, y_s, lat_p, kr_p, lat_s, kr_s, v_s):
    f32, f32r, i32 = mybir.dt.float32, mybir.dt.float32r, mybir.dt.int32
    ALU, ACT, AX = mybir.AluOpType, mybir.ActivationFunctionType, mybir.AxisListType.X
    MUL, ADD, SUB = ALU.mult, ALU.add, ALU.subtract
    ctx = ExitStack()
    with ctx:
        def sb(name, shape, dt=f32):
            return ctx.enter_context(nc.sbuf_tensor(name, shape, dt))

        def sem(name):
            return ctx.enter_context(nc.semaphore(name))

        W_KB = 107
        NW = 5
        ARENA = W_KB * 256 + NW * 4096
        slab_at = -(-nc.sbuf_base // 32) * 32
        ctx.enter_context(nc.sbuf_tensor("slab", [P, ARENA], f32))
        placed = {}
        X = sb("X", [P, NT, D_MODEL])
        K = sb("K", [P, C_END])
        G = sb("G", [P, G_END])
        brow = sb("brow", [P, KV_RANK + 2 * D_ROPE])
        pages_i = sb("pages_i", [1, DEC_BATCH * N_PAGES], i32)
        st = sb("st", [P, 128])
        rs_m, rs_t = sb("rs_m", [P, 64]), sb("rs_t", [P, 64])

        def area(kb, *shape, r=False):
            n = 1
            for s in shape:
                n *= s
            assert int(kb * 256) + n <= ARENA and kb * 32 == int(kb * 32)
            name = f"at{kb}_{n}" + ("_r" if r else "")
            if name not in placed:
                placed[name] = nc.alloc_sbuf_tensor_at(name.replace(".", "_"), [P, n], f32r if r else f32,
                                                       offset=slab_at + int(kb * 1024))
            v = placed[name][:, :]
            if len(shape) == 2:
                return v.rearrange("p (a b) -> p a b", a=shape[0])
            if len(shape) == 3:
                return v.rearrange("p (a b c) -> p a b c", a=shape[0], b=shape[1])
            if len(shape) == 4:
                return v.rearrange("p (a b c d) -> p a b c d", a=shape[0], b=shape[1], c=shape[2])
            return v

        ident, triu, causal = K[:, C_ID:C_ID + P], K[:, C_TRIU:C_TRIU + P], K[:, C_CAUS:C_CAUS + P]
        iota = K[:, C_IOTA:C_IOTA + P]
        XS = area(60.5, NT, D_MODEL)
        hT = area(72.5, KC, NTOK)
        hbT = area(82.5, KC, NTOK)
        V = area(0, NT, D_GATE)
        uT = area(24, 16, NTOK)
        bv_bc = area(44, D_GATE)
        sgu_bc = area(52, D_GATE)
        vjunk = area(60.5, D_GATE)
        bs_raw = area(102.5, N_GROUPS, P)
        bs_bc = area(72.5, N_GROUPS, NTOK)
        ws = area(92.5, N_GROUPS, P)
        bout_bc = area(96.5, D_MODEL)
        ws_new = area(100.5, N_GROUPS, DEC_BATCH, DEC_SEQ)
        gtmp = area(102.5, 2, NTOK)
        wrep = area(106.5, N_GROUPS, DEC_SEQ)
        hTp = (area(82.5, KC, NTOK, r=True), area(72.5, KC, NTOK, r=True))
        u_high = [area(k, 8, NTOK, r=True) for k in (44, 82.5)]
        u_low = area(24, 16, NTOK, r=True)
        ffT = area(0, FF_CH, NTOK)
        ffTp = (area(31, FF_CH, NTOK, r=True), area(0, FF_CH, NTOK, r=True))
        sg = area(28, 2, NTOK)
        wuk = area(0, 2, N_HEADS * D_NOPE)
        wuv = area(8, 2, N_HEADS * P)
        Cn = area(16, NT, KV_RANK)
        KRn = area(19, NT, D_ROPE)
        cTn = area(20, 2, NTOK)
        krTn = area(22.5, NTOK)
        qrP = area(24, N_HEADS, SEQ)
        qrS = area(32, DEC_BATCH, N_HEADS, DEC_SEQ)
        qnT = area(34, N_HEADS, NTOK)
        wukT = area(44, N_HEADS, KV_RANK)
        cqs = area(52, NT, Q_RANK)
        cqT = area(56.5, 3, NTOK)
        Q = area(60.5, NT, N_HEADS, D_NOPE + D_ROPE)
        QR = area(78.5, NT, N_HEADS, D_ROPE)
        qjunk = area(84.5, N_HEADS, D_NOPE + D_ROPE)
        kjunk = area(102.5, N_HEADS, D_NOPE)
        krtmp = area(92.5, NT, D_ROPE)
        rope1, rope2 = area(94.5, N_HEADS, 32), area(95.5, N_HEADS, 32)
        krope1, krope2 = area(93.5, NT, 32), area(94, NT, 32)
        qaP = area(60.5, 2, N_HEADS, SEQ)
        Rb = area(76.5, N_HEADS, SEQ)
        qaS = area(88.5, DEC_BATCH, 2, N_HEADS * DEC_SEQ)
        OLTp = area(34, 2, N_HEADS, SEQ)
        sP = area(52, 3, SEQ)
        PTp = area(55, 2, 2, P)
        cTp = (area(34, 2, PAST_LEN, r=True), area(W_KB + 32, 2, PAST_LEN, r=True))
        wukp = (area(W_KB + 40, 2, N_HEADS * D_NOPE, r=True), area(0, 2, N_HEADS * D_NOPE, r=True))
        qabp = (area(24, 2, N_HEADS * DEC_SEQ, r=True), area(24.5, 2, N_HEADS * DEC_SEQ, r=True))
        krT = area(42.25, PAST_LEN)
        S = area(46.34375, NKEYS)
        stmp = area(52, NKEYS)
        Rs = area(56.25, NKEYS)
        RsN = area(23.75, NSMP)
        qab = area(25, 2, N_HEADS * DEC_SEQ)
        qrb = area(26, N_HEADS * DEC_SEQ)
        oT = area(60.5, N_HEADS, NTOK)
        sksb = area(74.5, N_PAGES, N_HEADS * DEC_SEQ)
        rnb = area(58, N_HEADS * DEC_SEQ)
        OLTs = area(70.5, DEC_BATCH, 2, N_HEADS, DEC_SEQ)
        Cpg = [area(92.5, N_PAGES, KV_RANK), area(76.5, N_PAGES, KV_RANK)]
        KRpg = [area(100.5, N_PAGES, D_ROPE), area(102.5, N_PAGES, D_ROPE)]
        PT = area(104.5, 9, N_HEADS * DEC_SEQ)
        sjunk = area(84.5, N_HEADS, D_NOPE)
        at_raw = [W_KB + 8 * i for i in range(9)]
        raw = [area(k, UNIT) for k in at_raw]
        low_part = [area(k, UNIT, r=True) for k in at_raw]
        high_part = [area(k, UNIT, r=True) for k in (W_KB + 72, 0, 8, 16, 24, 72.5)]
        dense_high_part = [area(W_KB + 48 + 8 * i, UNIT, r=True) for i in range(4)]
        Sel = area(32, NT, P, r=True)
        SelT = area(34, NTOK, r=True)
        xg = area(36, KC, P)
        xgT = (area(40, KC, P, r=True), area(44, KC, P, r=True))
        gsil = area(48, 2, 256)
        hmul = area(50, 2, 256)
        hmT = (area(52, 2, 2, P, r=True), area(54, 2, 2, P, r=True))
        yg = area(56, D_MODEL)
        ygp = (area(94.5, D_MODEL, r=True), area(98.5, D_MODEL, r=True))
        XSp = (area(82.5, NT, D_MODEL, r=True), area(60.5, NT, D_MODEL, r=True))
        gt = area(102.5, 24, 24)
        item_pos = area(105, NITEM, NT)
        item_gate = area(105.25, NITEM, NT)
        posc = area(105.5, NT)
        gatec = area(105.59375, NT)
        gslot = area(105.6875, 1)
        wr = area(106.5, KC, N_EXPERTS)
        xtab = area(80.5, 8, 48)
        ones = area(82, P)
        cnt_i = sb("cnt_i", [1, 1 + MAX_EXTRA], i32)

        SS, RSTD, SSV, RSV = 0, 4, 8, 12
        SCK, RCK = 16, 24
        SQL, RQL = 32, 36
        SKN = 40
        SQN, SQR = 64, 88
        PMX, PNM, PSUM_, PRC = 112, 114, 116, 118
        SMX, SNM, SSUM, SRC = 120, 121, 122, 123
        sks = sb("sks", [P, N_PAGES, N_HEADS])

        bank = [ctx.enter_context(nc.psum_tensor(f"bank{i}", [P, 512], f32)) for i in range(8)]

        s_const, s_x, s_rows, s_gm, s_uk, s_mla, s_wr, s_pt = (sem(n) for n in (
            "const_loaded", "x_loaded", "rows_loaded", "gmlp_rows_loaded", "uk_loaded", "mla_weights_loaded",
            "router_loaded", "page_table_loaded"))
        w_ready = [sem(f"w_ready{i}") for i in range(NW)]
        w_used = sem("w_used")
        s_out, y_out = sem("keys_written"), sem("y_written")
        rnb_done = sem("new_key_rstd")
        s_zero = sem("zeroed")
        v_out = sem("v_rows_written")
        chain = sem("vector_chain")
        achain = sem("scalar_chain")
        x_ready = [sem(f"x_ready{i}") for i in range(5)]
        nsq, nxs, ntr, nht, n_hi, n_lo = (sem(n) for n in (
            "norm_squares", "norm_scaled", "norm_transposed", "norm_evacuated", "norm_high", "norm_split"))
        ug_hi, ug_lo, ff_hi, ff_lo = (sem(n) for n in ("gated_high", "gated_split", "ff_high", "ff_split"))
        (v_mm, v_biased, v_gelu, v_sq, v_norm, u_mm, u_done, rep_mm, ws_done, mix_mm, gu_done, gout_mm,
         g_mm, silu_done, up_mm, ff_done, dout_mm) = (sem(n) for n in (
             "v_mm", "v_biased", "v_gelu", "v_squares", "v_normed", "u_mm", "u_gelu", "ws_replicated",
             "ws_ready", "mix_mm", "gated", "gmlp_out_mm", "gate_mm", "silu_done", "up_mm", "ff_done",
             "dense_out_mm"))
        (ckr_mm, ckr_sq, c_new, kr_new, dq_mm, dq_sq, cq_scaled, cq_tr, cqT_done, ck_tr, ckT_done, kn_mm,
         kn_sq, kn_red, q_mm, q_copied, q_sq, q_scaled, qn_tr, qr_tr, qnT_done, qrT_done, qa_mm, qa_act, qa_dve,
         rb_mm, rb_done) = (sem(n) for n in (
             "ckr_mm", "ckr_squares", "c_new", "kr_new", "dq_mm", "dq_squares", "cq_scaled",
             "cq_transposed", "cqT_done", "ck_transposed", "ckT_done", "new_key_mm", "new_key_squares",
             "new_key_reduced", "q_mm", "q_copied", "q_squares", "q_scaled", "qn_transposed", "qr_transposed",
             "qnT_done", "qrT_done", "qabs_mm", "qabs_act", "qabs_dve", "r_spread", "r_copied"))
        (ps_mm, ps_max, ps_exp, ps_prob, pp_tr, pp_done, po_mm, po_done, oTp_mm, oTp_done, oTs_mm, oTs_done,
         wo_mm) = (sem(n) for n in (
             "p_scores_mm", "p_max", "p_exp", "p_prob", "p_prob_tr", "p_probT", "p_out_mm", "p_out",
             "oT_prompt_mm", "oT_prompt", "oT_sample_mm", "oT_sample", "wo_mm"))
        wuk_hi, wuk_lo, pg_lo = (sem(n) for n in ("w_uk_high", "w_uk_split", "page_split"))
        pg_first = [sem("first_pages_ready0"), sem("first_pages_ready1")]
        pg_ready = [sem("pages_ready0"), sem("pages_ready1")]
        (q_picked, pg_tr, pg_ev, kk_mm, kk_sq, kk_red, kk_rstd, sa_mm, sb_mm, sb_ev, rr_tr, rr_ev, ss_a, ss_done,
         se_exp, se_prob, st_tr, st_done, so_mm, so_done) = (sem(n) for n in (
             "query_picked", "page_transposed", "page_evacuated", "key_mm", "key_squares", "key_reduced",
             "key_rstd", "score_c_mm", "score_r_mm", "score_r_copied", "r_transposed", "r_evacuated",
             "score_c_read", "scores_max", "s_exp", "s_prob", "s_prob_tr", "s_probT", "s_out_mm", "s_out"))
        (lg_mm, lg_max, lg_exp, mask_done, cum_mm, table_done) = (sem(n) for n in (
            "logits_mm", "logits_max", "logits_exp", "routed", "ranks_mm", "tables_done"))
        raw_ready = [sem(f"unit_loaded{i}") for i in range(9)]
        (u_hi, u_lo, unit_used, xs_hi, xs_lo, e_low, xg_hi, xg_lo, y_hi, y_lo, e_silu, e_h, e_tr, e_trd, sel_done, ga_mm, ga_done, selT_mm, selT_done, y_done,
         sc_mm, sc_done) = (sem(n) for n in (
             "unit_high", "unit_split", "unit_used", "rows_high", "rows_split", "expert_hT_split", "gathered_high",
             "gathered_split", "y_high", "y_split", "expert_silu", "expert_h", "expert_h_tr", "expert_hT",
             "selection_done", "gather_mm", "gathered", "selT_mm", "selT_done",
             "expert_y_gated", "scatter_mm", "scattered"))

        def rows_of(w, a, b):
            return w[a * P:b * P, :].rearrange("(k p) n -> p k n", p=P)

        dense = [rows_of(w_in, 4 * h, 4 * h + 4)[:, :, D_GATE + n * 512:D_GATE + (n + 1) * 512]
                 for n in range(4) for h in range(2)]
        D_U = len(dense)
        dense += [rows_of(w_in, 0, KC)[:, :, n * 256:(n + 1) * 256] for n in range(8)]
        D_OUT = len(dense)
        dense += [rows_of(w_out, 2 * n, 2 * n + 2) for n in range(8)]
        D_GU = len(dense)
        dense += [d_gu[n] for n in range(FF_CH)]
        D_DN = len(dense)
        dense += [rows_of(d_down, 2 * n, 2 * n + 2) for n in range(FF_BL)]
        ND, ND_RAW, ND_HI = len(dense), 6, 4

        items = [(rows_of(w_ckr, 0, KC), KC, KV_RANK + D_ROPE), (rows_of(w_dq, 0, KC), KC, Q_RANK)]
        items += [(rows_of(w_uq, 0, 3)[:, :, n * 768:(n + 1) * 768], 3, 768) for n in range(2)]
        items += [(rows_of(w_o, 4 * n, 4 * n + 4), 4, D_MODEL) for n in range(2)]
        IT_CK, IT_DQ, IT_UQ, IT_WO = 0, 1, 2, 4
        IT_SLOT = [0, 1, 2, 3, 4, 3]
        IT_LAST = [1, 2, 5, 6, 5]

        def weights(n):
            _, k, c = items[n]
            return area(W_KB + IT_SLOT[n] * 16, k, c)

        def await_item(eng, n):
            eng.wait_ge(w_ready[IT_SLOT[n]], 16 * (IT_SLOT[:n].count(IT_SLOT[n]) + 1))

        NU = 3 * FF_BL

        def pos_gu(j, half):
            return 2 * j + half + max(0, j - 2)

        def pos_dn(j):
            return min(3 * j + 6, NU - FF_BL + j)

        def cycle(groups):
            slots = [i for n in groups for i in range(n)]
            assert len(slots) == NU
            last = [max(k for k in range(-NU, q) if slots[k % NU] == slots[q]) for q in range(NU)]
            return slots, last, [slots[:q].count(slots[q]) for q in range(NU)]

        raw_slot, raw_last, raw_nth = cycle([9] + [8] * 3)
        hi_slot, hi_last, _ = cycle([6] * 3 + [5] * 3)

        SCATTER_AT = {3: (0, 1), 4: (2, 3), 5: (4, 5)}
        SELECT_AT = 6
        GATHER_AT = {7: 0, 8: 1}

        def split_in(j, nxt):
            a = pos_gu(j, 0) + 4
            early, late = ([], [5]) if j == 0 else ([a], [a + 1] if j in (1, FF_BL - 1) else [a + 1, a + 2])
            return [[q for q in x if q < NU or nxt] for x in (early, late)]

        LAST_SPLIT = range(NU + 1, NU + 5)

        def unit_parts(q):
            return high_part[hi_slot[q]], low_part[raw_slot[q]]

        def raw_count(e, q):
            before = len(range(raw_slot[q], ND, ND_RAW)) if raw_slot[q] < ND_RAW else 0
            return (e * raw_slot.count(raw_slot[q]) + raw_nth[q] + 1 + before) * 16

        def wait_last(eng, done, e, last):
            if not (isinstance(e, int) and NU * e + last < 0):
                eng.wait_ge(done, ND + NU * e + last + 1)

        def dense_slots(n):
            return n % ND_RAW, n % ND_HI

        def in_order(step):
            done = [0]

            def ahead(n):
                for i in range(done[0], min(n + 1, ND)):
                    step(i)
                    done[0] = i + 1
            return ahead

        def u_parts(c):
            return u_high[c // 8][:, c % 8, :], u_low[:, c, :]

        MG = {}

        def group(name, n, empties):
            for i in range(n):
                MG[name, i] = (len(MG), *empties(i))

        group("ckr", 3, lambda i: (c_new, i + 1))
        group("dq", 3, lambda i: (cq_scaled, i + 1))
        group("cqT", 3, lambda i: (cqT_done, i + 1))
        group("ckT", 3, lambda i: (ckT_done, i + 1))
        group("kn", 6, lambda i: (kn_sq, i + 1))
        group("q", 12, lambda i: (q_copied, i + 1))
        group("qT", 12, lambda i: (qnT_done, 2 * (i // 4) + i % 4 + 1) if i % 4 < 2 else (qrT_done, 2 * (i // 4) + i % 4 - 1))
        group("qa", 16, lambda i: (qa_dve, i // 2 + 1) if i % 2 else (qa_act, i // 2 + 1))
        group("rb", 5, lambda i: (rb_done, i + 1))
        MGL = list(MG.values())

        def mla_bank(pe, name, i):
            n = MG[name, i][0]
            if pe is not None and n >= 8:
                pe.wait_ge(MGL[n - 8][1], MGL[n - 8][2])
            return bank[n % 8]

        P_BANK = [0, 1, 6]

        def over_sequences(eng, body):
            body(0, 0, 0, True)
            with eng.Fori(0, DEC_BATCH // 2 - 1) as i:
                body(2 * i + 1, 1, i, False)
                body(2 * i + 2, 0, i + 1, False)
            body(DEC_BATCH - 1, 1, DEC_BATCH // 2 - 1, False)

        def rr_bank(p, n=1):
            b, c = (bank[3], p) if p < 4 else (bank[2], p - 3) if p < 7 else (bank[4], 3)
            return b[0:64, c * P:(c + n) * P]

        def is_last(b):
            return isinstance(b, int) and b == DEC_BATCH - 1

        def over_passes(eng, body):
            body(0, False, True)
            with eng.Fori(1, N_EXPERTS - 1) as e:
                body(e, True, True)
            body(N_EXPERTS - 1, True, False)

        def further(eng, body):
            eng.wait_ge(table_done, 1)
            n = eng.value_load(cnt_i[0:1, 0:1], min_val=0, max_val=MAX_EXTRA)
            with eng.If(n > 0):
                with eng.Fori(0, n) as i:
                    body(i)

        def wait_pair(eng, used, e, j):
            if not (isinstance(e, int) and e == 0 and j < 2):
                eng.wait_ge(used, 11 * e + j - (0 if j == 0 else 1))

        mm = nc.tensor.matmul
        block = ctx.enter_context(nc.Block())

        @block.sync
        def _(sp):
            for t in range(NT):
                src = xp[t * P:(t + 1) * P, :] if t < 2 else xs_in
                sp.dma_start(X[0:ROWS[t], t, :], src).then_inc(s_x, 16)
            for n, src in enumerate(dense):
                if n >= ND_RAW:
                    sp.wait_ge(unit_used, n - ND_RAW + 1)
                dst = raw[dense_slots(n)[0]]
                if len(src.shape) == 3:
                    dst = dst.rearrange("p (k c) -> p k c", k=src.shape[1])
                sp.dma_start(dst, src).then_inc(raw_ready[dense_slots(n)[0]], 16)
            sp.wait_ge(unit_used, ND)
            for n, (src, k, c) in enumerate(items):
                if n == IT_UQ:
                    sp.wait_ge(x_ready[2], 3)
                    sp.dma_start(wuk[:, :, :], rows_of(w_uk, 0, 2)).then_inc(s_uk, 16)
                if n == IT_WO:
                    sp.dma_start(wukT[:, :, :], w_ukT).then_inc(s_mla, 16)
                    sp.dma_start(wuv[:, :, :], rows_of(w_uv, 0, 2)).then_inc(s_mla, 16)
                if n == len(items) - 1:
                    sp.wait_ge(w_used, IT_UQ + 2)
                sp.dma_start(weights(n), src).then_inc(w_ready[IT_SLOT[n]], 16)

            def load_unit(e, q, expert=None):
                wait_last(sp, unit_used, e, raw_last[q])
                x = e if expert is None else expert
                src = m_un[x, q] if isinstance(x, int) else m_un[bass.ds(x, 1), q].rearrange("a p n -> (a p) n")
                sp.dma_start(raw[raw_slot[q]], src).then_inc(raw_ready[raw_slot[q]], 16)

            for q in range(NU):
                if q < 9:
                    sp.wait_ge(w_used, IT_LAST[q // 2])
                load_unit(0, q)
            with sp.Fori(1, N_EXPERTS) as e:
                for q in range(NU):
                    load_unit(e, q)

            def sp_further(i):
                e = sp.value_load(cnt_i[0:1, bass.ds(i + 1, 1)], min_val=0, max_val=N_EXPERTS - 1)
                for q in range(NU):
                    load_unit(i + N_EXPERTS, q, expert=e)

            further(sp, sp_further)
            sp.wait_ge(x_ready[4], 1)
            for t in range(NT):
                dst = y_p[t * P:(t + 1) * P, :] if t < 2 else y_s
                sp.dma_start(dst, X[0:ROWS[t], t, :]).then_inc(y_out, 16)
            sp.wait_ge(y_out, 16 * NT)
            sp.wait_ge(s_out, 16 * 4)
            sp.wait_ge(v_out, 16)

        @block.gpsimd
        def _(pool):
            pool.dma_start(pages_i[:, :], ptab).then_inc(s_pt, 16)
            pool.wait_ge(v_norm, 3)
            pool.dma_start(v_s, V[0:NSMP, 2, :]).then_inc(v_out, 16)
            pool.wait_ge(c_new, 3)
            pool.dma_start(lat_p.rearrange("(t p) r -> p t r", p=P), Cn[:, 0:2, :]).then_inc(s_out, 16)
            pool.dma_start(lat_s, Cn[0:NSMP, 2, :]).then_inc(s_out, 16)
            pool.wait_ge(kr_new, 1)
            pool.dma_start(kr_p.rearrange("(t p) r -> p t r", p=P), KRn[:, 0:2, :]).then_inc(s_out, 16)
            pool.dma_start(kr_s, KRn[0:NSMP, 2, :]).then_inc(s_out, 16)
            pool.wait_ge(s_pt, 16)

            def load_pages(b, par):
                for p in range(N_PAGES):
                    arrived = pg_first[par] if p < 2 else pg_ready[par]
                    page = pool.value_load(pages_i[0:1, bass.ds(b * N_PAGES + p, 1)], min_val=0,
                                           max_val=c_lat.shape[0] - 1)
                    pool.dma_start(Cpg[par][:, p, :], c_lat[bass.ds(page, 1)].rearrange("a p r -> (a p) r"))\
                        .then_inc(arrived, 16)
                    pool.dma_start(KRpg[par][:, p, :], c_kr[bass.ds(page, 1)].rearrange("a p r -> (a p) r"))\
                        .then_inc(arrived, 16)

            pool.wait_ge(qnT_done, 6)
            pool.wait_ge(qrT_done, 6)
            load_pages(0, 0)
            pool.wait_ge(po_done, 16)
            load_pages(1, 1)
            with pool.Fori(1, DEC_BATCH // 2) as i:
                for par in range(2):
                    pool.wait_ge(so_mm, 2 * i + par - 1)
                    load_pages(2 * i + par, par)

        @block.scalar
        def _(act):
            A = nc.scalar.activation
            act.dma_start(K[:, :], consts).then_inc(s_const, 16)
            act.dma_start(G[:, :], cols).then_inc(s_const, 16)
            act.dma_start(ws[:, :, :], wsT).then_inc(s_gm, 16)
            act.dma_start(bs_raw, b_s.to_broadcast([P, N_GROUPS * P]).rearrange("p (g i) -> p g i", g=N_GROUPS))\
                .then_inc(s_gm, 16)
            act.dma_start(bv_bc, b_v.to_broadcast([P, D_GATE])).then_inc(s_gm, 16)
            act.dma_start(sgu_bc, sgu_g.to_broadcast([P, D_GATE])).then_inc(s_gm, 16)
            act.dma_start(bout_bc, b_out.to_broadcast([P, D_MODEL])).then_inc(s_gm, 16)
            act.dma_start(brow[:, 0:256], kv_lat_g.to_broadcast([P, KV_RANK])).then_inc(s_rows, 16)
            act.dma_start(brow[:, 256:320], kr_g.to_broadcast([P, D_ROPE])).then_inc(s_rows, 16)
            act.dma_start(brow[:, 320:384], qr_g.to_broadcast([P, D_ROPE])).then_inc(s_rows, 16)

            def norm_squares(s):
                for t in range(NT):
                    if s == 0 and t == 0:
                        act.wait_ge(s_x, 16 * NT)
                    elif s:
                        act.wait_ge(x_ready[s], t + 1)
                    A(XS[0:ROWS[t], t, :], X[0:ROWS[t], t, :], ACT.Square, scale=D_MODEL ** -0.5,
                      accum_out=st[0:ROWS[t], SS + t:SS + t + 1]).then_inc(nsq, 1)

            def dense_high(n):
                i, h = dense_slots(n)
                act.wait_ge(raw_ready[i], 16 * (n // ND_RAW + 1))
                if n >= ND_HI:
                    act.wait_ge(unit_used, n - ND_HI + 1)
                A(dense_high_part[h], raw[i], ACT.Copy).then_inc(u_hi, 1)

            ahead = in_order(dense_high)

            def norm_high(s):
                for t in range(NT):
                    for hf in range(2):
                        h = slice(4 * hf, 4 * hf + 4)
                        act.wait_ge(nht, 6 * s + 2 * t + hf + 1)
                        A(hTp[0][:, h, tok(t)], hT[:, h, tok(t)], ACT.Copy).then_inc(n_hi, 1)

            act.wait_ge(s_zero, 1)
            norm_squares(0)
            ahead(1)
            norm_high(0)
            ahead(3)
            for o in range(12):
                n, t = o // NT, o % NT
                if t == 0:
                    ahead(2 * n + 4)
                act.wait_ge(v_biased, o + 1)
                v = V[0:ROWS[t], t, n * 512:(n + 1) * 512]
                A(v, v, ACT.Gelu_apprx_tanh).then_inc(v_gelu, 1)
            for t in range(NT):
                act.wait_ge(v_gelu, 12)
                if t:
                    act.wait_ge(v_sq, t)
                A(vjunk[0:ROWS[t], :], V[0:ROWS[t], t, :], ACT.Square, scale=D_GATE ** -0.5,
                  accum_out=st[0:ROWS[t], SSV + t:SSV + t + 1]).then_inc(v_sq, 1)
            for c in range(16):
                if c % 2 == 0:
                    ahead(D_U + c // 2 + 3)
                act.wait_ge(u_mm, c + 1)
                A(uT[:, c, :], bank[(12 + c) % 8][:, 0:NTOK], ACT.Gelu_apprx_tanh,
                  bias=G[:, G_BU + c:G_BU + c + 1]).then_inc(u_done, 1)

            ahead(D_OUT + 3)
            for c in range(16):
                act.wait_ge(gu_done, c + 1)
                A(u_parts(c)[0], uT[:, c, :], ACT.Copy).then_inc(ug_hi, 1)
            ahead(D_GU + 2)

            norm_squares(1)
            ahead(D_GU + 3)
            norm_high(1)

            def ff_high(f):
                act.wait_ge(ff_done, f + 1)
                A(ffTp[0][:, f, :], ffT[:, f, :], ACT.Copy).then_inc(ff_hi, 1)

            for f in range(FF_CH):
                ahead(D_GU + f + 3)
                act.wait_ge(g_mm, f + 1)
                if f >= 2:
                    act.wait_ge(ff_done, f - 1)
                A(sg[:, f % 2, :], bank[2 * (f % 4)][:, 0:NTOK], ACT.Silu).then_inc(silu_done, 1)
                if f:
                    ff_high(f - 1)
            ff_high(FF_CH - 1)
            ahead(ND - 1)

            norm_squares(2)
            for t in range(NT):
                R = slice(0, ROWS[t])
                act.wait_ge(ckr_mm, t + 1)
                if t:
                    act.wait_ge(ckr_sq, t)
                b = mla_bank(None, "ckr", t)
                A(kjunk[R, 0:2, :], b[R, 0:256].rearrange("p (a b) -> p a b", a=2), ACT.Square, scale=1 / 16,
                  accum_out=st[R, SCK + 2 * t:SCK + 2 * t + 1])
                A(kjunk[R, 2, 0:64], b[R, 256:320], ACT.Square, scale=1 / 8,
                  accum_out=st[R, SCK + 2 * t + 1:SCK + 2 * t + 2]).then_inc(ckr_sq, 1)
            for t in range(NT):
                R = slice(0, ROWS[t])
                act.wait_ge(dq_mm, t + 1)
                if t:
                    act.wait_ge(dq_sq, t)
                else:
                    act.wait_ge(ckr_sq, 3)
                A(kjunk[R, 0:3, :], mla_bank(None, "dq", t)[R, 0:384].rearrange("p (a b) -> p a b", a=3),
                  ACT.Square, scale=Q_RANK ** -0.5, accum_out=st[R, SQL + t:SQL + t + 1]).then_inc(dq_sq, 1)
            for t in range(NT):
                act.wait_ge(ck_tr, t + 1)
                b, n = mla_bank(None, "ckT", t), ROWS[t]
                A(cTn[:, :, tok(t)], b[:, 0:256].rearrange("p (a b) -> p a b", a=2)[:, :, 0:n], ACT.Copy)
                A(krTn[0:64, tok(t)], b[0:64, 256:256 + n], ACT.Copy).then_inc(ckT_done, 1)
            act.wait_ge(dq_sq, 3)
            for o in range(6):
                t, hf = o // 2, o % 2
                R = slice(0, ROWS[t])
                act.wait_ge(kn_mm, o + 1)
                if hf == 0 and t:
                    act.wait_ge(kn_red, t)
                A(kjunk[R, 4 * hf:4 * hf + 4, :], mla_bank(None, "kn", o)[R, :].rearrange("p (h d) -> p h d", h=4),
                  ACT.Square).then_inc(kn_sq, 1)
            for o in range(12):
                t, n = o // 4, o % 4
                R = slice(0, ROWS[t])
                act.wait_ge(q_mm, o + 1)
                A(Q[R, t, 2 * n:2 * n + 2, :], mla_bank(None, "q", o)[R, 0:384].rearrange("p (h d) -> p h d", h=2),
                  ACT.Copy).then_inc(q_copied, 1)
                if n == 3:
                    act.wait_ge(q_copied, o + 1)
                    if t:
                        act.wait_ge(q_scaled, t)
                    A(qjunk[R, :, :], Q[R, t, :, :], ACT.Square).then_inc(q_sq, 1)
            for t in range(NT):
                for n in range(2):
                    act.wait_ge(qr_tr, 2 * t + n + 1)
                    b = mla_bank(None, "qT", 4 * t + 2 + n)
                    if t < 2:
                        out = qrP[0:64, 4 * n:4 * n + 4, tok(t)]
                        A(out, b[0:64, :].rearrange("p (h q) -> p h q", h=4), ACT.Copy).then_inc(qrT_done, 1)
                    else:
                        for hh in range(4):
                            i = A(qrS[0:64, :, 4 * n + hh, :],
                                  b[0:64, hh * P:hh * P + NSMP].rearrange("p (b q) -> p b q", b=8), ACT.Copy)
                        i.then_inc(qrT_done, 1)
            for h in range(N_HEADS):
                act.wait_ge(qa_mm, 2 * h + 1)
                b = mla_bank(None, "qa", 2 * h)
                A(qaP[:, 0, h, :], b[:, 0:SEQ], ACT.Copy)
                A(qaS[:, :, 0, h * 8:h * 8 + 8], b[:, SEQ:NTOK].rearrange("p (b q) -> p b q", b=8), ACT.Copy)\
                    .then_inc(qa_act, 1)
            for n in range(4):
                act.wait_ge(rb_mm, n + 1)
                A(Rb[:, 2 * n:2 * n + 2, :], mla_bank(None, "rb", n).rearrange("p (h q) -> p h q", h=2), ACT.Copy)\
                    .then_inc(rb_done, 1)
            act.wait_ge(rb_mm, 5)
            A(RsN[0:64, :], mla_bank(None, "rb", 4)[0:64, 0:NSMP], ACT.Copy).then_inc(rb_done, 1)

            for it in range(16 + 2):
                if it < 16:
                    par, nk = it % 2, (it % 2 + 1) * P
                    act.wait_ge(ps_max, it + 1)
                    A(sP[:, it % 3, 0:nk], sP[:, it % 3, 0:nk], ACT.Exp, bias=st[:, PNM + par:PNM + par + 1],
                      scale=ATTN_SCALE, accum_out=st[:, PSUM_ + par:PSUM_ + par + 1]).then_inc(ps_exp, 1)
                if 1 <= it <= 16:
                    n, par, nkt = it - 1, (it - 1) % 2, (it - 1) % 2 + 1
                    act.wait_ge(pp_tr, n + 1)
                    if n >= 2:
                        act.wait_ge(po_mm, n - 1)
                    A(PTp[:, par, 0:nkt, :], bank[2 + par][:, 0:nkt * P].rearrange("p (k q) -> p k q", k=nkt),
                      ACT.Copy).then_inc(pp_done, 1)
                if it >= 2:
                    n = it - 2
                    h, qt = n // 2, n % 2
                    act.wait_ge(po_mm, n + 1)
                    A(OLTp[:, :, h, qt * P:(qt + 1) * P], bank[4 + qt][:, 0:2 * P].rearrange("p (r q) -> p r q", r=2),
                      ACT.Copy).then_inc(po_done, 1)
            for h in range(N_HEADS):
                act.wait_ge(oTp_mm, h + 1)
                A(oT[:, h, 0:SEQ], bank[h % 8][:, 0:SEQ], ACT.Copy).then_inc(oTp_done, 1)

            act.wait_ge(kn_mm, 6)
            act.wait_ge(w_used, IT_UQ + 1)
            A(wukp[0], wuk, ACT.Copy).then_inc(wuk_hi, 1)
            act.wait_ge(rb_done, 5)
            A(Rs[0:64, PAST_LEN:NKEYS], RsN[0:64, :], ACT.Copy).then_inc(achain, 1)

            def evacuate_page(b, p):
                act.wait_ge(pg_tr, 8 * b + p + 1)
                k = bank[4 + p % 2]
                A(cTp[0][:, :, p * P:(p + 1) * P], k[:, 0:2 * P].rearrange("p (r q) -> p r q", r=2), ACT.Copy)
                A(krT[0:64, p * P:(p + 1) * P], k[0:64, 2 * P:3 * P], ACT.Copy).then_inc(pg_ev, 1)

            def evacuate_probs(b):
                act.wait_ge(st_tr, b + 1)
                A(PT[:, 0:8, :], bank[6].rearrange("p (k q) -> p k q", k=8), ACT.Copy)
                A(PT[0:64, 8, :], bank[7][0:64, 0:64], ACT.Copy).then_inc(st_done, 1)

            def seq_act(b, par, kth, first):
                for p in range(N_PAGES):
                    if 0 < p < N_PAGES - 1:
                        evacuate_page(b, p + 1)
                    act.wait_ge(kk_mm, 8 * b + p + 1)
                    if not (first and p == 0):
                        act.wait_ge(kk_red, 8 * b + p)
                    for hf in range(2):
                        i = A(sjunk[:, 4 * hf:4 * hf + 4, :],
                              bank[2 * (p % 2) + hf].rearrange("p (h d) -> p h d", h=4), ACT.Square)
                    i.then_inc(kk_sq, 1)
                    if p == 2 and not first:
                        evacuate_probs(b - 1)
                for n in range(3):
                    act.wait_ge(sb_mm, 3 * b + n + 1)
                    src = bank[n][0:64, :] if n < 2 else bank[2][0:64, 64:128]
                    A(S[0:64, n * 512:n * 512 + src.shape[1]], src, ACT.Copy).then_inc(sb_ev, 1)
                if not is_last(b):
                    evacuate_page(b + 1, 0)
                    evacuate_page(b + 1, 1)
                for n, pages in ((0, [(0, 4)]), (1, [(4, 7), (7, 8)])):
                    act.wait_ge(rr_tr, 2 * b + n + 1)
                    for p0, p1 in pages:
                        i = A(Rs[0:64, p0 * P:p1 * P], rr_bank(p0, p1 - p0), ACT.Copy)
                    i.then_inc(rr_ev, 1)
                act.wait_ge(ss_done, b + 1)
                A(S[0:64, :], S[0:64, :], ACT.Exp, bias=st[0:64, SNM:SNM + 1], scale=ATTN_SCALE,
                  accum_out=st[0:64, SSUM:SSUM + 1]).then_inc(se_exp, 1)

            evacuate_page(0, 0)
            evacuate_page(0, 1)
            over_sequences(act, seq_act)
            evacuate_probs(DEC_BATCH - 1)
            for h in range(N_HEADS):
                act.wait_ge(oTs_mm, h + 1)
                A(oT[:, h, SEQ:NTOK], bank[h % 4][:, 0:NSMP], ACT.Copy).then_inc(oTs_done, 1)

            act.wait_ge(wo_mm, 1)
            act.dma_start(wr[:, :, :], w_router).then_inc(s_wr, 16)
            norm_squares(3)
            for t in range(NT):
                R = slice(0, ROWS[t])
                act.wait_ge(nxs, 3 * 3 + t + 1)
                A(XSp[0][R, t, :], XS[R, t, :], ACT.Copy).then_inc(xs_hi, 1)
            act.wait_ge(w_used, len(items))
            act.wait_ge(s_out, 64)

            def high(e, q):
                if q >= NU:
                    e, q = e + 1, q - NU
                act.wait_ge(raw_ready[raw_slot[q]], raw_count(e, q))
                wait_last(act, unit_used, e, hi_last[q])
                A(high_part[hi_slot[q]], raw[raw_slot[q]], ACT.Copy).then_inc(u_hi, 1)

            def prologue(e):
                for q in range(5):
                    high(e, q)

            def gathered(e, hf):
                act.wait_ge(ga_done, 2 * e + hf + 1)
                if hf == 0 and not (isinstance(e, int) and e == 0):
                    wait_last(act, unit_used, e, pos_gu(FF_BL - 1, 1) - NU)
                A(xgT[0][:, 4 * hf:4 * hf + 4, :], xg[:, 4 * hf:4 * hf + 4, :], ACT.Copy).then_inc(xg_hi, 1)

            def evacuate_hT(e, j):
                n = 11 * e + j
                act.wait_ge(e_tr, n + 1)
                wait_last(act, unit_used, e, pos_dn(j - 2) if j >= 2 else j - 1 - 1)
                A(hmT[0][:, j % 2, :, :], bank[4 + j % 2][:, 0:2 * P].rearrange("p (k s) -> p k s", k=2),
                  ACT.Copy).then_inc(e_trd, 1)

            def pass_act(e, prev, nxt):
                for j in range(FF_BL):
                    early, late = split_in(j, nxt)
                    if j:
                        evacuate_hT(e, j - 1)
                    for q in early:
                        high(e, q)
                    wait_last(act, unit_used, e, pos_gu(j, 1))
                    wait_pair(act, e_h, e, j)
                    A(gsil[:, j % 2, :], bank[2 + j % 2][:, 0:256], ACT.Silu).then_inc(e_silu, 1)
                    if j == FF_BL - 1 and nxt:
                        gathered(e + 1, 0)
                        gathered(e + 1, 1)
                    for q in late:
                        high(e, q)
                evacuate_hT(e, FF_BL - 1)
                if nxt:
                    for q in LAST_SPLIT:
                        high(e, q)
                wait_last(act, unit_used, e, NU - 1)
                act.wait_ge(selT_done, e + 1)
                if not (isinstance(e, int) and e == 0):
                    act.wait_ge(sc_mm, 6 * e)
                for hf in range(2):
                    A(yg[:, hf * 512:(hf + 1) * 512], bank[hf][:, :], ACT.Copy, scale=gslot[:, 0:1]).then_inc(y_done, 1)
                for hf in range(2):
                    act.wait_ge(y_done, 2 * e + hf + 1)
                    A(ygp[0][:, hf * 512:(hf + 1) * 512], yg[:, hf * 512:(hf + 1) * 512], ACT.Copy).then_inc(y_hi, 1)

            prologue(0)
            act.wait_ge(lg_max, 1)
            A(gt[:, 1, :], gt[:, 1, :], ACT.Exp).then_inc(lg_exp, 1)
            gathered(0, 0)
            gathered(0, 1)
            over_passes(act, pass_act)

            def act_further(i):
                e = i + N_EXPERTS
                prologue(e)
                gathered(e, 0)
                gathered(e, 1)
                pass_act(e, False, False)

            further(act, act_further)

        @block.vector
        def _(dve):
            V_ = nc.vector
            TT, TS, STT, RED, CP = V_.tensor_tensor, V_.tensor_scalar, V_.scalar_tensor_tensor, V_.tensor_reduce, V_.tensor_copy
            count = [0]

            def link(ins):
                count[0] = count[0] + 1
                ins.then_inc(chain, 1)
                dve.wait_ge(chain, count[0])

            def rstd(out, mean, scale=1.0):
                n = out.shape[-1]
                R = slice(0, out.shape[0])
                m, t = rs_m[R, 0:n], rs_t[R, 0:n]
                link(TS(m, mean, scale, EPS, MUL, ADD))
                link(TS(out.bitcast(i32), m.bitcast(i32), -0.5, float(0x5F3759DF), MUL, ADD))
                for _ in range(3):
                    link(TT(t, out, out, MUL))
                    link(STT(t, t, -0.5, m, MUL, MUL))
                    link(STT(out, t, 1.5, out, ADD, MUL))

            def gain(col, n, w):
                return G[:, col:col + n].unsqueeze(2).to_broadcast([P, n, w])

            def dense_low(n):
                i, h = dense_slots(n)
                dve.wait_ge(u_hi, n + 1)
                TT(low_part[i], raw[i], dense_high_part[h].bitcast(f32), SUB).then_inc(u_lo, 1)

            ahead = in_order(dense_low)

            def norm_low(s):
                for t in range(NT):
                    for hf in range(2):
                        h = slice(4 * hf, 4 * hf + 4)
                        dve.wait_ge(n_hi, 6 * s + 2 * t + hf + 1)
                        TT(hTp[1][:, h, tok(t)], hT[:, h, tok(t)], hTp[0][:, h, tok(t)].bitcast(f32), SUB)\
                            .then_inc(n_lo, 1)

            def norm(s, outs, units=-1):
                dve.wait_ge(nsq, 3 * s + 3)
                rstd(st[:, RSTD:RSTD + NT], st[:, SS:SS + NT])
                for t in range(NT):
                    R = slice(0, ROWS[t])
                    TS(XS[R, t, :], X[R, t, :], st[R, RSTD + t:RSTD + t + 1], None, MUL).then_inc(nxs, 1)
                ahead(units)
                for t in range(NT):
                    for hf in range(2):
                        dve.wait_ge(ntr, 6 * s + 2 * t + hf + 1)
                        src = bank[2 * t + hf].rearrange("p (k q) -> p k q", k=4)[:, :, 0:ROWS[t]]
                        for out, col in outs:
                            i = TT(out[:, 4 * hf:4 * hf + 4, tok(t)], src, gain(col + 4 * hf, 4, ROWS[t]), MUL)
                        i.then_inc(nht, 1)

            def add_residual(done, ready):
                for t in range(NT):
                    for hf in range(2):
                        x = X[0:ROWS[t], t, hf * 512:(hf + 1) * 512]
                        dve.wait_ge(done, 2 * t + hf + 1)
                        i = TT(x, bank[2 * t + hf][0:ROWS[t], :], x, ADD)
                    i.then_inc(ready, 1)

            V_.memset(st[:, :], 0.0)
            V_.memset(sks[:, :, :], 0.0).then_inc(s_zero, 1)
            dve.wait_ge(s_const, 32)
            dve.wait_ge(s_zero, 1)
            dve.wait_ge(s_x, 48)
            norm(0, [(hT, G_A)], 0)
            norm_low(0)
            ahead(3)
            for o in range(12):
                n, t = o // NT, o % NT
                R, c = slice(0, ROWS[t]), slice(n * 512, (n + 1) * 512)
                if t == 0:
                    ahead(2 * n + 4)
                if o == 0:
                    dve.wait_ge(s_gm, 16 * 5)
                dve.wait_ge(v_mm, o + 1)
                TT(V[R, t, c], bank[o % 8][R, :], bv_bc[R, c], ADD).then_inc(v_biased, 1)
            TT(ws[:, :, :], ws[:, :, :], triu.unsqueeze(1).to_broadcast([P, N_GROUPS, P]), MUL).then_inc(ws_done, 1)
            dve.wait_ge(rep_mm, 1)
            link(CP(wrep[0:64, :, :], bank[7][0:64, 0:64].rearrange("p (g i) -> p g i", g=8)))
            for g in range(N_GROUPS):
                i = TT(ws_new[0:64, g, :, :], wrep[0:64, g, :].unsqueeze(1).to_broadcast([64, 8, 8]),
                       K[0:64, C_BLK:C_BLK + 64].rearrange("p (b i) -> p b i", b=8), MUL)
            i.then_inc(ws_done, 1)
            for t in range(NT):
                R = slice(0, ROWS[t])
                ahead(D_U + t + 2)
                dve.wait_ge(v_sq, t + 1)
                rstd(st[R, RSV + t:RSV + t + 1], st[R, SSV + t:SSV + t + 1])
                STT(V[R, t, :], V[R, t, :], st[R, RSV + t:RSV + t + 1], sgu_bc[R, :], MUL, MUL).then_inc(v_norm, 1)
            for t in range(NT):
                R = slice(0, ROWS[t])
                ahead(D_U + t + 5)
                TT(X[R, t, :], X[R, t, :], bout_bc[R, :], ADD)
            for p in range(D_U + 5, D_OUT):
                ahead(p + 3)
            dve.wait_ge(u_mm, 16)
            for t in range(2):
                CP(bs_bc[:, :, tok(t)], bs_raw)
            link(CP(bs_bc[:, :, tok(2)].rearrange("p g (b i) -> p g b i", b=8),
                    bs_raw[:, :, 0:8].unsqueeze(2).to_broadcast([P, N_GROUPS, 8, 8])))

            def gated_low(c):
                dve.wait_ge(ug_hi, c + 1)
                TT(u_low[:, c, :], uT[:, c, :], u_parts(c)[0].bitcast(f32), SUB).then_inc(ug_lo, 1)

            for c in range(16):
                dve.wait_ge(mix_mm, c + 1)
                dve.wait_ge(u_done, c + 1)
                link(TT(gtmp[:, c % 2, :], bank[(28 + c) % 8][:, 0:NTOK], bs_bc[:, c // 2, :], ADD))
                TT(uT[:, c, :], uT[:, c, :], gtmp[:, c % 2, :], MUL).then_inc(gu_done, 1)
            for c in range(16):
                gated_low(c)
            ahead(D_GU + 2)
            add_residual(gout_mm, x_ready[1])

            norm(1, [(hT, G_F0)], D_GU + 3)
            norm_low(1)
            dve.wait_ge(v_out, 16)

            def ff_low(f):
                dve.wait_ge(ff_hi, f + 1)
                TT(ffTp[1][:, f, :], ffT[:, f, :], ffTp[0][:, f, :].bitcast(f32), SUB).then_inc(ff_lo, 1)

            for f in range(FF_CH):
                ahead(D_GU + f + 3)
                dve.wait_ge(silu_done, f + 1)
                dve.wait_ge(up_mm, f + 1)
                TT(ffT[:, f, :], sg[:, f % 2, :], bank[2 * (f % 4) + 1][:, 0:NTOK], MUL).then_inc(ff_done, 1)
                if f:
                    ff_low(f - 1)
            ff_low(FF_CH - 1)
            ahead(ND - 1)
            add_residual(dout_mm, x_ready[2])

            norm(2, [(hT, G_KV), (hbT, G_B)])
            dve.wait_ge(s_rows, 48)
            link(V_.memset(krtmp[:, :, :], 0.0))
            for t in range(NT):
                R = slice(0, ROWS[t])
                b = mla_bank(None, "ckr", t)
                dve.wait_ge(ckr_sq, t + 1)
                rstd(st[R, RCK + 2 * t:RCK + 2 * t + 2], st[R, SCK + 2 * t:SCK + 2 * t + 2])
                STT(krtmp[R, t, :], b[R, 256:320], st[R, RCK + 2 * t + 1:RCK + 2 * t + 2], brow[R, 256:320], MUL, MUL)
                STT(Cn[R, t, :], b[R, 0:256], st[R, RCK + 2 * t:RCK + 2 * t + 1], brow[R, 0:256], MUL, MUL)\
                    .then_inc(c_new, 1)
            dve.wait_ge(c_new, 3)

            def rotate(out, src, cos, sin, a, b):
                x1, x2 = src[:, :, 0:32], src[:, :, 32:64]
                TT(a, x1, cos, MUL)
                link(TT(b, x2, sin, MUL))
                link(TT(out[:, :, 0:32], a, b, SUB))
                TT(a, x1, sin, MUL)
                link(TT(b, x2, cos, MUL))
                return TT(out[:, :, 32:64], a, b, ADD)

            cos3 = K[:, C_COS:C_COS + 96].rearrange("p (t c) -> p t c", t=3)
            sin3 = K[:, C_SIN:C_SIN + 96].rearrange("p (t c) -> p t c", t=3)
            rotate(KRn, krtmp, cos3, sin3, krope1, krope2).then_inc(kr_new, 1)
            for t in range(NT):
                R = slice(0, ROWS[t])
                dve.wait_ge(dq_sq, t + 1)
                rstd(st[R, RQL + t:RQL + t + 1], st[R, SQL + t:SQL + t + 1])
                TS(cqs[R, t, :], mla_bank(None, "dq", t)[R, 0:384], st[R, RQL + t:RQL + t + 1], None, MUL)\
                    .then_inc(cq_scaled, 1)
            for t in range(NT):
                dve.wait_ge(cq_tr, t + 1)
                TT(cqT[:, :, tok(t)], mla_bank(None, "cqT", t)[:, 0:384].rearrange("p (k q) -> p k q", k=3)[:, :, 0:ROWS[t]],
                   gain(G_QL, 3, ROWS[t]), MUL).then_inc(cqT_done, 1)
            skn = st[:, SKN:SKN + 24].rearrange("p (t h) -> p t h", t=3)
            for t in range(NT):
                R = slice(0, ROWS[t])
                dve.wait_ge(kn_sq, 2 * t + 2)
                RED(skn[R, t, :], kjunk[R, :, :], AX, ADD).then_inc(kn_red, 1)
            dve.wait_ge(kn_red, 3)
            rstd(st[:, SKN:SKN + 24], st[:, SKN:SKN + 24], 1.0 / D_NOPE)
            sqn = st[:, SQN:SQN + 24].rearrange("p (t h) -> p t h", t=3)
            sqr = st[:, SQR:SQR + 24].rearrange("p (t h) -> p t h", t=3)
            for t in range(NT):
                R, n = slice(0, ROWS[t]), ROWS[t]
                dve.wait_ge(q_sq, t + 1)
                RED(sqn[R, t, :], qjunk[R, :, 0:D_NOPE], AX, ADD)
                link(RED(sqr[R, t, :], qjunk[R, :, D_NOPE:192], AX, ADD))
                rstd(sqn[R, t, :], sqn[R, t, :], 1.0 / D_NOPE)
                rstd(sqr[R, t, :], sqr[R, t, :], 1.0 / D_ROPE)
                qn, qr = Q[R, t, :, 0:D_NOPE], Q[R, t, :, D_NOPE:192]
                TT(qn, qn, sqn[R, t, :].unsqueeze(2).to_broadcast([n, 8, D_NOPE]), MUL)
                link(TT(qr, qr, sqr[R, t, :].unsqueeze(2).to_broadcast([n, 8, D_ROPE]), MUL))
                link(TT(qr, qr, brow[R, 320:384].unsqueeze(1).to_broadcast([n, 8, D_ROPE]), MUL))
                rotate(QR[R, t, :, :], qr, cos3[R, t, :].unsqueeze(1).to_broadcast([n, 8, 32]),
                       sin3[R, t, :].unsqueeze(1).to_broadcast([n, 8, 32]), rope1[R, :, :], rope2[R, :, :])\
                    .then_inc(q_scaled, 1)
            for t in range(NT):
                for n in range(2):
                    dve.wait_ge(qn_tr, 2 * t + n + 1)
                    TS(qnT[:, 4 * n:4 * n + 4, tok(t)],
                       mla_bank(None, "qT", 4 * t + n).rearrange("p (h q) -> p h q", h=4)[:, :, 0:ROWS[t]],
                       G[:, G_QN:G_QN + 1], G[:, G_KN:G_KN + 1], MUL, MUL).then_inc(qnT_done, 1)
            for h in range(N_HEADS):
                dve.wait_ge(qa_mm, 2 * h + 2)
                b = mla_bank(None, "qa", 2 * h + 1)
                CP(qaP[:, 1, h, :], b[:, 0:SEQ])
                CP(qaS[:, :, 1, h * 8:h * 8 + 8], b[:, SEQ:NTOK].rearrange("p (b q) -> p b q", b=8)).then_inc(qa_dve, 1)

            CP(rnb[0:64, :].rearrange("p (h q) -> p h q", h=8), st[0:64, SKN + 16:SKN + 24].unsqueeze(2).to_broadcast([64, 8, 8]))\
                .then_inc(rnb_done, 1)

            dve.wait_ge(rb_done, 4)
            for it in range(16 + 1):
                if it < 16:
                    h, qt, par = it // 2, it % 2, it % 2
                    nk = (qt + 1) * P
                    s, b = sP[:, it % 3, 0:nk], bank[P_BANK[it % 3]]
                    dve.wait_ge(ps_mm, it + 1)
                    if it >= 3:
                        dve.wait_ge(pp_tr, it - 2)
                    link(TT(s, b[:, 0:nk], Rb[:, h, 0:nk], MUL))
                    link(TT(s, b[:, 256:256 + nk], s, ADD))
                    link(TT(s[:, nk - P:nk], s[:, nk - P:nk], causal, ADD))
                    link(RED(st[:, PMX + par:PMX + par + 1], s, AX, ALU.max))
                    TS(st[:, PNM + par:PNM + par + 1], st[:, PMX + par:PMX + par + 1], -ATTN_SCALE, None, MUL)\
                        .then_inc(ps_max, 1)
                if it >= 1:
                    n = it - 1
                    par, nk = n % 2, (n % 2 + 1) * P
                    dve.wait_ge(ps_exp, n + 1)
                    link(V_.reciprocal(st[:, PRC + par:PRC + par + 1], st[:, PSUM_ + par:PSUM_ + par + 1]))
                    TS(sP[:, n % 3, 0:nk], sP[:, n % 3, 0:nk], st[:, PRC + par:PRC + par + 1], None, MUL).then_inc(ps_prob, 1)

            def pick_query(b):
                q = qaS[:, bass.ds(b, 1), :, :].rearrange("p a r q -> p (a r) q")
                CP(qab, q)
                link(CP(qabp[0], q))
                TT(qabp[1], q, qabp[0].bitcast(f32), SUB)
                CP(qrb[0:64], qrS[0:64, bass.ds(b, 1), :, :].rearrange("p a h q -> p (a h q)")).then_inc(q_picked, 1)

            def page_low(b, p):
                c = slice(p * P, (p + 1) * P)
                dve.wait_ge(pg_ev, 8 * b + p + 1)
                TT(cTp[1][:, :, c], bank[4 + p % 2][:, 0:2 * P].rearrange("p (r q) -> p r q", r=2),
                   cTp[0][:, :, c].bitcast(f32), SUB).then_inc(pg_lo, 1)

            def take_out(b):
                dve.wait_ge(so_mm, b + 1)
                CP(OLTs[:, bass.ds(b, 1), :, :, :].rearrange("p a r h q -> p (a r h q)"), bank[7][:, 128:256])\
                    .then_inc(so_done, 1)

            SEQ_LINKS = 16
            seq_base = count[0]

            def seq_dve(b, par, kth, first):
                count[0] = seq_base + SEQ_LINKS * b
                if first:
                    dve.wait_ge(ps_mm, 16)
                else:
                    dve.wait_ge(sb_mm, 3 * b)
                pick_query(b)
                for p in range(N_PAGES):
                    if 0 < p < N_PAGES - 1:
                        page_low(b, p + 1)
                    dve.wait_ge(kk_sq, 8 * b + p + 1)
                    if p == 0 and not first:
                        dve.wait_ge(rr_tr, 2 * b)
                    RED(sks[:, p, :], sjunk, AX, ADD).then_inc(kk_red, 1)
                    if p == 3 and not first:
                        take_out(b - 1)
                dve.wait_ge(kk_red, 8 * b + 8)
                k = sks[:, :, :].rearrange("p a h -> p (a h)")
                rstd(k, k, 1.0 / D_NOPE)
                if not is_last(b):
                    page_low(b + 1, 0)
                    page_low(b + 1, 1)
                CP(sksb[:, :, :].rearrange("p a (h q) -> p (a h) q", h=8), k.unsqueeze(2).to_broadcast([P, 64, 8]))\
                    .then_inc(kk_rstd, 1)
                for n in range(2):
                    dve.wait_ge(sa_mm, 2 * b + n + 1)
                    dve.wait_ge(rr_ev, 2 * b + n + 1)
                    c = slice(n * 512, (n + 1) * 512)
                    TT(stmp[0:64, c], bank[6 + n][0:64, :], Rs[0:64, c], MUL).then_inc(ss_a, 1)
                new = slice(PAST_LEN, NKEYS)
                dve.wait_ge(sb_mm, 3 * b + 3)
                TT(stmp[0:64, new], bank[2][0:64, 0:64], Rs[0:64, new], MUL).then_inc(ss_a, 1)
                dve.wait_ge(ss_a, 3 * b + 3)
                link(TT(stmp[0:64, new], stmp[0:64, new],
                        K[0:64, C_NEWM:C_NEWM + 512].rearrange("p (b k) -> p b k", b=8)[:, bass.ds(b, 1), :]
                        .rearrange("p a k -> p (a k)"), ADD))
                dve.wait_ge(sb_ev, 3 * b + 3)
                link(TT(S[0:64, :], stmp[0:64, :], S[0:64, :], ADD))
                link(RED(st[0:64, SMX:SMX + 1], S[0:64, :], AX, ALU.max))
                TS(st[0:64, SNM:SNM + 1], st[0:64, SMX:SMX + 1], -ATTN_SCALE, None, MUL).then_inc(ss_done, 1)
                dve.wait_ge(se_exp, b + 1)
                link(V_.reciprocal(st[0:64, SRC:SRC + 1], st[0:64, SSUM:SSUM + 1]))
                TS(S[0:64, :], S[0:64, :], st[0:64, SRC:SRC + 1], None, MUL).then_inc(se_prob, 1)
                assert not first or count[0] == seq_base + SEQ_LINKS

            dve.wait_ge(wuk_hi, 1)
            TT(wukp[1], wuk, wukp[0].bitcast(f32), SUB).then_inc(wuk_lo, 1)
            page_low(0, 0)
            page_low(0, 1)
            over_sequences(dve, seq_dve)
            count[0] = seq_base + SEQ_LINKS * DEC_BATCH
            take_out(DEC_BATCH - 1)
            add_residual(wo_mm, x_ready[3])

            def select(e, first=False):
                if not first:
                    dve.wait_ge(selT_mm, e)
                CP(gatec, item_gate[:, bass.ds(e, 1), :].rearrange("p a t -> p (a t)"))
                link(CP(posc, item_pos[:, bass.ds(e, 1), :].rearrange("p a t -> p (a t)")))
                for t in range(NT):
                    R = slice(0, ROWS[t])
                    i = TS(Sel[R, t, :], iota[R, :], posc[R, t:t + 1], None, ALU.is_equal)
                i.then_inc(sel_done, 1)

            def low(e, q):
                if q >= NU:
                    e, q = e + 1, q - NU
                dve.wait_ge(u_hi, ND + NU * e + q + 1)
                TT(low_part[raw_slot[q]], raw[raw_slot[q]], high_part[hi_slot[q]].bitcast(f32), SUB).then_inc(u_lo, 1)

            norm(3, [(hT, G_F1)])
            LG, EX, PR, EQ, O1, P2, O2, GA, MK, PO, T0, T1 = range(12)
            NE, F, FA, FB = 14, 15, 16, 17

            def g(i, w=24):
                return gt[:, i, 0:w]

            def g3(i):
                return gt[:, i, :].rearrange("p (t e) -> p t e", t=3)

            def c3(i):
                return gt[:, 13, 3 * i:3 * i + 3]

            def b3(i):
                return c3(i).unsqueeze(2).to_broadcast([P, 3, 8])

            pri3 = K[:, C_PRI:C_PRI + 8].unsqueeze(1).to_broadcast([P, 3, 8])
            link(V_.memset(gt[:, :, :], 0.0))
            for t in range(NT):
                R = slice(0, ROWS[t])
                dve.wait_ge(xs_hi, t + 1)
                dve.wait_ge(ntr, 6 * 4)
                TT(XSp[1][R, t, :], XS[R, t, :], XSp[0][R, t, :].bitcast(f32), SUB).then_inc(xs_lo, 1)
            low(0, 0)
            low(0, 1)
            dve.wait_ge(lg_mm, 1)
            V_.memset(ones, 1.0)
            for t in range(NT):
                i = CP(gt[0:ROWS[t], LG, 8 * t:8 * t + 8], bank[0][0:ROWS[t], 8 * t:8 * t + 8])
            link(i)
            link(RED(c3(0), g3(LG), AX, ALU.max))
            TT(g3(EX), g3(LG), b3(0), SUB).then_inc(lg_max, 1)
            dve.wait_ge(lg_exp, 1)
            link(RED(c3(1), g3(EX), AX, ADD))
            link(V_.reciprocal(c3(1), c3(1)))
            link(TT(g3(PR), g3(EX), b3(1), MUL))

            def top(src, c, onehot):
                link(RED(c3(c), g3(src), AX, ALU.max))
                link(TT(g3(EQ), g3(src), b3(c), ALU.is_equal))
                link(TT(g3(EQ), g3(EQ), pri3, MUL))
                link(RED(c3(c + 1), g3(EQ), AX, ALU.max))
                link(TT(g3(onehot), g3(EQ), b3(c + 1), ALU.is_equal))

            top(PR, 2, O1)
            link(STT(g(P2), g(O1), -2.0, g(PR), MUL, ADD))
            top(P2, 4, O2)
            link(TT(c3(6), c3(2), c3(4), ADD))
            link(V_.reciprocal(c3(6), c3(6)))
            link(TT(g3(T0), g3(O1), b3(2), MUL))
            link(TT(g3(T1), g3(O2), b3(4), MUL))
            link(TT(g(T0), g(T0), g(T1), ADD))
            link(TT(g3(GA), g3(T0), b3(6), MUL))
            link(TT(g(MK), g(O1), g(O2), ADD))
            TT(g3(MK), g3(MK), K[:, C_VALID:C_VALID + 3].unsqueeze(2).to_broadcast([P, 3, 8]), MUL).then_inc(mask_done, 1)
            low(0, 2)
            dve.wait_ge(cum_mm, 1)
            CP(g(NE, 8), bank[1][:, 24:32])
            link(TT(g(T0), bank[1][:, 0:24], g(MK), MUL))
            link(TS(g(PO), g(T0), -1.0, None, ADD))
            CP(item_pos[:, 0:8, :], g3(PO).rearrange("p t e -> p e t"))
            link(CP(item_gate[:, 0:8, :], g3(GA).rearrange("p t e -> p e t")))
            def gather_out(e, hf):
                dve.wait_ge(ga_mm, 2 * e + hf + 1)
                if not (isinstance(e, int) and e == 0):
                    dve.wait_ge(xg_lo, 2 * e)
                TT(xg[:, 4 * hf:4 * hf + 4, :], bank[6 + hf].rearrange("p (k q) -> p k q", k=4),
                   gain(G_F1 + 4 * hf, 4, P), MUL).then_inc(ga_done, 1)

            def gather_low(e, hf):
                h = slice(4 * hf, 4 * hf + 4)
                dve.wait_ge(xg_hi, 2 * e + hf + 1)
                TT(xgT[1][:, h, :], xg[:, h, :], xgT[0][:, h, :].bitcast(f32), SUB).then_inc(xg_lo, 1)

            def h_low(e, j):
                dve.wait_ge(e_trd, 11 * e + j + 1)
                TT(hmT[1][:, j % 2, :, :], bank[4 + j % 2][:, 0:2 * P].rearrange("p (k s) -> p k s", k=2),
                   hmT[0][:, j % 2, :, :].bitcast(f32), SUB).then_inc(e_low, 1)

            def y_low(e):
                for hf in range(2):
                    c = slice(hf * 512, (hf + 1) * 512)
                    dve.wait_ge(y_hi, 2 * e + hf + 1)
                    TT(ygp[1][:, c], yg[:, c], ygp[0][:, c].bitcast(f32), SUB).then_inc(y_lo, 1)

            def scatter_out(e, steps=range(6)):
                for n in steps:
                    t, hf = n // 2, n % 2
                    x = X[0:ROWS[t], t, hf * 512:(hf + 1) * 512]
                    dve.wait_ge(sc_mm, 6 * e + n + 1)
                    TT(x, bank[6 + hf][0:ROWS[t], :], x, ADD).then_inc(sc_done, 1)

            def pass_dve(e, prev, nxt):
                for j in range(FF_BL):
                    early, late = split_in(j, nxt)
                    if j:
                        h_low(e, j - 1)
                    for q in early:
                        low(e, q)
                    dve.wait_ge(e_silu, 11 * e + j + 1)
                    wait_pair(dve, e_tr, e, j)
                    TT(hmul[:, j % 2, :], gsil[:, j % 2, :], bank[2 + j % 2][:, 256:512], MUL).then_inc(e_h, 1)
                    if j == FF_BL - 1 and nxt:
                        gather_low(e + 1, 0)
                        gather_low(e + 1, 1)
                    for q in late:
                        low(e, q)
                    if j == 2 and prev:
                        y_low(e - 1)
                    if j in SCATTER_AT and prev:
                        scatter_out(e - 1, SCATTER_AT[j])
                    if j == SELECT_AT:
                        dve.wait_ge(selT_mm, e + 1)
                        if not (isinstance(e, int) and e == 0):
                            dve.wait_ge(y_done, 2 * e)
                        CP(SelT, bank[6][:, 0:NTOK])
                        CP(gslot, bank[7][:, 0:1]).then_inc(selT_done, 1)
                        if nxt:
                            count[0] = pass_base + e
                            select(e + 1)
                    if j in GATHER_AT and nxt:
                        gather_out(e + 1, GATHER_AT[j])
                h_low(e, FF_BL - 1)
                if nxt:
                    for q in LAST_SPLIT:
                        low(e, q)

            select(0, True)
            low(0, 3)
            low(0, 4)
            for step in (gather_out, gather_low):
                for hf in range(2):
                    step(0, hf)
            for k in range(2):
                i = TS(gt[:, F, 8 * k:8 * k + 8], g(NE, 8), float(CAP * (k + 1)), None, ALU.is_gt)
            link(i)
            link(CP(g(FA, 16), g(F, 16)))
            a, b = FA, FB
            for sh in (1, 2, 4, 8):
                CP(gt[:, b, 0:sh], gt[:, a, 0:sh])
                link(TT(gt[:, b, sh:16], gt[:, a, sh:16], gt[:, a, 0:16 - sh], ADD))
                a, b = b, a
            link(CP(gt[:, 18, 0:1], gt[:, a, 15:16]))
            link(TT(g(T1, 16), g(a, 16), g(F, 16), SUB))
            for k in range(2):
                xp3 = xtab[:, 0, :].rearrange("p (t k e) -> p t k e", t=3, k=2)
                xg3 = xtab[:, 1, :].rearrange("p (t k e) -> p t k e", t=3, k=2)
                TS(xp3[:, :, k, :], g3(PO), -float(CAP * (k + 1)), None, ADD)
                i = CP(xg3[:, :, k, :], g3(GA))
            link(i)
            for o in range(MAX_EXTRA):
                link(TS(g(T0, 16), g(T1, 16), float(o), None, ALU.is_equal))
                link(TT(g(T0, 16), g(T0, 16), g(F, 16), MUL))
                pick = gt[:, T0, 0:16].unsqueeze(1).to_broadcast([P, 3, 16])
                for x, dst in ((0, item_pos), (1, item_gate)):
                    y = xtab[:, 2 + x, :].rearrange("p (t k) -> p t k", t=3)
                    link(TT(y, xtab[:, x, :].rearrange("p (t k) -> p t k", t=3), pick, MUL))
                    link(RED(dst[:, 8 + o, :], y, AX, ADD))
                link(TT(xtab[:, 4, 0:16], gt[:, T0, 0:16], K[:, C_EIDX:C_EIDX + 16], MUL))
                link(RED(gt[:, 18, o + 1:o + 2], xtab[:, 4, 0:16], AX, ADD))
            CP(cnt_i[0:1, :], gt[0:1, 18, 0:1 + MAX_EXTRA]).then_inc(table_done, 1)

            pass_base = count[0]
            over_passes(dve, pass_dve)
            count[0] = pass_base + N_EXPERTS - 1
            y_low(N_EXPERTS - 1)
            scatter_out(N_EXPERTS - 1)
            far_base = count[0]

            def dve_further(i):
                count[0] = far_base + i
                for q in range(5):
                    low(i + N_EXPERTS, q)
                select(i + N_EXPERTS)
                for step in (gather_out, gather_low):
                    for hf in range(2):
                        step(i + N_EXPERTS, hf)
                pass_dve(i + N_EXPERTS, False, False)
                y_low(i + N_EXPERTS)
                scatter_out(i + N_EXPERTS)

            further(dve, dve_further)
            dve.drain().then_inc(x_ready[4], 1)

        @block.tensor
        def _(pe):
            T = nc.tensor.transpose

            def norm(s, split=False):
                for t in range(NT):
                    pe.wait_ge(nxs, 3 * s + t + 1)
                    n = ROWS[t]
                    for hf in range(2):
                        for k in range(4):
                            i = T(bank[2 * t + hf][:, k * P:k * P + n],
                                  XS[0:n, t, (4 * hf + k) * P:(4 * hf + k + 1) * P], ident[0:n, 0:n])
                        i.then_inc(ntr, 1)
                if not split:
                    pe.wait_ge(nht, 6 * s + 6)
                else:
                    pe.wait_ge(n_lo, 6 * s + 6)

            def products(out, x, w, first, last):
                (xh, xl), (wh, wl) = x, w
                mm(out, xh, wh, start=first, stop=False)
                mm(out, xh, wl, start=False, stop=False)
                return mm(out, xl, wh, start=False, stop=last)

            def dense_unit(n, chunks):
                pe.wait_ge(u_lo, n + 1)
                i, h = dense_slots(n)
                return [x.rearrange("p (k c) -> p k c", k=chunks) for x in (dense_high_part[h], low_part[i])]

            def residual_units(n0, units, lhs, ready, done):
                for c in range(2 * units):
                    pe.wait_ge(ready, c + 1)
                    if c % 2 == 0:
                        w = dense_unit(n0 + c // 2, 2)
                    last = c == 2 * units - 1
                    for t in range(NT):
                        for hf in range(2):
                            i = products(bank[2 * t + hf][0:ROWS[t], :], [x[:, tok(t)] for x in lhs(c)],
                                         [x[:, c % 2, hf * 512:(hf + 1) * 512] for x in w], c == 0, last)
                            if last:
                                i.then_inc(done, 1)
                    if last:
                        pe.wait_ge(done, 6)
                        pe.sem_inc(unit_used, 1)
                    elif c % 2:
                        i.then_inc(unit_used, 1)

            def residual_mm(n0, chunks, lhs, done):
                for c in range(chunks):
                    if c % 4 == 0:
                        await_item(pe, n0 + c // 4)
                    for t in range(NT):
                        for hf in range(2):
                            i = mm(bank[2 * t + hf][0:ROWS[t], :], lhs(c, t),
                                   weights(n0 + c // 4)[:, c % 4, hf * 512:(hf + 1) * 512],
                                   start=(c == 0), stop=(c == chunks - 1))
                            if c == chunks - 1:
                                i.then_inc(done, 1)
                    if c % 4 == 3 or c == chunks - 1:
                        if c == chunks - 1:
                            pe.wait_ge(done, 6)
                            pe.sem_inc(w_used, 1)
                        else:
                            i.then_inc(w_used, 1)

            pe.wait_ge(s_const, 32)
            norm(0, True)
            for n in range(4):
                for h in range(2):
                    w = dense_unit(2 * n + h, 4)
                    for t in range(NT):
                        o = NT * n + t
                        if o >= 8 and h == 0:
                            pe.wait_ge(v_biased, o - 7)
                        for k in range(4):
                            i = products(bank[o % 8][0:ROWS[t], :], [x[:, 4 * h + k, tok(t)] for x in hTp],
                                         [x[:, k, :] for x in w], h == 0 and k == 0, h == 1 and k == 3)
                        if h:
                            i.then_inc(v_mm, 1)
                    if h:
                        pe.wait_ge(v_mm, o + 1)
                        pe.sem_inc(unit_used, 1)
                    else:
                        i.then_inc(unit_used, 1)
            pe.wait_ge(ws_done, 1)
            pe.wait_ge(v_biased, 8)
            mm(bank[7][0:64, 0:64], K[0:8, C_REP:C_REP + 64], ws[0:8, :, 0:8], start=True, stop=True).then_inc(rep_mm, 1)
            for c in range(16):
                o = 12 + c
                if c % 2 == 0:
                    w = dense_unit(D_U + c // 2, KC)
                if o < 20:
                    pe.wait_ge(v_biased, o - 7)
                else:
                    pe.wait_ge(u_done, o - 19)
                if c == 3:
                    pe.wait_ge(ws_done, 2)
                for k in range(KC):
                    i = products(bank[o % 8][:, 0:NTOK], [x[:, k, c % 2 * P:(c % 2 + 1) * P] for x in w],
                                 [x[:, k, :] for x in hTp], k == 0, k == KC - 1)
                i.then_inc(u_mm, 1)
                if c % 2:
                    pe.wait_ge(u_mm, c + 1)
                    pe.sem_inc(unit_used, 1)
            pe.wait_ge(v_norm, 3)
            pe.wait_ge(ws_done, 2)
            for c in range(16):
                o = 28 + c
                if o < 36:
                    pe.wait_ge(u_done, o - 19)
                else:
                    pe.wait_ge(gu_done, o - 35)
                for t in range(2):
                    mm(bank[o % 8][:, tok(t)], V[:, t, c * P:(c + 1) * P], ws[:, c // 2, :], start=True, stop=True)
                mm(bank[o % 8][:, tok(2)], V[0:NSMP, 2, c * P:(c + 1) * P],
                   ws_new[0:NSMP, c // 2, :, :].rearrange("p b i -> p (b i)"), start=True, stop=True).then_inc(mix_mm, 1)
            pe.wait_ge(gu_done, 16)
            residual_units(D_OUT, 8, u_parts, ug_lo, gout_mm)

            norm(1, True)
            for f in range(FF_CH):
                w = dense_unit(D_GU + f, KC)
                if f >= 4:
                    pe.wait_ge(ff_done, f - 3)
                for h, done in ((0, g_mm), (1, up_mm)):
                    for k in range(KC):
                        i = products(bank[2 * (f % 4) + h][:, 0:NTOK], [x[:, k, h * P:(h + 1) * P] for x in w],
                                     [x[:, k, :] for x in hTp], k == 0, k == KC - 1)
                    i.then_inc(done, 1)
                pe.wait_ge(up_mm, f + 1)
                pe.sem_inc(unit_used, 1)
            pe.wait_ge(ff_done, FF_CH)
            residual_units(D_DN, FF_BL, lambda c: [x[:, c, :] for x in ffTp], ff_lo, dout_mm)

            norm(2)
            for name, it, w, src, done in (("ckr", IT_CK, 320, hT, ckr_mm), ("dq", IT_DQ, Q_RANK, hbT, dq_mm)):
                await_item(pe, it)
                for t in range(NT):
                    b = mla_bank(pe, name, t)
                    for k in range(KC):
                        i = mm(b[0:ROWS[t], 0:w], src[:, k, tok(t)], weights(it)[:, k, :], start=(k == 0), stop=(k == KC - 1))
                    i.then_inc(done, 1)
                pe.wait_ge(done, 3)
                pe.sem_inc(w_used, 1)
            for t in range(NT):
                b, n = mla_bank(pe, "cqT", t), ROWS[t]
                pe.wait_ge(cq_scaled, t + 1)
                for k in range(3):
                    i = T(b[:, k * P:k * P + n], cqs[0:n, t, k * P:(k + 1) * P], ident[0:n, 0:n])
                i.then_inc(cq_tr, 1)
            pe.wait_ge(c_new, 3)
            pe.wait_ge(kr_new, 1)
            for t in range(NT):
                b, n = mla_bank(pe, "ckT", t), ROWS[t]
                for r in range(2):
                    T(b[:, r * P:r * P + n], Cn[0:n, t, r * P:(r + 1) * P], ident[0:n, 0:n])
                T(b[0:64, 256:256 + n], KRn[0:n, t, :], ident[0:n, 0:n]).then_inc(ck_tr, 1)
            pe.wait_ge(s_uk, 16)
            for o in range(6):
                t, hf = o // 2, o % 2
                b = mla_bank(pe, "kn", o)
                pe.wait_ge(ckT_done, t + 1)
                for r in range(2):
                    i = mm(b[0:ROWS[t], :], cTn[:, r, tok(t)], wuk[:, r, hf * 512:(hf + 1) * 512], start=(r == 0), stop=(r == 1))
                i.then_inc(kn_mm, 1)
            pe.wait_ge(cqT_done, 3)
            await_item(pe, IT_UQ)
            await_item(pe, IT_UQ + 1)
            for o in range(12):
                t, n = o // 4, o % 4
                b = mla_bank(pe, "q", o)
                for k in range(3):
                    i = mm(b[0:ROWS[t], 0:384], cqT[:, k, tok(t)], weights(IT_UQ + n // 2)[:, k, n % 2 * 384:(n % 2 + 1) * 384],
                           start=(k == 0), stop=(k == 2))
                i.then_inc(q_mm, 1)
            pe.wait_ge(q_mm, 12)
            pe.sem_inc(w_used, 2)
            for t in range(NT):
                n = ROWS[t]
                pe.wait_ge(q_scaled, t + 1)
                for i4 in range(4):
                    b = mla_bank(pe, "qT", 4 * t + i4)
                    for hh in range(4):
                        if i4 < 2:
                            i = T(b[:, hh * P:hh * P + n], Q[0:n, t, 4 * i4 + hh, 0:D_NOPE], ident[0:n, 0:n])
                        else:
                            i = T(b[0:64, hh * P:hh * P + n], QR[0:n, t, 4 * (i4 - 2) + hh, :], ident[0:n, 0:n])
                    i.then_inc(qn_tr if i4 < 2 else qr_tr, 1)
            pe.wait_ge(qnT_done, 6)
            pe.wait_ge(s_mla, 32)
            for o in range(16):
                h, r = o // 2, o % 2
                mm(mla_bank(pe, "qa", o)[:, 0:NTOK], wukT[:, h, r * P:(r + 1) * P], qnT[:, h, :], start=True, stop=True)\
                    .then_inc(qa_mm, 1)
            pe.wait_ge(rnb_done, 1)
            skn = st[:, SKN:SKN + 24].rearrange("p (t h) -> p t h", t=3)
            for n in range(4):
                b = mla_bank(pe, "rb", n)
                for h in range(2):
                    for t in range(2):
                        i = mm(b[:, (2 * h + t) * P:(2 * h + t + 1) * P],
                               skn[:, t, 2 * n + h:2 * n + h + 1].to_broadcast([P, P]), ident, start=True, stop=True)
                i.then_inc(rb_mm, 1)
            mm(mla_bank(pe, "rb", 4)[0:64, 0:64], rnb[0:64, :],
               ident[0:64, 0:64], start=True, stop=True).then_inc(rb_mm, 1)

            pe.wait_ge(rb_done, 5)
            pe.wait_ge(qa_dve, 8)
            pe.wait_ge(qrT_done, 6)

            def p_scores(it):
                h, qt = it // 2, it % 2
                nk, b = (qt + 1) * P, bank[P_BANK[it % 3]]
                if it >= 3:
                    pe.wait_ge(ps_max, it - 2)
                for r in range(2):
                    mm(b[:, 0:nk], qaP[:, r, h, tok(qt)], cTn[:, r, 0:nk], start=(r == 0), stop=(r == 1))
                mm(b[:, 256:256 + nk], qrP[0:64, h, tok(qt)], krTn[0:64, 0:nk], start=True, stop=True).then_inc(ps_mm, 1)

            p_scores(0)
            for it in range(16 + 2):
                if it + 1 < 16:
                    p_scores(it + 1)
                if 1 <= it <= 16:
                    n, nkt = it - 1, (it - 1) % 2 + 1
                    pe.wait_ge(ps_prob, n + 1)
                    if n >= 2:
                        pe.wait_ge(pp_done, n - 1)
                    for k in range(nkt):
                        i = T(bank[2 + n % 2][:, k * P:(k + 1) * P], sP[:, n % 3, k * P:(k + 1) * P], ident)
                    i.then_inc(pp_tr, 1)
                if it >= 2:
                    n, nkt = it - 2, it % 2 + 1
                    pe.wait_ge(pp_done, n + 1)
                    if n >= 2:
                        pe.wait_ge(po_done, n - 1)
                    for r in range(2):
                        for k in range(nkt):
                            i = mm(bank[4 + n % 2][:, r * P:(r + 1) * P], Cn[:, k, r * P:(r + 1) * P], PTp[:, n % 2, k, :],
                                   start=(k == 0), stop=(k == nkt - 1))
                    i.then_inc(po_mm, 1)
            pe.wait_ge(po_done, 16)
            for h in range(N_HEADS):
                for r in range(2):
                    i = mm(bank[h][:, 0:SEQ], wuv[:, r, h * P:(h + 1) * P], OLTp[:, r, h, :], start=(r == 0), stop=(r == 1))
                i.then_inc(oTp_mm, 1)

            pe.wait_ge(oTp_done, 8)

            def page_tr(b, par, p):
                if not (isinstance(b, int) and b == 0 and p < 2):
                    pe.wait_ge(pg_lo, 8 * b + p - 1)
                k = bank[4 + p % 2]
                for r in range(2):
                    T(k[:, r * P:(r + 1) * P], Cpg[par][:, p, r * P:(r + 1) * P], ident)
                T(k[0:64, 2 * P:3 * P], KRpg[par][:, p, :], ident).then_inc(pg_tr, 1)

            def probs_tr(b):
                pe.wait_ge(s_const, 32)
                pe.wait_ge(se_prob, b + 1)
                for p in range(N_PAGES):
                    T(bank[6][:, p * 64:(p + 1) * 64], S[0:64, p * P:(p + 1) * P], ident[0:64, 0:64])
                T(bank[7][0:64, 0:64], S[0:64, PAST_LEN:NKEYS], ident[0:64, 0:64]).then_inc(st_tr, 1)

            def outputs_mm(b, par):
                pe.wait_ge(st_done, b + 1)
                for r in range(2):
                    o = bank[7][:, 128 + r * 64:192 + r * 64]
                    for p in range(N_PAGES):
                        mm(o, Cpg[par][:, p, r * P:(r + 1) * P], PT[:, p, :], start=(p == 0), stop=False)
                    i = mm(o, Cn[0:64, 2, r * P:(r + 1) * P], PT[0:64, 8, :], start=False, stop=True)
                i.then_inc(so_mm, 1)

            def seq_pe(b, par, kth, first):
                if first:
                    pe.wait_ge(pg_first[par], 64 * kth + 64)
                    page_tr(b, par, 0)
                    page_tr(b, par, 1)
                for p in range(N_PAGES):
                    if p == 1:
                        pe.wait_ge(pg_ready[par], 192 * kth + 192)
                    if 0 < p < N_PAGES - 1:
                        page_tr(b, par, p + 1)
                    pe.wait_ge(pg_lo, 8 * b + p + 1)
                    if not (first and p < 2):
                        pe.wait_ge(kk_sq, 8 * b + p - 1)
                    if not first and p < 2:
                        pe.wait_ge(sb_ev, 3 * b)
                        pe.wait_ge(ss_a, 3 * b)
                        pe.wait_ge(rr_ev, 2 * b)
                    for hf in range(2):
                        for r in range(2):
                            i = products(bank[2 * (p % 2) + hf][:, :], [x[:, r, p * P:(p + 1) * P] for x in cTp],
                                         [x[:, r, hf * 512:(hf + 1) * 512] for x in wukp], r == 0, r == 1)
                    i.then_inc(kk_mm, 1)
                    if p == 2 and not first:
                        probs_tr(b - 1)
                    if p == 3 and not first:
                        outputs_mm(b - 1, 1 - par)
                pe.wait_ge(q_picked, b + 1)
                if not first:
                    pe.wait_ge(so_done, b)
                for n in range(2):
                    for r in range(2):
                        i = products(bank[6 + n][0:64, :], [x[:, r, :] for x in qabp],
                                     [x[:, r, n * 512:(n + 1) * 512] for x in cTp], r == 0, r == 1)
                    i.then_inc(sa_mm, 1)
                pe.wait_ge(kk_sq, 8 * b + 8)
                for r in range(2):
                    mm(bank[2][0:64, 0:64], qab[:, r, :], cTn[:, r, SEQ:NTOK], start=(r == 0), stop=(r == 1))
                for n in range(2):
                    mm(bank[n][0:64, :], qrb[0:64, :], krT[0:64, n * 512:(n + 1) * 512], start=True, stop=True).then_inc(sb_mm, 1)
                mm(bank[2][0:64, 64:128], qrb[0:64, :], krTn[0:64, SEQ:NTOK], start=True, stop=True).then_inc(sb_mm, 1)
                if not is_last(b):
                    pe.wait_ge(pg_first[1 - par], 64 * (kth + par) + 64)
                    page_tr(b + 1, 1 - par, 0)
                    pe.wait_ge(sb_ev, 3 * b + 3)
                    page_tr(b + 1, 1 - par, 1)
                else:
                    pe.wait_ge(sb_ev, 3 * b + 3)
                pe.wait_ge(s_const, 32)
                pe.wait_ge(kk_rstd, b + 1)
                for n in range(2):
                    for p in range(4 * n, 4 * n + 4):
                        i = T(rr_bank(p), sksb[:, p, :], ident)
                    i.then_inc(rr_tr, 1)

            pe.wait_ge(wuk_lo, 1)
            over_sequences(pe, seq_pe)
            probs_tr(DEC_BATCH - 1)
            outputs_mm(DEC_BATCH - 1, 1)
            pe.wait_ge(so_done, 8)
            for h in range(N_HEADS):
                if h >= 4:
                    pe.wait_ge(oTs_done, h - 3)
                for r in range(2):
                    i = mm(bank[h % 4][:, 0:NSMP], wuv[:, r, h * P:(h + 1) * P], OLTs[:, :, r, h, :], start=(r == 0), stop=(r == 1))
                i.then_inc(oTs_mm, 1)
            pe.wait_ge(oTs_done, 8)
            residual_mm(IT_WO, N_HEADS, lambda c, t: oT[:, c, tok(t)], wo_mm)

            norm(3)
            pe.wait_ge(s_wr, 16)
            for t in range(NT):
                for k in range(KC):
                    i = mm(bank[0][0:ROWS[t], 8 * t:8 * t + 8], hT[:, k, tok(t)], wr[:, k, :], start=(k == 0), stop=(k == KC - 1))
            i.then_inc(lg_mm, 1)
            pe.wait_ge(mask_done, 1)
            for t in range(NT):
                for u in range(t + 1):
                    mm(bank[1][:, 8 * t:8 * t + 8], triu if u == t else ones, gt[:, 8, 8 * u:8 * u + 8],
                       start=(u == 0), stop=(u == t))
            for u in range(NT):
                i = mm(bank[1][:, 24:32], ones, gt[:, 8, 8 * u:8 * u + 8], start=(u == 0), stop=(u == 2))
            i.then_inc(cum_mm, 1)

            def gather_mm(e, halves=(0, 1)):
                pe.wait_ge(sel_done, e + 1)
                for hf in halves:
                    for k in range(4):
                        c = slice((4 * hf + k) * P, (4 * hf + k + 1) * P)
                        for part in range(2):
                            for t in range(NT):
                                R = slice(0, ROWS[t])
                                i = mm(bank[6 + hf][:, k * P:(k + 1) * P], XSp[part][R, t, c], Sel[R, t, :],
                                       start=(part == 0 and t == 0), stop=(part == 1 and t == 2))
                    i.then_inc(ga_mm, 1)

            def scatter_mm(e, steps=range(6)):
                pe.wait_ge(y_lo, 2 * e + 2)
                for n in steps:
                    t, hf = n // 2, n % 2
                    if n >= 2:
                        pe.wait_ge(sc_done, 6 * e + n - 1)
                    for part in range(2):
                        i = mm(bank[6 + hf][0:ROWS[t], :], SelT[:, tok(t)], ygp[part][:, hf * 512:(hf + 1) * 512],
                               start=(part == 0), stop=(part == 1))
                    i.then_inc(sc_mm, 1)

            def h_tr(e, j):
                pe.wait_ge(e_h, 11 * e + j + 1)
                wait_pair(pe, e_low, e, j)
                for q in range(2):
                    i = T(bank[4 + j % 2][:, q * P:(q + 1) * P], hmul[:, j % 2, q * P:(q + 1) * P], ident)
                i.then_inc(e_tr, 1)

            def down_mm(e, j):
                pe.wait_ge(e_low, 11 * e + j + 1)
                pe.wait_ge(u_lo, ND + NU * e + pos_dn(j) + 1)
                if j == 0 and not (isinstance(e, int) and e == 0):
                    pe.wait_ge(y_done, 2 * e)
                w = [x.rearrange("p (k c) -> p k c", k=2) for x in unit_parts(pos_dn(j))]
                for q in range(2):
                    for hf in range(2):
                        i = products(bank[hf][:, :], [x[:, j % 2, q, :] for x in hmT],
                                     [x[:, q, hf * 512:(hf + 1) * 512] for x in w],
                                     j == 0 and q == 0, j == FF_BL - 1 and q == 1)
                i.then_inc(unit_used, 1)

            def pass_pe(e, prev, nxt):
                for j in range(FF_BL):
                    if j == 0:
                        pe.wait_ge(xg_lo, 2 * e + 2)
                    wait_pair(pe, e_h, e, j)
                    for half in range(2):
                        if half and j:
                            h_tr(e, j - 1)
                        pe.wait_ge(u_lo, ND + NU * e + pos_gu(j, half) + 1)
                        w = [x.rearrange("p (k c) -> p k c", k=4) for x in unit_parts(pos_gu(j, half))]
                        for k in range(4):
                            i = products(bank[2 + j % 2][:, :], [x[:, 4 * half + k, :] for x in xgT],
                                         [x[:, k, :] for x in w], half == 0 and k == 0, half == 1 and k == 3)
                        i.then_inc(unit_used, 1)
                    if j >= 2:
                        down_mm(e, j - 2)
                    if j in SCATTER_AT and prev:
                        scatter_mm(e - 1, SCATTER_AT[j])
                    if j == SELECT_AT:
                        if prev:
                            pe.wait_ge(sc_done, 6 * e)
                        for t in range(NT):
                            R = slice(0, ROWS[t])
                            T(bank[6][:, tok(t)], Sel[R, t, :].bitcast(f32), ident[R, R])
                        for t in range(NT):
                            R = slice(0, ROWS[t])
                            i = mm(bank[7][:, 0:1], Sel[R, t, :].bitcast(f32), gatec[R, t:t + 1], start=(t == 0), stop=(t == 2))
                        i.then_inc(selT_mm, 1)
                    if j in GATHER_AT and nxt:
                        pe.wait_ge(selT_done, e + 1)
                        gather_mm(e + 1, (GATHER_AT[j],))
                h_tr(e, FF_BL - 1)
                down_mm(e, FF_BL - 2)
                down_mm(e, FF_BL - 1)

            pe.wait_ge(xs_lo, 3)
            gather_mm(0)
            over_passes(pe, pass_pe)
            scatter_mm(N_EXPERTS - 1)

            def pe_further(i):
                e = i + N_EXPERTS
                pe.wait_ge(sc_done, 6 * e)
                gather_mm(e)
                pass_pe(e, False, False)
                scatter_mm(e)

            further(pe, pe_further)


_OUTS = [("y_p", (SEQ, D_MODEL)), ("y_s", (64, D_MODEL)), ("lat_p", (SEQ, KV_RANK)), ("kr_p", (SEQ, D_ROPE)),
         ("lat_s", (64, KV_RANK)), ("kr_s", (64, D_ROPE)), ("v_s", (64, D_GATE))]


def _constants():
    import numpy as np
    K = np.zeros((P, C_END), np.float32)
    r = np.arange(P)
    K[:, C_ID:C_ID + P] = np.eye(P)
    K[:, C_TRIU:C_TRIU + P] = r[:, None] <= r[None, :]
    K[:, C_CAUS:C_CAUS + P] = np.where(r[None, :] <= r[:, None], 0, MASKED)
    K[0:64, C_BLK:C_BLK + 64] = np.kron(np.eye(8), np.ones((8, 8)))
    K[0:8, C_REP:C_REP + 64] = np.tile(np.eye(8), (1, 8))
    h, q, b, b2, s = np.ix_(*[np.arange(8)] * 5)
    new = np.where((b == b2) & (s <= q) & (h >= 0), 0, MASKED)
    K[0:64, C_NEWM:C_NEWM + 512] = new.reshape(64, 512)
    K[:, C_IOTA:C_IOTA + P] = r[None, :]
    K[:, C_VALID:C_VALID + 3] = r[:, None] < np.array(ROWS)[None, :]
    K[:, C_PRI:C_PRI + 8] = np.arange(8, 0, -1)[None, :]
    K[:, C_EIDX:C_EIDX + 16] = np.tile(np.arange(8), 2)[None, :]
    pos = np.stack([r, r + P, PAST_LEN + r % DEC_SEQ], 1).astype(np.float32)
    half = D_ROPE // 2
    inv = np.float32(10000.0) ** (-np.arange(half, dtype=np.float32) / np.float32(half))
    ang = pos[:, :, None] * inv[None, None, :]
    K[:, C_COS:C_COS + 96] = np.cos(ang).reshape(P, 96)
    K[:, C_SIN:C_SIN + 96] = np.sin(ang).reshape(P, 96)
    return K


def kernel(**x):
    import numpy as np
    import concourse.bacc as bacc
    from concourse.bass_utils import run_bass_kernel_spmd

    x = {k: np.asarray(v) for k, v in x.items()}

    def columns(v):
        return v.reshape(-1, P).T

    def gate_up(g, u, w):
        n, blocks = g.shape[0], D_FF // w
        x = np.stack([a.reshape(n, KC, P, blocks, w) for a in (g, u)], 4)
        return np.ascontiguousarray(x.transpose(0, 3, 2, 1, 4, 5)).reshape(n, blocks, P, KC * 2 * w)

    G = np.concatenate([columns(x[k].reshape(-1)) if isinstance(k, str) else columns(k) for k in (
        "a_norm_g", x["a_b_in"][0, :D_GATE], x["f_norm_g"][0], "kv_norm_g", "b_norm_g", "b_q_lat_g", "b_qn_g",
        "kn_g", x["f_norm_g"][1])], 1)
    md = x["m_w_down"][0].reshape(N_EXPERTS, FF_BL, 2, P, D_MODEL).transpose(0, 1, 3, 2, 4)
    gu = gate_up(x["m_w_gate"][0], x["m_w_up"][0], 256).reshape(N_EXPERTS, FF_BL, P, 2, UNIT)
    units = np.empty((N_EXPERTS, 3 * FF_BL, P, UNIT), np.float32)
    for j in range(FF_BL):
        for half in range(2):
            units[:, 2 * j + half + max(0, j - 2)] = gu[:, j, :, half]
        units[:, min(3 * j + 6, 2 * FF_BL + j)] = md[:, j].reshape(N_EXPERTS, P, UNIT)
    data = {
        "xp": x["x_prompt"][0], "xs_in": x["x_sample"].reshape(64, D_MODEL), "c_lat": x["cache_latent"],
        "c_kr": x["cache_krope"], "ptab": x["page_table"].reshape(1, -1), "consts": _constants(), "cols": G,
        "b_v": x["a_b_in"][:, D_GATE:], "sgu_g": x["a_sgu_g"], "w_in": x["a_w_in"][0],
        "wsT": x["a_w_s"][0].transpose(2, 0, 1), "b_s": x["a_b_s"].reshape(1, -1), "w_out": x["a_w_out"][0],
        "b_out": x["a_b_out"], "kv_lat_g": x["kv_lat_g"][None], "kr_g": x["kr_g"][None], "qr_g": x["b_qr_g"],
        "w_ckr": np.concatenate([x["w_dkv"], x["w_kr"]], 1), "w_uk": x["w_uk"].reshape(KV_RANK, -1),
        "w_ukT": x["w_uk"].transpose(2, 1, 0), "w_uv": x["w_uv"].reshape(KV_RANK, -1), "w_dq": x["b_w_dq"][0],
        "w_uq": x["b_w_uq"][0].reshape(Q_RANK, -1), "w_o": x["b_w_o"][0],
        "w_router": x["m_w_router"][0].reshape(KC, P, N_EXPERTS).transpose(1, 0, 2),
        "d_gu": gate_up(x["d_w_gate"], x["d_w_up"], P)[0].reshape(FF_CH, P, KC, 2 * P), "d_down": x["d_w_down"][0],
        "m_un": units,
    }
    nc = bacc.Bacc("TRN2", target_bir_lowering=False, num_devices=1)
    arrays, args = {}, {}
    for name, a in data.items():
        a = np.ascontiguousarray(a)
        arrays["in_" + name] = a
        args[name] = nc.dram_tensor("in_" + name, a.shape, mybir.dt.from_np(a.dtype), kind="ExternalInput").ap()
    for name, shape in _OUTS:
        args[name] = nc.dram_tensor("out_" + name, shape, mybir.dt.float32, kind="ExternalOutput").ap()
    yoco_step(nc, **args)
    r = run_bass_kernel_spmd(nc, [arrays], core_ids=[0]).results[0]
    y_p, y_s, lat_p, kr_p, lat_s, kr_s, v_s = (r["out_" + n] for n, _ in _OUTS)
    return (y_p[None], y_s.reshape(8, 8, -1), lat_p[None], kr_p[None], lat_s.reshape(8, 8, -1),
            kr_s.reshape(8, 8, -1), v_s.reshape(1, 8, 8, -1))
```
